# Optimizing a Trainium2 kernel written in Bass

```python
import jax, jax.numpy as jnp
from jax import lax
import numpy as np

D_MODEL = 1024
BATCH = 1
SEQ = 512
DEPTH = 1

CTX_LEN = 256
GRID_W = 64
N_HEADS = 8
HEAD_DIM = 64
D_ATT = N_HEADS * HEAD_DIM
WIN_ROWS_MAX = 8
WIN_COLS = 16
D_CONV = 512
CONV_WIDTH = 31
N_GROUPS = 4
EXPERTS_PER_GROUP = 8
N_EXPERTS = N_GROUPS * EXPERTS_PER_GROUP
TOP_K_IN_GROUP = 2
D_EXPERT = 512
MOE_BLOCK = 128
NORM_EPS = 1e-6
NEG_INF = -1e30

Q0 = 0
K0 = Q0 + D_ATT
V0 = K0 + D_ATT
GLU0 = V0 + D_ATT
GA0 = GLU0 + 2 * D_CONV
GB0 = GA0 + D_MODEL
D_IN = GB0 + D_MODEL


def rmsnorm(x, g):
    xf = x.astype(jnp.float32)
    y = xf * lax.rsqrt(jnp.mean(xf * xf, axis=-1, keepdims=True) + NORM_EPS)
    return (y * g.astype(jnp.float32)).astype(x.dtype)

def layernorm(x, g, b):
    xf = x.astype(jnp.float32)
    mu = jnp.mean(xf, axis=-1, keepdims=True)
    var = jnp.mean(jnp.square(xf - mu), axis=-1, keepdims=True)
    y = (xf - mu) * lax.rsqrt(var + NORM_EPS)
    return (y * g.astype(jnp.float32) + b.astype(jnp.float32)).astype(x.dtype)

def modulate(h, shift, scale):
    return h * (1 + scale) + shift

def split_heads(t):
    return t.reshape(t.shape[0], t.shape[1], N_HEADS, HEAD_DIM)

def latent_neighbourhood_attention(q, k, v, k_ctx, v_ctx, rpb):
    B, N, H, hd = q.shape
    rows = N // GRID_W
    kh = min(WIN_ROWS_MAX, rows)
    scale = hd ** -0.5
    q_rows = q.reshape(B, rows, GRID_W, H, hd).transpose(1, 0, 3, 2, 4)
    k_grid = k.reshape(B, rows, GRID_W, H, hd).transpose(0, 3, 1, 2, 4)
    v_grid = v.reshape(B, rows, GRID_W, H, hd).transpose(0, 3, 1, 2, 4)
    cq = jnp.arange(GRID_W)[:, None]
    ck = jnp.arange(GRID_W)[None, :]
    c_start = jnp.clip(cq - WIN_COLS // 2, 0, GRID_W - WIN_COLS)
    col_mask = (ck >= c_start) & (ck < c_start + WIN_COLS)
    band_mask = jnp.broadcast_to(col_mask[:, None, :], (GRID_W, kh, GRID_W)).reshape(GRID_W, kh * GRID_W)
    dc_idx = jnp.clip(ck - cq + WIN_COLS - 1, 0, 2 * WIN_COLS - 2)
    rpb_cols = rpb[:, :, dc_idx]

    def row_block(args):
        q_r, r = args
        r_start = jnp.clip(r - kh // 2, 0, rows - kh)
        k_blk = lax.dynamic_slice_in_dim(k_grid, r_start, kh, axis=2).reshape(B, H, kh * GRID_W, hd)
        v_blk = lax.dynamic_slice_in_dim(v_grid, r_start, kh, axis=2).reshape(B, H, kh * GRID_W, hd)
        dr_idx = r_start + jnp.arange(kh) - r + WIN_ROWS_MAX - 1
        bias = jnp.take(rpb_cols, dr_idx, axis=1)
        bias = bias.transpose(0, 2, 1, 3).reshape(H, GRID_W, kh * GRID_W).astype(jnp.float32)
        s_loc = jnp.einsum('bhqd,bhkd->bhqk', q_r, k_blk, preferred_element_type=jnp.float32) * scale + bias
        s_loc = jnp.where(band_mask, s_loc, NEG_INF)
        s_ctx = jnp.einsum('bhqd,bhkd->bhqk', q_r, k_ctx, preferred_element_type=jnp.float32) * scale
        p = jax.nn.softmax(jnp.concatenate([s_loc, s_ctx], axis=-1), axis=-1).astype(v.dtype)
        n_loc = kh * GRID_W
        return (jnp.einsum('bhqk,bhkd->bhqd', p[..., :n_loc], v_blk)
                + jnp.einsum('bhqk,bhkd->bhqd', p[..., n_loc:], v_ctx))

    o = lax.map(row_block, (q_rows, jnp.arange(rows)))
    return o.transpose(1, 0, 3, 2, 4).reshape(B, N, H * hd)

def context_attention(q_c, k_c, v_c):
    s = jnp.einsum('bhqd,bhkd->bhqk', q_c, k_c, preferred_element_type=jnp.float32) * (HEAD_DIM ** -0.5)
    p = jax.nn.softmax(s, axis=-1).astype(v_c.dtype)
    o = jnp.einsum('bhqk,bhkd->bhqd', p, v_c)
    return o.transpose(0, 2, 1, 3).reshape(q_c.shape[0], q_c.shape[2], D_ATT)

def conformer_conv(glu_in, conv_w, conv_b, ln_g, ln_b, w_out):
    a, g = jnp.split(glu_in, 2, axis=-1)
    u = a * jax.nn.sigmoid(g)
    y = lax.conv_general_dilated(u, conv_w[:, None, :].astype(u.dtype), window_strides=(1,),
                                 padding=[(CONV_WIDTH // 2, CONV_WIDTH // 2)],
                                 dimension_numbers=('NWC', 'WIO', 'NWC'),
                                 feature_group_count=D_CONV) + conv_b
    y = jax.nn.silu(layernorm(y, ln_g, ln_b))
    return y @ w_out

def merge_branches(proj, att, conv_w, conv_b, ln_g, ln_b, w_att_out, w_conv_out, w_o):
    y_att = att @ w_att_out
    y_conv = conformer_conv(proj[..., GLU0:GA0], conv_w, conv_b, ln_g, ln_b, w_conv_out)
    gate_att = jax.nn.sigmoid(proj[..., GA0:GB0])
    gate_conv = jax.nn.sigmoid(proj[..., GB0:D_IN])
    return (gate_att * y_att + gate_conv * y_conv) @ w_o

def hierarchical_moe(h, w_rg, b_rg, w_re, b_re, w_g, w_u, w_d):
    T, D = h.shape
    hf = h.astype(jnp.float32)
    g_logits = hf @ w_rg.astype(jnp.float32) + b_rg.astype(jnp.float32)
    g_idx = jnp.argmax(g_logits, axis=-1)
    p_group = jnp.take_along_axis(jax.nn.softmax(g_logits, axis=-1), g_idx[:, None], axis=-1)
    e_logits = (hf @ w_re.astype(jnp.float32) + b_re.astype(jnp.float32)).reshape(T, N_GROUPS, EXPERTS_PER_GROUP)
    e_sel = jnp.take_along_axis(e_logits, g_idx[:, None, None], axis=1)[:, 0]
    top_v, top_i = lax.top_k(e_sel, TOP_K_IN_GROUP)
    gate = p_group * jax.nn.softmax(top_v, axis=-1)
    flat_e = (g_idx[:, None] * EXPERTS_PER_GROUP + top_i).reshape(-1)
    flat_tok = jnp.repeat(jnp.arange(T), TOP_K_IN_GROUP)
    flat_w = gate.reshape(-1)
    A = T * TOP_K_IN_GROUP
    order = jnp.argsort(flat_e)
    e_s, tok_s, w_s = flat_e[order], flat_tok[order], flat_w[order]
    counts = jnp.bincount(flat_e, length=N_EXPERTS)
    padded = (counts + MOE_BLOCK - 1) // MOE_BLOCK * MOE_BLOCK
    pad_end = jnp.cumsum(padded)
    pad_start = pad_end - padded
    start = jnp.cumsum(counts) - counts
    dest = pad_start[e_s] + (jnp.arange(A) - start[e_s])
    n_blocks = -(-A // MOE_BLOCK) + N_EXPERTS
    P = n_blocks * MOE_BLOCK
    row_tok = jnp.zeros((P,), jnp.int32).at[dest].set(tok_s.astype(jnp.int32))
    row_w = jnp.zeros((P,), jnp.float32).at[dest].set(w_s)
    block_e = jnp.clip(jnp.searchsorted(pad_end, jnp.arange(n_blocks) * MOE_BLOCK, side='right'), 0, N_EXPERTS - 1)

    def run_block(args):
        tok, e, wt = args
        xb = h[tok]
        y = (jax.nn.silu(xb @ w_g[e]) * (xb @ w_u[e])) @ w_d[e]
        return y.astype(jnp.float32) * wt[:, None]

    ys = lax.map(run_block, (row_tok.reshape(n_blocks, MOE_BLOCK), block_e, row_w.reshape(n_blocks, MOE_BLOCK)))
    out = jnp.zeros((T, D), jnp.float32).at[row_tok].add(ys.reshape(P, D))
    return out.astype(h.dtype)

def first_inputs(seed: int = 0) -> dict:
    key = jax.random.key(seed)
    ks = jax.random.split(key, 25)
    L, D = DEPTH, D_MODEL

    def nrm(k, shape, s):
        return jax.random.normal(k, shape, jnp.float32) * s

    return {
        "x": nrm(ks[0], (BATCH, SEQ, D), 1.0),
        "c": nrm(ks[1], (BATCH, D), 1.0),
        "ctx": nrm(ks[2], (BATCH, CTX_LEN, D), 1.0),
        "c_ctx": nrm(ks[3], (D,), 1.0),
        "w_mod": nrm(ks[4], (L, D, 6 * D), 0.5 * D ** -0.5),
        "b_mod": nrm(ks[5], (L, 6 * D), 0.01),
        "norm_mix": 1.0 + nrm(ks[6], (L, D), 0.02),
        "w_in": nrm(ks[7], (L, D, D_IN), D ** -0.5),
        "rpb": nrm(ks[8], (L, N_HEADS, 2 * WIN_ROWS_MAX - 1, 2 * WIN_COLS - 1), 0.1),
        "w_att_out": nrm(ks[9], (L, D_ATT, D), D_ATT ** -0.5),
        "conv_w": nrm(ks[10], (L, CONV_WIDTH, D_CONV), CONV_WIDTH ** -0.5),
        "conv_b": nrm(ks[11], (L, D_CONV), 0.01),
        "conv_ln_g": 1.0 + nrm(ks[12], (L, D_CONV), 0.02),
        "conv_ln_b": nrm(ks[13], (L, D_CONV), 0.01),
        "w_conv_out": nrm(ks[14], (L, D_CONV, D), D_CONV ** -0.5),
        "w_o": nrm(ks[15], (L, D, D), D ** -0.5),
        "norm_ffn": 1.0 + nrm(ks[16], (L, D), 0.02),
        "w_router_group": nrm(ks[17], (L, D, N_GROUPS), D ** -0.5),
        "b_router_group": nrm(ks[18], (L, N_GROUPS), 0.01),
        "w_router_expert": nrm(ks[19], (L, D, N_EXPERTS), D ** -0.5),
        "b_router_expert": nrm(ks[20], (L, N_EXPERTS), 0.01),
        "w_exp_gate": nrm(ks[21], (L, N_EXPERTS, D, D_EXPERT), D ** -0.5),
        "w_exp_up": nrm(ks[22], (L, N_EXPERTS, D, D_EXPERT), D ** -0.5),
        "w_exp_down": nrm(ks[23], (L, N_EXPERTS, D_EXPERT, D), D_EXPERT ** -0.5),
        "final_norm": 1.0 + nrm(ks[24], (D,), 0.02),
    }

def first_block(x, c, ctx, c_ctx, w_mod, b_mod, norm_mix, w_in, rpb, w_att_out, conv_w, conv_b,
              conv_ln_g, conv_ln_b, w_conv_out, w_o, norm_ffn, w_router_group, b_router_group,
              w_router_expert, b_router_expert, w_exp_gate, w_exp_up, w_exp_down, final_norm):
    B, N, D = x.shape
    n_ctx = ctx.shape[1]
    for l in range(DEPTH):
        last = l == DEPTH - 1
        m_lat = jax.nn.silu(c) @ w_mod[l] + b_mod[l]
        sh1, sc1, g1, sh2, sc2, g2 = jnp.split(m_lat[:, None, :], 6, axis=-1)
        m_ctx = jax.nn.silu(c_ctx) @ w_mod[l] + b_mod[l]
        sh1c, sc1c, g1c, sh2c, sc2c, g2c = jnp.split(m_ctx, 6, axis=-1)

        h = modulate(rmsnorm(x, norm_mix[l]), sh1, sc1)
        hc = modulate(rmsnorm(ctx, norm_mix[l]), sh1c, sc1c)
        proj = h @ w_in[l]
        q = split_heads(proj[..., Q0:K0])
        k = split_heads(proj[..., K0:V0])
        v = split_heads(proj[..., V0:GLU0])
        if last:
            kv_c = hc @ w_in[l][:, K0:GLU0]
            proj_c = None
        else:
            proj_c = hc @ w_in[l]
            kv_c = proj_c[..., K0:GLU0]
        k_c = split_heads(kv_c[..., :D_ATT]).transpose(0, 2, 1, 3)
        v_c = split_heads(kv_c[..., D_ATT:]).transpose(0, 2, 1, 3)
        att = latent_neighbourhood_attention(q, k, v, k_c, v_c, rpb[l])
        y = merge_branches(proj, att, conv_w[l], conv_b[l], conv_ln_g[l], conv_ln_b[l],
                           w_att_out[l], w_conv_out[l], w_o[l])
        x_mid = x + g1 * y
        h2 = modulate(rmsnorm(x_mid, norm_ffn[l]), sh2, sc2)

        if last:
            tokens = h2.reshape(B * N, D)
        else:
            q_c = split_heads(proj_c[..., Q0:K0]).transpose(0, 2, 1, 3)
            att_c = context_attention(q_c, k_c, v_c)
            y_c = merge_branches(proj_c, att_c, conv_w[l], conv_b[l], conv_ln_g[l], conv_ln_b[l],
                                 w_att_out[l], w_conv_out[l], w_o[l])
            ctx_mid = ctx + g1c * y_c
            h2c = modulate(rmsnorm(ctx_mid, norm_ffn[l]), sh2c, sc2c)
            tokens = jnp.concatenate([h2.reshape(B * N, D), h2c.reshape(B * n_ctx, D)], axis=0)
        f = hierarchical_moe(tokens, w_router_group[l], b_router_group[l], w_router_expert[l],
                             b_router_expert[l], w_exp_gate[l], w_exp_up[l], w_exp_down[l])
        x = x_mid + g2 * f[:B * N].reshape(B, N, D)
        if not last:
            ctx = ctx_mid + g2c * f[B * N:].reshape(B, n_ctx, D)
    return rmsnorm(x, final_norm)


MIX_WIDTH = D_MODEL
POOL_WIDTH = MIX_WIDTH // 2
POOL_WINDOWS = (2, 4, 8, 16)
N_POOL_GROUPS = len(POOL_WINDOWS)
POOL_GROUP_WIDTH = POOL_WIDTH // N_POOL_GROUPS
ATTN_WIDTH = MIX_WIDTH - POOL_WIDTH
N_HEADS_2 = ATTN_WIDTH // HEAD_DIM
IN_WIDTH = POOL_WIDTH + 3 * ATTN_WIDTH + N_HEADS_2
D_FF = 4 * D_MODEL
BLOCK_Q = 128
LN_EPS = 1e-5
NEG_INF_2 = -1e30
ALPHA = float((2.0 * DEPTH) ** 0.25)
BETA = float((8.0 * DEPTH) ** -0.25)


def layer_norm(x, g, b):
    xf = x.astype(jnp.float32)
    mu = jnp.mean(xf, axis=-1, keepdims=True)
    var = jnp.mean(jnp.square(xf - mu), axis=-1, keepdims=True)
    y = (xf - mu) * lax.rsqrt(var + LN_EPS)
    return (y * g.astype(jnp.float32) + b.astype(jnp.float32)).astype(x.dtype)

def pool_mixer(u, w, scale):
    B, S, _ = u.shape
    uf = u.astype(jnp.float32)
    c = jnp.cumsum(uf, axis=1)
    pos = jnp.arange(1, S + 1, dtype=jnp.float32)
    diffs = []
    for g, win in enumerate(POOL_WINDOWS):
        sl = slice(g * POOL_GROUP_WIDTH, (g + 1) * POOL_GROUP_WIDTH)
        cg = c[..., sl]
        shifted = jnp.pad(cg, ((0, 0), (win, 0), (0, 0)))[:, :S]
        count = jnp.minimum(pos, float(win))[None, :, None]
        diffs.append((cg - shifted) / count - uf[..., sl])
    d = jnp.concatenate(diffs, axis=-1).astype(u.dtype)
    d = d.reshape(B, S, N_POOL_GROUPS, POOL_GROUP_WIDTH)
    y = jnp.einsum('bsgc,gcd->bsgd', d, w).reshape(B, S, POOL_WIDTH)
    return y * scale

def forgetting_attention(q, k, v, f_logit):
    B, S, _ = q.shape
    to_heads = lambda t: t.reshape(B, S, N_HEADS_2, HEAD_DIM).transpose(0, 2, 1, 3)
    q, k, v = to_heads(q), to_heads(k), to_heads(v)
    log_f = jax.nn.log_sigmoid(f_logit.astype(jnp.float32)).transpose(0, 2, 1)
    cf = jnp.cumsum(log_f, axis=-1)
    scale = HEAD_DIM ** -0.5
    kpos = jnp.arange(S)
    n_blocks = S // BLOCK_Q

    def one_block(i):
        start = i * BLOCK_Q
        qb = lax.dynamic_slice_in_dim(q, start, BLOCK_Q, axis=2)
        cq = lax.dynamic_slice_in_dim(cf, start, BLOCK_Q, axis=2)
        qpos = start + jnp.arange(BLOCK_Q)
        s = jnp.einsum('bhqd,bhkd->bhqk', qb, k, preferred_element_type=jnp.float32) * scale
        s = s + cq[..., :, None] - cf[..., None, :]
        s = jnp.where(kpos[None, :] <= qpos[:, None], s, NEG_INF_2)
        p = jax.nn.softmax(s, axis=-1)
        return jnp.einsum('bhqk,bhkd->bhqd', p.astype(v.dtype), v)

    out = lax.map(one_block, jnp.arange(n_blocks))
    out = out.transpose(1, 0, 3, 2, 4).reshape(B, S, ATTN_WIDTH)
    return out

def hybrid_mixer(x, w_in, b_f, pool_w, pool_scale, w_out):
    h = x @ w_in
    o = 0
    u = h[..., o:o + POOL_WIDTH]; o += POOL_WIDTH
    q = h[..., o:o + ATTN_WIDTH]; o += ATTN_WIDTH
    k = h[..., o:o + ATTN_WIDTH]; o += ATTN_WIDTH
    v = h[..., o:o + ATTN_WIDTH]; o += ATTN_WIDTH
    f_logit = h[..., o:o + N_HEADS_2] + b_f
    pool_out = pool_mixer(u, pool_w, pool_scale)
    attn_out = forgetting_attention(q, k, v, f_logit)
    return jnp.concatenate([pool_out, attn_out], axis=-1) @ w_out

def second_inputs(seed: int = 0) -> dict:
    key = jax.random.key(seed)
    ks = jax.random.split(key, 12)
    f32 = jnp.float32
    x = jax.random.normal(ks[0], (BATCH, SEQ, D_MODEL), f32)
    w_in = jax.random.normal(ks[1], (DEPTH, D_MODEL, IN_WIDTH), f32) * D_MODEL ** -0.5
    col_scale = np.ones((IN_WIDTH,), np.float32)
    col_scale[:POOL_WIDTH] = BETA
    col_scale[POOL_WIDTH + 2 * ATTN_WIDTH:POOL_WIDTH + 3 * ATTN_WIDTH] = BETA
    w_in = w_in * jnp.asarray(col_scale)
    b_f = 3.0 + 0.5 * jax.random.normal(ks[2], (DEPTH, N_HEADS_2), f32)
    pool_w = jax.random.normal(ks[3], (DEPTH, N_POOL_GROUPS, POOL_GROUP_WIDTH, POOL_GROUP_WIDTH), f32) * POOL_GROUP_WIDTH ** -0.5
    pool_scale = 1.0 + 0.1 * jax.random.normal(ks[4], (DEPTH, POOL_WIDTH), f32)
    w_out = jax.random.normal(ks[5], (DEPTH, MIX_WIDTH, D_MODEL), f32) * (MIX_WIDTH ** -0.5 * BETA)
    ln1_g = 1.0 + 0.05 * jax.random.normal(ks[6], (DEPTH, D_MODEL), f32)
    ln1_b = 0.02 * jax.random.normal(ks[7], (DEPTH, D_MODEL), f32)
    w_mlp1 = jax.random.normal(ks[8], (DEPTH, D_MODEL, D_FF), f32) * D_MODEL ** -0.5
    w_mlp2 = jax.random.normal(ks[9], (DEPTH, D_FF, D_MODEL), f32) * (D_FF ** -0.5 * BETA)
    ln2_g = 1.0 + 0.05 * jax.random.normal(ks[10], (DEPTH, D_MODEL), f32)
    ln2_b = 0.02 * jax.random.normal(ks[11], (DEPTH, D_MODEL), f32)
    return {"x": x, "w_in": w_in, "b_f": b_f, "pool_w": pool_w, "pool_scale": pool_scale,
            "w_out": w_out, "ln1_g": ln1_g, "ln1_b": ln1_b, "w_mlp1": w_mlp1,
            "w_mlp2": w_mlp2, "ln2_g": ln2_g, "ln2_b": ln2_b}

def second_block(x, w_in, b_f, pool_w, pool_scale, w_out, ln1_g, ln1_b, w_mlp1, w_mlp2, ln2_g, ln2_b):
    for l in range(DEPTH):
        mix = hybrid_mixer(x, w_in[l], b_f[l], pool_w[l], pool_scale[l], w_out[l])
        x = layer_norm(ALPHA * x + mix, ln1_g[l], ln1_b[l])
        hid = jnp.square(jax.nn.relu(x @ w_mlp1[l]))
        x = layer_norm(ALPHA * x + hid @ w_mlp2[l], ln2_g[l], ln2_b[l])
    return x


def setup_inputs(seed=0):
    out = dict(first_inputs(seed))
    for name, value in second_inputs(seed + 1).items():
        if name != "x":
            out[name + "_2"] = value
    return out


def reference(
    x, c, ctx, c_ctx, w_mod, b_mod, norm_mix, w_in, rpb, w_att_out, conv_w, conv_b, conv_ln_g,
    conv_ln_b, w_conv_out, w_o, norm_ffn, w_router_group, b_router_group, w_router_expert,
    b_router_expert, w_exp_gate, w_exp_up, w_exp_down, final_norm, w_in_2, b_f_2, pool_w_2,
    pool_scale_2, w_out_2, ln1_g_2, ln1_b_2, w_mlp1_2, w_mlp2_2, ln2_g_2, ln2_b_2,
):
    x = first_block(
        x, c, ctx, c_ctx, w_mod, b_mod, norm_mix, w_in, rpb, w_att_out, conv_w, conv_b,
        conv_ln_g, conv_ln_b, w_conv_out, w_o, norm_ffn, w_router_group, b_router_group,
        w_router_expert, b_router_expert, w_exp_gate, w_exp_up, w_exp_down, final_norm,
    )
    return second_block(
        x, w_in_2, b_f_2, pool_w_2, pool_scale_2, w_out_2, ln1_g_2, ln1_b_2, w_mlp1_2, w_mlp2_2,
        ln2_g_2, ln2_b_2,
    )


_drawn_inputs = setup_inputs


def setup_inputs(seed=0):
    import zlib

    import numpy as np

    out = dict(_drawn_inputs(seed))
    spreads = {}
    factors = {'ctx': 2.951,
     'b_mod': 4.598,
     'norm_mix': 8.0,
     'rpb': 8.0,
     'conv_b': 8.0,
     'conv_ln_g': 8.0,
     'conv_ln_b': 8.0,
     'norm_ffn': 3.773,
     'b_router_group': 8.0,
     'b_router_expert': 8.0,
     'final_norm': 2.734,
     'b_f_2': 64.0,
     'pool_scale_2': 3.064,
     'ln2_b_2': 2.667}
    for name, (base, spread) in spreads.items():
        noise = np.random.default_rng([zlib.crc32(name.encode()), seed]).standard_normal(out[name].shape)
        drawn = base * np.exp(spread * noise) if base else spread * noise
        out[name] = __import__('jax').numpy.asarray(drawn.astype(out[name].dtype))
    for name, factor in factors.items():
        out[name] = (out[name] * factor).astype(out[name].dtype)
    return out
```

```python
from contextlib import ExitStack

import concourse.bass as bass
from concourse import mybir

F32 = mybir.dt.float32
F32R = mybir.dt.float32r
I32 = mybir.dt.int32
U32 = mybir.dt.uint32
ALU = mybir.AluOpType
ACT = mybir.ActivationFunctionType
AX = mybir.AxisListType

P = 128
D = 1024
SEQ = 512
CTX = 256
KC = D // P
TC = SEQ // P
HEADS = 8
HD = 64
N_EXPERTS = 32
NB_MAX = 2 * SEQ // P + N_EXPERTS
NBX = 48
NORM_EPS = 1e-6
LN_EPS = 1e-5
NEG = -1.0e30
RAW = 4
SPLIT = 4
ALPHA = float(2.0 ** 0.25)


GRID = 64
WIN = 16
TAPS = 31
HALF = TAPS // 2
NDC = 2 * WIN - 1
NDR = 15
NM = NDR - 1
RING = 3


def mixer_stage(nc, cst, x_mid, mod_col, vec_all, w, dram):
    used = []
    with ExitStack() as ctx:
        def sb(name, shape, dt=F32):
            return ctx.enter_context(nc.sbuf_tensor("mixer_" + name, shape, dt))

        def sem(name):
            used.append(ctx.enter_context(nc.semaphore("mixer_" + name)))
            return used[-1]

        bank = [ctx.enter_context(nc.psum_tensor(f"mixer_bank{i}", [P, 512], F32)) for i in range(8)]
        ident, ones = cst["ident"], cst["ones"]
        raw = [sb(f"a_raw{i}", [P, 2048]) for i in range(RING)]
        w_hi = [sb(f"a_hi{i}", [P, 2048], F32R) for i in range(2)]
        w_lo = [sb(f"a_lo{i}", [P, 2048], F32R) for i in range(2)]
        h_hi = sb("h_hi", [P, KC, SEQ], F32R)
        h_lo = sb("h_lo", [P, KC, SEQ], F32R)
        g_hi = sb("ag_hi", [P, KC, SEQ], F32R)
        g_lo = sb("ag_lo", [P, KC, SEQ], F32R)
        vals = sb("vals", [P, 4096])
        table = sb("table", [P, NM * HEADS * GRID])
        work = sb("a_work", [P, 4096])
        y_conv = sb("y_conv", [P, 4, SEQ])
        conv_w = sb("conv_w_col", [P, 128])
        c_silu = sb("c_silu", [P, KC, 2])
        mod_ctx = sb("mod_ctx", [P, 16])
        s1 = sb("s1", [P, 16])
        ssq = sb("a_ssq", [P, 8])
        IT = [(h, i) for h in range(HEADS) for i in range(TC)]
        NIT = len(IT)
        m_loc = sb("m_loc", [P, NIT])
        m_ctx = sb("m_ctx", [P, NIT])
        m_neg = sb("m_neg", [P, NIT])
        r_loc = sb("r_loc", [P, NIT])
        r_ctx = sb("r_ctx", [P, NIT])

        k_t, q_t, m = x_mid[:, 0:4, :], x_mid[:, 4:8, :], x_mid
        v_t = vals[:, 0:2048].rearrange("p (t d) -> p t d", t=TC)
        kc_t = vals[:, 2048:3072].rearrange("p (c t) -> p c t", c=4)
        vc_t = vals[:, 3072:4096].rearrange("p (t d) -> p t d", t=2)
        gate_c = vals[:].rearrange("p (c t) -> p c t", c=KC)
        x_rows = table[:, 0:4096].rearrange("p (t d) -> p t d", t=TC)
        c_rows = table[:, 4096:6144].rearrange("p (t d) -> p t d", t=2)
        vec_rows = table[:, 6144:6272]
        conv_rows = table[:, 6272:6400]
        cond_rows = table[:, 6400:6528]
        rpb_rows = table[:, 6528:6528 + NDC]
        bias = table[:].rearrange("p (h m c) -> p h m c", h=HEADS, m=NM)
        UW = SEQ + 2 * HALF
        u_pad = work[:, 0:4 * UW].rearrange("p (c t) -> p c t", c=4)
        sig = [work[:, 2176 + 512 * i:2688 + 512 * i] for i in range(2)]
        tmp = [work[:, 2176 + 512 * i:2688 + 512 * i] for i in range(2)]
        onehot = work[:, 3200:3200 + 192]
        rpb_t = work[:, 3400:3520]
        junk = work[:, 0:1024]
        s_t = [work[:, 768 * i:768 * i + 768] for i in range(2)]
        pt_t = [work[:, 1536 + 768 * i:2304 + 768 * i] for i in range(2)]
        att = [work[:, 3072 + 512 * i:3584 + 512 * i].rearrange("p (i d) -> p i d", i=TC) for i in range(2)]
        sq = work[:, 0:2048].rearrange("p (c t) -> p c t", c=4)
        mean_t = work[:, 2048:2560]
        rstd = work[:, 2560:3072]

        NV = 120
        V_BMOD, V_NORM, V_CB, V_CG, V_CO = 0, 48, 56, 60, 64

        MOD = [("mod", 256 * j) for j in range(24)]
        W_IN = [("in", c) for c in (2048, 1536, 2304, 1792, 512, 768, 1024, 1280, 0, 256,
                                    2560, 2816, 3072, 3328)]
        W_ATT = [("att", 512 * j) for j in range(2)]
        W_GB = [("in", 3584 + 256 * j) for j in range(4)]
        W_CONV = [("conv", 512 * j) for j in range(2)]
        W_O = [("o", 256 * j) for j in range(4)]
        SPLITS = W_IN + W_ATT + W_GB + W_CONV + W_O
        NS = len(SPLITS)
        STREAM = MOD[0:8] + SPLITS[0:12] + MOD[8:24] + SPLITS[12:]
        place = {}
        nmod = nsplit = 0
        for pos, (kind, _) in enumerate(STREAM):
            if kind == "mod":
                place["mod", nmod] = pos
                nmod += 1
            else:
                place["split", nsplit] = pos
                nsplit += 1
        where = {pos: key for key, pos in place.items()}

        def name_of(s):
            return ("glu_g glu_a glu_g glu_a k k v v q q ga ga ga ga att att gb gb gb gb "
                    "conv conv o o o o").split()[s]

        COUNT = {"glu_g": 2, "glu_a": 2, "k": 3, "v": 3, "q": 2, "ga": 2, "att": 4, "gb": 2, "conv": 4, "o": 2}
        READER = {"glu_g": "act", "glu_a": "dve", "k": "act", "v": "act", "q": "act", "ga": "act", "att": "dve",
                  "gb": "act", "conv": "dve", "o": "dve"}
        TILES = [(s, k) for s in range(NS) for k in range(COUNT[name_of(s)])]
        first_tile = [min(t for t, (s, _) in enumerate(TILES) if s == u) for u in range(NS)] + [len(TILES)]

        def reads_upto(engine, t):
            return sum(1 for (s, _) in TILES[:t + 1] if READER[name_of(s)] == engine)

        rows_landed = sem("rows_landed")
        cond_landed = sem("cond_landed")
        vec_landed = sem("vec_landed")
        again_landed = sem("again_landed")
        raw_landed = [sem(f"a_landed{i}") for i in range(RING)]
        pool_step = sem("a_pool_step")
        dve_step = sem("a_dve_step")
        ident_ready = sem("ident_ready")
        onehot_ready = sem("onehot_ready")
        pad_ready = sem("pad_ready")
        vt_ready = sem("vt_ready")
        vt_used = sem("vt_used")
        rpbt_ready = sem("rpbt_ready")
        silu_ready = sem("silu_ready")
        mod_done = sem("mod_done")
        s1_ready = sem("s1_ready")
        ssq_done = sem("a_ssq_done")
        var_ready = sem("a_var_ready")
        std_ready = sem("a_std_ready")
        scaled = sem("scaled")
        ht_ready = sem("ht_ready")
        tmp_ready = sem("tmp_ready")
        hhi_done = sem("hhi_done")
        hlo_done = sem("hlo_done")
        hi_done = sem("a_hi_done")
        lo_done = sem("a_lo_done")
        acc_ready = sem("a_acc_ready")
        read_act = sem("acc_read_by_act")
        read_dve = sem("acc_read_by_dve")
        tb_ready = sem("tb_ready")
        tb_used = sem("tb_used")
        masked = sem("masked")
        tap_done = sem("tap_done")
        s_ready = sem("as_ready")
        sc_ready = sem("asc_ready")
        s_used = sem("as_used")
        mc_ready = sem("amc_ready")
        m_ready = sem("am_ready")
        p_ready = sem("ap_ready")
        pt_ready = sem("apt_ready")
        pt_used = sem("apt_used")
        o_ready = sem("ao_ready")
        o_used = sem("ao_used")
        at_ready = sem("aat_ready")
        athi_done = sem("athi_done")
        atlo_done = sem("atlo_done")
        mean_ready = sem("a_mean_ready")
        cent_ready = sem("a_cent_ready")
        sq_ready = sem("a_sq_ready")
        cssq_ready = sem("cssq_ready")
        cvar_ready = sem("cvar_ready")
        cstd_ready = sem("cstd_ready")
        cn_ready = sem("cn_ready")
        act_step = sem("a_act_step")
        cvhi_done = sem("cvhi_done")
        cvlo_done = sem("cvlo_done")
        m_done = sem("m_done")
        mhi_done = sem("mhi_done")
        mlo_done = sem("mlo_done")
        xt_ready = sem("xt_ready")
        xt_used = sem("xt_used")

        w_in = w["w_in"][0].rearrange("(k p) n -> p k n", p=P)
        w_mod = w["w_mod"][0].rearrange("(k p) n -> p k n", p=P)
        w_att = w["w_att_out"][0].rearrange("(k p) n -> p k n", p=P)
        w_cv = w["w_conv_out"][0].rearrange("(k p) n -> p k n", p=P)
        w_o = w["w_o"][0].rearrange("(k p) n -> p k n", p=P)

        def as_k8(t):
            return t[:].rearrange("p (k n) -> p k n", k=KC)

        def as_k4(t):
            return t[:].rearrange("p (k n) -> p k n", k=4)

        def free_slot(engine, pos):
            if pos >= RING:
                kind, idx = where[pos - RING]
                if kind == "mod":
                    engine.wait_ge(mod_done, 2 * (idx + 1))
                else:
                    engine.wait_ge(lo_done, idx + 1)

        def wait_landed(engine, pos):
            engine.wait_ge(raw_landed[pos % RING], 16 * (pos // RING + 1))

        block = ctx.enter_context(nc.Block())

        @block.sync
        def _(sp):
            sp.dma_start(cond_rows[0:KC, :], w["c"][0].rearrange("(k p) -> k p", p=P)).then_inc(cond_landed, 16)
            sp.dma_start(cond_rows[KC:2 * KC, :], w["c_ctx"].rearrange("(k p) -> k p", p=P)).then_inc(cond_landed, 16)
            for pos, (kind, col) in enumerate(STREAM):
                free_slot(sp, pos)
                if kind in ("att", "conv"):
                    src = (w_att if kind == "att" else w_cv)[:, :, col:col + 512]
                    dst = as_k4(raw[pos % RING])
                else:
                    src = {"mod": w_mod, "in": w_in, "o": w_o}[kind][:, :, col:col + 256]
                    dst = as_k8(raw[pos % RING])
                sp.dma_start(dst, src).then_inc(raw_landed[pos % RING], 16)
                if pos == 1:
                    sp.dma_start(x_rows, w["x"][0].rearrange("(t p) d -> p t d", p=P)).then_inc(rows_landed, 16)
                    sp.dma_start(c_rows, w["ctx"][0].rearrange("(t p) d -> p t d", p=P)).then_inc(rows_landed, 16)

        @block.gpsimd
        def _(pool):
            n = [0]

            def step(ins):
                n[0] += 1
                ins.then_inc(pool_step, 1)
                pool.wait_ge(pool_step, n[0])

            step(pool.memset(ident[:], 1.0))
            step(pool.affine_select(out=ident[:], in_=ident[:], compare_op=ALU.is_equal, fill=0.0, base=0,
                                    pattern=[[-1, P]], channel_multiplier=1))
            pool.memset(ones[:], 1.0).then_inc(ident_ready, 1)
            step(pool.memset(onehot, 0.0))
            for at in (GRID + NDC // 2 - 1, 2 * GRID + NDC // 2 - 1):
                ins = pool.affine_select(out=onehot, in_=onehot, compare_op=ALU.not_equal, fill=1.0, base=-at,
                                         pattern=[[1, 192]], channel_multiplier=1)
                if at < 2 * GRID:
                    step(ins)
                else:
                    ins.then_inc(onehot_ready, 1)
            pool.wait_ge(ssq_done, 6)
            pool.memset(u_pad[:, :, 0:HALF], 0.0)
            pool.memset(u_pad[:, :, HALF + SEQ:UW], 0.0).then_inc(pad_ready, 1)
            pool.wait_ge(tb_used, 16)
            for half in (0, 64):
                flat = bias[half:half + 64, :, :, :].rearrange("p h m c -> p (h m) c")
                step(pool.affine_select(out=flat[:, :, 0:GRID - WIN], in_=flat[:, :, 0:GRID - WIN],
                                        compare_op=ALU.is_ge, fill=NEG, base=WIN // 2,
                                        pattern=[[0, HEADS * NM], [1, GRID - WIN]], channel_multiplier=-1))
                pool.affine_select(out=flat[:, :, WIN:GRID], in_=flat[:, :, WIN:GRID],
                                   compare_op=ALU.is_ge, fill=NEG, base=WIN // 2 - 1 - WIN,
                                   pattern=[[0, HEADS * NM], [-1, GRID - WIN]], channel_multiplier=1)\
                    .then_inc(masked, 1)
            pool.wait_ge(s_used, NIT)
            pool.dma_start(x_rows, w["x"][0].rearrange("(t p) d -> p t d", p=P)).then_inc(again_landed, 16)
            pool.wait_ge(again_landed, 16)

        @block.scalar
        def _(act):
            for i, (name, a) in enumerate((("b_mod", 0), ("norm_mix", 48), ("conv_b", 56), ("conv_ln_g", 60),
                                           ("conv_ln_b", 64), ("norm_ffn", 68), ("final_norm", 76),
                                           ("pool_scale_2", 84), ("ln1_g_2", 88), ("ln1_b_2", 96),
                                           ("ln2_g_2", 104), ("ln2_b_2", 112))):
                src = w[name] if name == "final_norm" else w[name][0]
                rows = src.shape[0] // P
                act.dma_start(vec_rows[a:a + rows, :], src.rearrange("(k p) -> k p", p=P)).then_inc(vec_landed, 16)
            act.dma_start(conv_rows[0:4 * TAPS, :], w["conv_w"][0].rearrange("t (c p) -> (t c) p", p=P))\
               .then_inc(vec_landed, 16)
            act.dma_start(rpb_rows[0:HEADS * NDR, :], w["rpb"][0].rearrange("h r c -> (h r) c"))\
               .then_inc(vec_landed, 16)
            act.wait_ge(vt_ready, 1)
            act.activation(c_silu[:].rearrange("p k s -> p s k"),
                           bank[0][:, 0:16].rearrange("p (s k) -> p s k", s=2), ACT.Silu).then_inc(silu_ready, 1)
            act.wait_ge(rows_landed, 32)
            for t in range(6):
                src = x_rows[:, t, :] if t < 4 else c_rows[:, t - 4, :]
                act.activation(junk, src, ACT.Square, accum_out=ssq[:, t:t + 1]).then_inc(ssq_done, 1)
                act.wait_ge(ssq_done, t + 1)
            act.wait_ge(var_ready, 1)
            act.activation(ssq[:, 0:6], ssq[:, 0:6], ACT.Sqrt).then_inc(std_ready, 1)

            def high(s):
                pos = place["split", s]
                if s >= 2:
                    act.wait_ge(acc_ready, first_tile[s - 1])
                wait_landed(act, pos)
                act.activation(w_hi[s % 2][:], raw[pos % RING][:], ACT.Copy).then_inc(hi_done, 1)

            for c in range(2 * KC):
                act.wait_ge(tmp_ready, c + 1)
                if c < KC:
                    act.activation(h_hi[:, c, :], tmp[c % 2], ACT.Copy).then_inc(hhi_done, 1)
                else:
                    act.activation(g_hi[:, c - KC, 0:CTX], tmp[c % 2][:, 0:CTX], ACT.Copy).then_inc(hhi_done, 1)
                if c == KC - 1:
                    high(0)
                    high(1)

            def table_part(b):
                act.wait_ge(tb_ready, b + 1)
                src = bank[(4, 5, 6)[b % 3]][:, 0:480].rearrange("p (c h m) -> p h m c", c=4, h=HEADS)
                act.activation(bias[0:64, :, :, 4 * b:4 * b + 4], src[0:64, :, 1:NDR, :], ACT.Copy)
                act.activation(bias[64:128, :, :, 4 * b:4 * b + 4], src[64:128, :, 0:NM, :], ACT.Copy)\
                   .then_inc(tb_used, 1)

            def read_tiles(s):
                name = name_of(s)
                for t in range(first_tile[s], first_tile[s + 1]):
                    k = t - first_tile[s]
                    src = bank[t % 4]
                    act.wait_ge(acc_ready, t + 1)
                    if name == "glu_g":
                        if s == 2:
                            act.wait_ge(read_dve, k + 1)
                        else:
                            act.wait_ge(hlo_done, 2 * KC - 1 + k)
                        ins = act.activation(sig[k], src[:], ACT.Sigmoid)
                    elif name == "k":
                        j = s - 4
                        if k < 2:
                            ins = act.activation(k_t[:, 2 * j + k, :], src[:], ACT.Copy)
                        else:
                            ins = act.activation(kc_t[:, 2 * j:2 * j + 2, :],
                                                 src[:].rearrange("p (c t) -> p c t", c=2), ACT.Copy)
                    elif name == "v":
                        j = 256 * (s - 6)
                        dst = v_t[:, 2 * k:2 * k + 2, j:j + 256] if k < 2 else vc_t[:, :, j:j + 256]
                        ins = act.activation(dst, src[:].rearrange("p (t d) -> p t d", t=2), ACT.Copy)
                    elif name == "q":
                        ins = act.activation(q_t[:, 2 * (s - 8) + k, :], src[:], ACT.Copy, scale=HD ** -0.5)
                    elif name == "ga":
                        ins = act.activation(m[:, 2 * (s - 10) + k, :], src[:], ACT.Sigmoid)
                    else:
                        ins = act.activation(gate_c[:, 2 * (s - 16) + k, :], src[:], ACT.Sigmoid)
                    ins.then_inc(read_act, 1)

            for s in range(10):
                if 4 <= s < 8:
                    for b in range(4 * (s - 4), 4 * (s - 3)):
                        table_part(b)
                if READER[name_of(s)] == "act":
                    read_tiles(s)
                high(s + 2)

            def p_transposed(n):
                act.wait_ge(pt_ready, n + 1)
                if n >= 2:
                    act.wait_ge(o_ready, n - 1)
                act.activation(pt_t[n % 2][:, 0:512], bank[3 + n % 2][:], ACT.Copy)
                act.activation(pt_t[n % 2][:, 512:768], bank[5][:, 0:CTX], ACT.Copy)\
                   .then_inc(pt_used, 1)

            def att_high(pair):
                act.wait_ge(at_ready, pair + 1)
                act.activation(g_hi[:, pair, :], bank[6][:], ACT.Copy).then_inc(athi_done, 1)

            for n in range(NIT):
                act.wait_ge(m_ready, n + 1)
                act.activation(s_t[n % 2][:, 0:512], s_t[n % 2][:, 0:512], ACT.Exp, bias=m_neg[:, n:n + 1],
                               accum_out=r_loc[:, n:n + 1])
                act.activation(s_t[n % 2][:, 512:768], bank[2][:, 0:CTX], ACT.Exp,
                               bias=m_neg[:, n:n + 1], accum_out=r_ctx[:, n:n + 1]).then_inc(p_ready, 1)
                if n >= 1:
                    p_transposed(n - 1)
                if n >= 12 and n % 8 == 4:
                    att_high(n // 8 - 1)
            p_transposed(NIT - 1)
            att_high(3)

            def norm_squares():
                for c in range(4):
                    act.wait_ge(cent_ready, c + 1)
                    act.activation(sq[:, c, :], y_conv[:, c, :], ACT.Square).then_inc(sq_ready, 1)

            def norm_root():
                act.wait_ge(cvar_ready, 1)
                act.activation(rstd, rstd, ACT.Sqrt).then_inc(cstd_ready, 1)

            def norm_silu():
                for c in range(4):
                    act.wait_ge(cn_ready, c + 1)
                    act.activation(y_conv[:, c, :], y_conv[:, c, :], ACT.Silu,
                                   scale=vec_all[:, V_CG + c:V_CG + c + 1], bias=vec_all[:, V_CO + c:V_CO + c + 1])\
                       .then_inc(act_step, 1)
                for c in range(4):
                    act.wait_ge(act_step, c + 1)
                    act.activation(g_hi[:, 4 + c, :], y_conv[:, c, :], ACT.Copy).then_inc(cvhi_done, 1)

            def merged_high(c):
                act.wait_ge(m_done, c + 1)
                act.activation(h_hi[:, c, :], m[:, c, :], ACT.Copy).then_inc(mhi_done, 1)

            for s in range(10, NS):
                if s == 10:
                    norm_squares()
                if READER[name_of(s)] == "act":
                    read_tiles(s)
                if s == 11:
                    norm_root()
                if s == 13:
                    norm_silu()
                if s + 2 < NS:
                    high(s + 2)
                if name_of(s) == "conv":
                    for c in range(4 * (s - 20), 4 * (s - 19)):
                        merged_high(c)

        @block.vector
        def _(dve):
            n_step = [0]

            def step(ins):
                n_step[0] += 1
                ins.then_inc(dve_step, 1)
                dve.wait_ge(dve_step, n_step[0])

            dve.wait_ge(vt_ready, 2)
            dve.tensor_copy(vec_all[:, 0:NV], bank[1][:, 0:NV])
            dve.tensor_copy(conv_w[:, 0:4 * TAPS], bank[2][:, 0:4 * TAPS])
            dve.tensor_copy(rpb_t[0:NDC, 0:HEADS * NDR], bank[3][0:NDC, 0:HEADS * NDR]).then_inc(vt_used, 1)
            dve.wait_ge(ssq_done, 6)
            dve.tensor_scalar(ssq[:, 0:6], ssq[:, 0:6], 1.0 / D, NORM_EPS, ALU.mult, ALU.add).then_inc(var_ready, 1)
            dve.wait_ge(std_ready, 1)
            step(dve.reciprocal(ssq[:, 0:6], ssq[:, 0:6]))
            for t in range(6):
                src = x_rows[:, t, :] if t < 4 else c_rows[:, t - 4, :]
                dve.tensor_scalar(src, src, ssq[:, t:t + 1], None, ALU.mult).then_inc(scaled, 1)
            dve.wait_ge(vt_used, 1)
            dve.wait_ge(mod_done, 16)
            mod_acc = bank[7][:, 0:96].rearrange("p (j s) -> p j s", s=2)
            dve.tensor_tensor(mod_col[:, 0:16], mod_acc[:, 0:16, 0], vec_all[:, V_BMOD:V_BMOD + 16], ALU.add)
            step(dve.tensor_tensor(mod_ctx[:], mod_acc[:, 0:16, 1], vec_all[:, V_BMOD:V_BMOD + 16], ALU.add))
            for i, src in enumerate((mod_col, mod_ctx)):
                ins = dve.scalar_tensor_tensor(out=s1[:, 8 * i:8 * i + 8], in0=src[:, 8:16], scalar=1.0,
                                               in1=vec_all[:, V_NORM:V_NORM + KC], op0=ALU.add, op1=ALU.mult)
            step(ins)

            def low(s):
                pos = place["split", s]
                dve.wait_ge(hi_done, s + 1)
                dve.tensor_tensor(w_lo[s % 2][:], raw[pos % RING][:], w_hi[s % 2][:].bitcast(F32), ALU.subtract)\
                   .then_inc(lo_done, 1)

            def h_low(c):
                dve.wait_ge(hhi_done, c + 1)
                if c < KC:
                    ins = dve.tensor_tensor(h_lo[:, c, :], tmp[c % 2], h_hi[:, c, :].bitcast(F32), ALU.subtract)
                else:
                    ins = dve.tensor_tensor(g_lo[:, c - KC, 0:CTX], tmp[c % 2][:, 0:CTX],
                                            g_hi[:, c - KC, 0:CTX].bitcast(F32), ALU.subtract)
                ins.then_inc(hlo_done, 1)

            for c in range(2 * KC):
                dve.wait_ge(ht_ready, c + 1)
                b = bank[(4, 5, 6)[c % 3]]
                if c >= 2:
                    dve.wait_ge(hlo_done, c - 1)
                if c < KC:
                    ins = dve.tensor_scalar(tmp[c % 2], b[:], s1[:, c:c + 1], mod_col[:, c:c + 1], ALU.mult, ALU.add)
                else:
                    ins = dve.tensor_scalar(tmp[c % 2][:, 0:CTX], b[:, 0:CTX], s1[:, c:c + 1],
                                            mod_ctx[:, c - KC:c - KC + 1], ALU.mult, ALU.add)
                ins.then_inc(tmp_ready, 1)
                if c >= 1:
                    h_low(c - 1)
                if c == KC:
                    low(0)
                    low(1)
            h_low(2 * KC - 1)

            def read_tiles(s):
                name = name_of(s)
                for t in range(first_tile[s], first_tile[s + 1]):
                    k = t - first_tile[s]
                    src = bank[t % 4]
                    dve.wait_ge(acc_ready, t + 1)
                    if name == "glu_a":
                        j = (s - 1) // 2
                        dve.wait_ge(read_act, 2 * j + k + 1)
                        if t == first_tile[1]:
                            dve.wait_ge(pad_ready, 1)
                        dve.tensor_tensor(u_pad[:, 2 * j + k, HALF:HALF + SEQ], src[:], sig[k], ALU.mult)\
                           .then_inc(read_dve, 1)
                    elif name == "att":
                        c = 4 * (s - 14) + k
                        dve.wait_ge(read_act, reads_upto("act", first_tile[14]))
                        dve.tensor_tensor(m[:, c, :], m[:, c, :], src[:], ALU.mult).then_inc(read_dve, 1)
                    elif name == "conv":
                        c = 4 * (s - 20) + k
                        dve.wait_ge(read_act, reads_upto("act", first_tile[20]))
                        dve.tensor_tensor(gate_c[:, c, :], gate_c[:, c, :], src[:], ALU.mult).then_inc(read_dve, 1)
                        dve.wait_ge(read_dve, reads_upto("dve", t))
                        dve.tensor_tensor(m[:, c, :], m[:, c, :], gate_c[:, c, :], ALU.add).then_inc(m_done, 1)
                    else:
                        c = 2 * (s - 22) + k
                        dve.wait_ge(xt_used, c + 1)
                        dve.scalar_tensor_tensor(out=x_mid[:, c, :], in0=src[:], scalar=mod_col[:, 16 + c:17 + c],
                                                 in1=m[:, c, :], op0=ALU.mult, op1=ALU.add)\
                           .then_inc(read_dve, 1)

            taps = [(tap, c) for tap in range(TAPS) for c in range(4)]

            def convolve(upto, start=[0]):
                while start[0] < upto:
                    n = start[0]
                    tap, c = taps[n]
                    if n == 0:
                        dve.wait_ge(read_dve, 4)
                        dve.wait_ge(pad_ready, 1)
                    if n >= 4:
                        dve.wait_ge(tap_done, n - 3)
                    wcol = conv_w[:, 4 * tap + c:4 * tap + c + 1]
                    if tap == 0:
                        ins = dve.tensor_scalar(y_conv[:, c, :], u_pad[:, c, 0:SEQ], wcol,
                                                vec_all[:, V_CB + c:V_CB + c + 1], ALU.mult, ALU.add)
                    else:
                        ins = dve.scalar_tensor_tensor(out=y_conv[:, c, :], in0=u_pad[:, c, tap:tap + SEQ],
                                                       scalar=wcol, in1=y_conv[:, c, :], op0=ALU.mult, op1=ALU.add)
                    ins.then_inc(tap_done, 1)
                    start[0] = n + 1

            for s in range(10):
                if READER[name_of(s)] == "dve":
                    read_tiles(s)
                low(s + 2)
                if s >= 3:
                    convolve(len(taps) * (s - 2) // 7)
            dve.wait_ge(tap_done, len(taps))

            def normed(n):
                h, i = IT[n]
                dve.wait_ge(p_ready, n + 1)
                step(dve.tensor_tensor(r_loc[:, n:n + 1], r_loc[:, n:n + 1], r_ctx[:, n:n + 1], ALU.add))
                step(dve.reciprocal(r_loc[:, n:n + 1], r_loc[:, n:n + 1]))
                dve.wait_ge(o_ready, n + 1)
                if i == 0 and h % 2 == 0 and h >= 4:
                    dve.wait_ge(at_ready, h // 2 - 1)
                dve.tensor_scalar(att[h // 2 % 2][:, i, 64 * (h % 2):64 * (h % 2) + 64],
                                  bank[6][:, 0:HD], r_loc[:, n:n + 1], None, ALU.mult)\
                   .then_inc(o_used, 1)

            def att_low(pair):
                dve.wait_ge(athi_done, pair + 1)
                dve.tensor_tensor(g_lo[:, pair, :], bank[6][:], g_hi[:, pair, :].bitcast(F32),
                                  ALU.subtract).then_inc(atlo_done, 1)

            dve.wait_ge(masked, 2)
            for n, (h, i) in enumerate(IT):
                dve.wait_ge(s_ready, n + 1)
                if n >= 2:
                    dve.wait_ge(pt_ready, n - 1)
                a = 6 - 2 * i
                dve.tensor_tensor_reduce(s_t[n % 2][:, 0:512], bank[n % 2][:],
                                         bias[:, h, a:a + 8, :].rearrange("p m c -> p (m c)"), 1.0, -3.0e38,
                                         ALU.add, ALU.max, m_loc[:, n:n + 1]).then_inc(s_used, 1)
                dve.wait_ge(sc_ready, n + 1)
                dve.reduce_max(m_ctx[:, n:n + 1], bank[2][:, 0:CTX], axis=AX.X).then_inc(mc_ready, 1)
                dve.wait_ge(s_used, n + 1)
                dve.wait_ge(mc_ready, n + 1)
                dve.tensor_scalar(m_neg[:, n:n + 1], m_loc[:, n:n + 1], m_ctx[:, n:n + 1], -1.0, ALU.max, ALU.mult)\
                   .then_inc(m_ready, 1)
                if n >= 2:
                    normed(n - 2)
                if n >= 12 and n % 8 == 4:
                    att_low(n // 8 - 1)
            normed(NIT - 2)
            normed(NIT - 1)
            att_low(3)
            dve.wait_ge(mod_done, 48)
            step(dve.tensor_tensor(mod_col[:, 16:48], mod_acc[:, 16:48, 0], vec_all[:, V_BMOD + 16:V_BMOD + 48],
                                   ALU.add))

            def norm_mean():
                dve.wait_ge(mean_ready, 1)
                step(dve.tensor_scalar(mean_t, bank[4][:], 1.0 / 512, None, ALU.mult))
                for c in range(4):
                    dve.tensor_tensor(y_conv[:, c, :], y_conv[:, c, :], mean_t, ALU.subtract).then_inc(cent_ready, 1)

            def norm_var():
                dve.wait_ge(cssq_ready, 1)
                dve.tensor_scalar(rstd, bank[5][:], 1.0 / 512, NORM_EPS, ALU.mult, ALU.add).then_inc(cvar_ready, 1)
                dve.wait_ge(cstd_ready, 1)
                step(dve.reciprocal(rstd, rstd))
                for c in range(4):
                    dve.tensor_tensor(y_conv[:, c, :], y_conv[:, c, :], rstd, ALU.mult).then_inc(cn_ready, 1)

            def conv_low():
                for c in range(4):
                    dve.wait_ge(cvhi_done, c + 1)
                    dve.tensor_tensor(g_lo[:, 4 + c, :], y_conv[:, c, :], g_hi[:, 4 + c, :].bitcast(F32),
                                      ALU.subtract).then_inc(cvlo_done, 1)

            def merged_low(c):
                dve.wait_ge(mhi_done, c + 1)
                dve.tensor_tensor(h_lo[:, c, :], m[:, c, :], h_hi[:, c, :].bitcast(F32), ALU.subtract)\
                   .then_inc(mlo_done, 1)

            for s in range(10, NS):
                if s == 10:
                    norm_mean()
                if READER[name_of(s)] == "dve":
                    read_tiles(s)
                if s == 11:
                    norm_var()
                if s + 2 < NS:
                    low(s + 2)
                if s == 14:
                    conv_low()
                if name_of(s) == "conv":
                    for c in range(4 * (s - 20), 4 * (s - 19)):
                        merged_low(c)
                if s == 21:
                    dve.wait_ge(mlo_done, KC)
                    for c in range(KC):
                        dve.wait_ge(xt_ready, c + 1)
                        dve.tensor_copy(x_mid[:, c, :], bank[4 + c % 4][:]).then_inc(xt_used, 1)

        @block.tensor
        def _(pe):
            pe.wait_ge(ident_ready, 1)
            pe.wait_ge(cond_landed, 32)
            pe.transpose(bank[0][:, 0:16], cond_rows[0:16, :], ident[0:16, 0:16]).then_inc(vt_ready, 1)
            pe.wait_ge(vec_landed, 16 * 14)
            pe.transpose(bank[1][:, 0:NV], vec_rows[0:NV, :], ident[0:NV, 0:NV])
            pe.transpose(bank[2][:, 0:4 * TAPS], conv_rows[0:4 * TAPS, :], ident[0:4 * TAPS, 0:4 * TAPS])
            pe.transpose(bank[3][0:NDC, 0:HEADS * NDR], rpb_rows[0:HEADS * NDR, :],
                         ident[0:HEADS * NDR, 0:HEADS * NDR]).then_inc(vt_ready, 1)

            mod_acc = bank[7][:, 0:96].rearrange("p (j s) -> p j s", s=2)

            def modulation(j):
                pos = place["mod", j // 2]
                if j % 2 == 0:
                    wait_landed(pe, pos)
                a = 128 * (j % 2)
                for k in range(KC):
                    ins = pe.matmul(mod_acc[:, j, :], as_k8(raw[pos % RING])[:, k, a:a + 128], c_silu[:, k, :],
                                    start=(k == 0), stop=(k == KC - 1))
                ins.then_inc(mod_done, 1)

            pe.wait_ge(silu_ready, 1)
            for j in range(16):
                modulation(j)

            def turned(c):
                if c >= 3:
                    pe.wait_ge(tmp_ready, c - 2)
                b = bank[(4, 5, 6)[c % 3]]
                nt, rows = (4, x_rows) if c < KC else (2, c_rows)
                cc = c % KC
                for t in range(nt):
                    ins = pe.transpose(b[:, 128 * t:128 * t + 128], rows[:, t, 128 * cc:128 * cc + 128], ident[:])
                ins.then_inc(ht_ready, 1)

            pe.wait_ge(scaled, 6)
            for c in range(2 * KC):
                turned(c)

            def product(out, a_hi, a_lo, b_hi, b_lo, first, last):
                pe.matmul(out, a_hi, b_lo, start=first, stop=False)
                pe.matmul(out, a_lo, b_hi, start=False, stop=False)
                return pe.matmul(out, a_hi, b_hi, start=False, stop=last)

            def features(out, s, k, b_hi, b_lo, n):
                hi, lo = as_k8(w_hi[s % 2]), as_k8(w_lo[s % 2])
                for c in range(KC):
                    ins = product(out, hi[:, c, 128 * k:128 * k + 128], lo[:, c, 128 * k:128 * k + 128],
                                  b_hi[:, c, 0:n], b_lo[:, c, 0:n], c == 0, c == KC - 1)
                return ins

            def positions(out, s, b_hi, b_lo, t):
                hi, lo = as_k8(w_hi[s % 2]), as_k8(w_lo[s % 2])
                for c in range(KC):
                    ins = product(out, b_hi[:, c, 128 * t:128 * t + 128], b_lo[:, c, 128 * t:128 * t + 128],
                                  hi[:, c, :], lo[:, c, :], c == 0, c == KC - 1)
                return ins

            def half_features(out, s, k, at):
                hi, lo = as_k4(w_hi[s % 2]), as_k4(w_lo[s % 2])
                for c in range(4):
                    ins = product(out, hi[:, c, 128 * k:128 * k + 128], lo[:, c, 128 * k:128 * k + 128],
                                  g_hi[:, at + c, :], g_lo[:, at + c, :], c == 0, c == 3)
                return ins

            def unit(s):
                name = name_of(s)
                pe.wait_ge(lo_done, s + 1)
                if s == 0:
                    pe.wait_ge(hlo_done, KC)
                if s == 4:
                    pe.wait_ge(hlo_done, 2 * KC)
                if s == 14:
                    pe.wait_ge(atlo_done, 4)
                if s == 20:
                    pe.wait_ge(cvlo_done, 4)
                if s == 22:
                    pe.wait_ge(mlo_done, KC)
                for t in range(first_tile[s], first_tile[s + 1]):
                    k = t - first_tile[s]
                    if t >= 4:
                        engine = READER[name_of(TILES[t - 4][0])]
                        pe.wait_ge(read_act if engine == "act" else read_dve, reads_upto(engine, t - 4))
                    dst = bank[t % 4]
                    if name == "k" and k == 2:
                        features(dst[:, 0:256], s, 0, g_hi, g_lo, CTX)
                        ins = features(dst[:, 256:512], s, 1, g_hi, g_lo, CTX)
                    elif name == "v":
                        b_hi, b_lo, t0 = (h_hi, h_lo, 2 * k) if k < 2 else (g_hi, g_lo, 0)
                        positions(dst[:, 0:256], s, b_hi, b_lo, t0)
                        ins = positions(dst[:, 256:512], s, b_hi, b_lo, t0 + 1)
                    elif name in ("att", "conv"):
                        ins = half_features(dst[:], s, k, 0 if name == "att" else 4)
                    else:
                        ins = features(dst[:], s, k, h_hi, h_lo, SEQ)
                    ins.then_inc(acc_ready, 1)

            def table_part(b):
                if b == 0:
                    pe.wait_ge(onehot_ready, 1)
                    pe.wait_ge(tmp_ready, 2 * KC)
                if b >= 3:
                    pe.wait_ge(tb_used, b - 2)
                for q in range(4):
                    ck = 4 * b + q
                    ins = pe.matmul(bank[(4, 5, 6)[b % 3]][:, 120 * q:120 * q + 120],
                                    onehot[0:NDC, GRID - 1 - ck:GRID - 1 - ck + 128], rpb_t[0:NDC, 0:120],
                                    start=True, stop=True)
                ins.then_inc(tb_ready, 1)

            for s in range(10):
                if 4 <= s < 8:
                    for b in range(4 * (s - 4), 4 * (s - 3)):
                        table_part(b)
                unit(s)
            pe.wait_ge(read_act, reads_upto("act", first_tile[10] - 1))

            def scores(n):
                h, i = IT[n]
                if n >= 2:
                    pe.wait_ge(s_used, n - 1)
                a = 64 * (h % 2)
                pe.matmul(bank[n % 2][:], q_t[a:a + 64, h // 2, 128 * i:128 * i + 128], k_t[a:a + 64, h // 2, :],
                          start=True, stop=True).then_inc(s_ready, 1)

            def context_scores(n):
                h, i = IT[n]
                if n:
                    pe.wait_ge(p_ready, n)
                a = 64 * (h % 2)
                pe.matmul(bank[2][:, 0:CTX], q_t[a:a + 64, h // 2, 128 * i:128 * i + 128],
                          kc_t[a:a + 64, h // 2, :], start=True, stop=True).then_inc(sc_ready, 1)

            def turn(n):
                pe.wait_ge(p_ready, n + 1)
                for j in range(6):
                    if j == 4 and n >= 1:
                        pe.wait_ge(pt_used, n)
                    dst = bank[3 + n % 2][:, 128 * j:128 * j + 128] if j < 4 else \
                        bank[5][:, 128 * (j - 4):128 * (j - 3)]
                    ins = pe.transpose(dst, s_t[n % 2][:, 128 * j:128 * j + 128], ident[:])
                ins.then_inc(pt_ready, 1)

            def values(n):
                h, i = IT[n]
                pe.wait_ge(pt_used, n + 1)
                if n >= 1:
                    pe.wait_ge(o_used, n)
                if n >= 11 and n % 8 == 3:
                    pe.wait_ge(atlo_done, n // 8)
                for j in range(6):
                    v = v_t[:, j, HD * h:HD * h + HD] if j < 4 else vc_t[:, j - 4, HD * h:HD * h + HD]
                    ins = pe.matmul(bank[6][:, 0:HD], pt_t[n % 2][:, 128 * j:128 * j + 128],
                                    v, start=(j == 0), stop=(j == 5))
                ins.then_inc(o_ready, 1)

            def turn_att(pair):
                pe.wait_ge(o_used, min(8 * pair + 11, NIT))
                for t in range(TC):
                    ins = pe.transpose(bank[6][:, 128 * t:128 * t + 128], att[pair % 2][:, t, :], ident[:])
                ins.then_inc(at_ready, 1)

            scores(0)
            context_scores(0)
            for n in range(NIT):
                if n + 1 < NIT:
                    scores(n + 1)
                modulation(16 + n)
                if n + 1 < NIT:
                    context_scores(n + 1)
                turn(n)
                if n >= 1:
                    values(n - 1)
                if n >= 11 and n % 8 == 3:
                    turn_att(n // 8 - 1)
            values(NIT - 1)
            turn_att(3)
            for c in range(4):
                ins = pe.matmul(bank[4][:], ones[:], y_conv[:, c, :], start=(c == 0), stop=(c == 3))
            ins.then_inc(mean_ready, 1)
            for s in range(10, NS):
                if s == 22:
                    pe.wait_ge(again_landed, 16)
                    for c in range(KC):
                        if c >= 4:
                            pe.wait_ge(xt_used, c - 3)
                        for t in range(TC):
                            ins = pe.transpose(bank[4 + c % 4][:, 128 * t:128 * t + 128],
                                               x_rows[:, t, 128 * c:128 * c + 128], ident[:])
                        ins.then_inc(xt_ready, 1)
                unit(s)
                if s == 10:
                    for c in range(4):
                        pe.wait_ge(sq_ready, c + 1)
                        ins = pe.matmul(bank[5][:], ones[:], sq[:, c, :], start=(c == 0), stop=(c == 3))
                    ins.then_inc(cssq_ready, 1)
    return used


def moe_stage(nc, cst, x_mid, mod_col, vec, w, dram):
    used = []
    with ExitStack() as ctx:
        def sb(name, shape, dt=F32):
            return ctx.enter_context(nc.sbuf_tensor("moe_" + name, shape, dt))

        def sem(name):
            used.append(ctx.enter_context(nc.semaphore("moe_" + name)))
            return used[-1]

        bank = [ctx.enter_context(nc.psum_tensor(f"moe_bank{i}", [P, 512], F32)) for i in range(8)]
        ident, ones = cst["ident"], cst["ones"]
        gates = cst["gates"]

        raw = [sb(f"expert_raw{i}", [P, 4, 512]) for i in range(RAW)]
        w_hi = [sb(f"expert_hi{i}", [P, 4, 512], F32R) for i in range(SPLIT)]
        w_lo = [sb(f"expert_lo{i}", [P, 4, 512], F32R) for i in range(SPLIT)]
        pool0 = sb("moe_tiles", [P, 8192])
        x_rows = [pool0[:, 1024 * i:1024 * (i + 1)] for i in range(2)]
        silu_g = [pool0[:, 2048 + 512 * i:2560 + 512 * i] for i in range(2)]
        act = [pool0[:, 3072 + 512 * i:3584 + 512 * i] for i in range(2)]
        y_rows = [pool0[:, 4096 + 1024 * i:5120 + 1024 * i] for i in range(2)]
        h2 = pool0[:, 0:4096].rearrange("p (c t) -> p c t", c=KC)
        sq = pool0[:, 4096:8192].rearrange("p (c t) -> p c t", c=KC)
        h2_rows = pool0[:, 4096:8192].rearrange("p (t d) -> p t d", t=TC)
        x_hi = [sb(f"x_hi{i}", [P, KC, 128], F32R) for i in range(2)]
        x_lo = [sb(f"x_lo{i}", [P, KC, 128], F32R) for i in range(2)]
        a_hi = [sb(f"a_hi{i}", [P, 4, 128], F32R) for i in range(2)]
        a_lo = [sb(f"a_lo{i}", [P, 4, 128], F32R) for i in range(2)]

        rstd = sb("moe_rstd", [P, SEQ])
        s2 = sb("s2", [P, KC])
        w_router = sb("w_router", [P, KC, 36])
        b_router = sb("b_router", [P, 36])
        logits = sb("logits", [P, TC, 36])
        group8 = sb("group8", [P, TC, 8])
        gmax = sb("gmax", [P, TC, 8])
        gidx = sb("gidx", [P, TC, 8], U32)
        gidx_f = sb("gidx_f", [P, TC])
        gexp = sb("gexp", [P, TC, 4])
        p_group = sb("p_group", [P, TC])
        g_one = sb("g_one", [P, TC, 4])
        e_sel = sb("e_sel", [P, TC, 8])
        e_part = sb("e_part", [P, TC, 8])
        emax = sb("emax", [P, TC, 8])
        eidx = sb("eidx", [P, TC, 8], U32)
        eidx_f = sb("eidx_f", [P, TC, 2])
        e2 = sb("e2", [P, TC])
        den = sb("den", [P, TC])
        flat_e = sb("flat_e", [P, TC, 2])
        chosen = sb("chosen", [P, 8, 32])
        totals = sb("totals", [P, 8, 32])
        before = sb("before", [P, 8, 32])
        prod = sb("prod", [P, 8, 32])
        rank = sb("rank", [P, 8])
        counts = sb("counts", [P, 32])
        n_blk = sb("n_blk", [P, 32])
        end_blk = sb("end_blk", [P, 32])
        first_blk = sb("first_blk", [P, 32])
        fl = sb("fl", [P, 8])
        slot = sb("slot", [P, 8])
        blk = sb("blk", [P, 8])
        ident1 = sb("ident1", [P, 8])
        slot_one = sb("slot_one", [P, 8, 128])
        blk_one = sb("blk_one", [P, 8, NBX])
        list_f = sb("list_f", [P, NBX])
        empty = sb("empty", [P, NBX])
        row_f = sb("row_f", [P, NBX])
        tok_f = sb("tok_f", [P, NBX])
        row_i = sb("row_i", [P, NBX], I32)
        tok_i = sb("tok_i", [P, NBX], I32)
        le = sb("le", [1, NBX, 32])
        exp_f = sb("exp_f", [1, NBX])
        exp_i = sb("exp_i", [1, NBX], I32)
        pairs_f = sb("pairs_f", [1, 1])
        pairs_i = sb("pairs_i", [1, 1], I32)
        iota_row = sb("iota_row", [P, 128])
        iota_p = sb("iota_p", [P, 8])
        tri = sb("tri", [P, 128])
        tok_col = [sb(f"tok_col{i}", [P, 1], I32) for i in range(2)]
        row_col = [sb(f"row_col{i}", [P, 1], I32) for i in range(2)]

        router_landed = sem("router_landed")
        tables_ready = sem("tables_ready")
        index_ready = sem("index_ready")
        pool_step = sem("pool_step")
        dve_step = sem("moe_dve_step")
        sq_ready = sem("sq_ready")
        ssq_ready = sem("ssq_ready")
        var_ready = sem("var_ready")
        std_ready = sem("std_ready")
        h2_ready = sem("h2_ready")
        h2t_ready = sem("h2t_ready")
        h2t_evac_v = sem("h2t_evac_v")
        h2t_evac_s = sem("h2t_evac_s")
        h2_stored = sem("h2_stored")
        logits_ready = sem("logits_ready")
        gd_ready = sem("gd_ready")
        gexp_ready = sem("gexp_ready")
        ed_ready = sem("ed_ready")
        eexp_ready = sem("eexp_ready")
        chosen_ready = sem("chosen_ready")
        ranks_ready = sem("ranks_ready")
        ones_ready = sem("ones_ready")
        list_ready = sem("list_ready")
        lists_done = sem("lists_done")
        raw_landed = [sem(f"expert_landed{i}") for i in range(RAW)]
        hi_done = sem("expert_hi_done")
        lo_done = sem("expert_lo_done")
        unit_used = sem("expert_unit_used")
        gathered = [sem(f"gathered{i}") for i in range(2)]
        xt_ready = sem("xt_ready")
        xhi_done = sem("xhi_done")
        xlo_done = sem("xlo_done")
        silu_done = sem("silu_done")
        act_done = sem("act_done")
        at_ready = sem("at_ready")
        ahi_done = sem("ahi_done")
        alo_done = sem("alo_done")
        y_s = sem("y_s")
        y_v = sem("y_v")
        scattered = [sem(f"scattered{i}") for i in range(2)]

        wg = w["w_exp_gate"][0].rearrange("e (h k p) f -> e h p k f", p=P, k=4)
        wu = w["w_exp_up"][0].rearrange("e (h k p) f -> e h p k f", p=P, k=4)
        wd = w["w_exp_down"][0].rearrange("e (k p) (h f) -> e h p k f", p=P, f=512)

        def unit(i, s, j):
            return 4 + 12 * i + 6 * s + j

        def unit_slot(s, j):
            return (4 + 6 * s + j) % RAW, (4 + 6 * s + j) % SPLIT

        def unit_landed(i, s, j):
            return 16 * (12 // RAW * i + (4 + 6 * s + j) // RAW + 1)

        block = ctx.enter_context(nc.Block())

        @block.sync
        def _(sp):
            with nc.allow_non_contiguous_dma(reason="router columns"):
                sp.dma_start(w_router[:, :, 0:4],
                             w["w_router_group"][0].rearrange("(k p) g -> p k g", p=P)).then_inc(router_landed, 16)
                sp.dma_start(w_router[:, :, 4:36],
                             w["w_router_expert"][0].rearrange("(k p) g -> p k g", p=P)).then_inc(router_landed, 16)
                sp.dma_start(b_router[:, 0:4], w["b_router_group"].to_broadcast([P, 4])).then_inc(router_landed, 16)
                sp.dma_start(b_router[:, 4:36], w["b_router_expert"].to_broadcast([P, 32])).then_inc(router_landed, 16)
            for t in range(TC):
                sp.wait_ge(h2t_evac_v, t + 1)
                sp.wait_ge(h2t_evac_s, t + 1)
                sp.dma_start(dram["h2"][t * 128:(t + 1) * 128, :], h2_rows[:, t, :]).then_inc(h2_stored, 16)
            sp.wait_ge(lists_done, 1)
            pairs = sp.value_load(pairs_i[0:1, 0:1], min_val=1, max_val=NB_MAX // 2)
            first = sp.value_load(exp_i[0:1, 0:1], min_val=0, max_val=31)
            for n, src in enumerate((wg, wg, wu, wu)):
                sp.dma_start(raw[n][:], src[bass.ds(first, 1), n % 2]).then_inc(raw_landed[n], 16)
            with sp.Fori(0, pairs) as i:
                for s in range(2):
                    here = sp.value_load(exp_i[0:1, bass.ds(2 * i + s, 1)], min_val=0, max_val=31)
                    after = sp.value_load(exp_i[0:1, bass.ds(2 * i + s + 1, 1)], min_val=0, max_val=31)
                    for j, (src, e) in enumerate(((wg, after), (wd, here), (wu, after))):
                        for h in range(2):
                            r, _ = unit_slot(s, 2 * j + h)
                            sp.wait_ge(lo_done, unit(i, s, 2 * j + h) + 1)
                            sp.dma_start(raw[r][:], src[bass.ds(e, 1), h]).then_inc(raw_landed[r], 16)

        @block.gpsimd
        def _(pool):
            n = [0]

            def step(ins):
                n[0] += 1
                ins.then_inc(pool_step, 1)
                pool.wait_ge(pool_step, n[0])

            step(pool.iota(iota_row[:], pattern=[[1, 128]], base=0, channel_multiplier=0,
                           allow_small_or_imprecise_dtypes=True))
            step(pool.iota(iota_p[:].rearrange("p (t k) -> p t k", k=2), pattern=[[128, TC], [SEQ, 2]], base=1,
                           channel_multiplier=1, allow_small_or_imprecise_dtypes=True))
            step(pool.memset(tri[:], 1.0))
            step(pool.affine_select(out=tri[:], in_=tri[:], compare_op=ALU.is_gt, fill=0.0, base=0,
                                    pattern=[[1, 128]], channel_multiplier=-1))
            pool.memset(group8[:], -3.0e38).then_inc(tables_ready, 1)
            pool.wait_ge(lists_done, 1)
            pool.wait_ge(h2_stored, 16 * TC)
            for s in range(2):
                step(pool.memset(x_rows[s], 0.0))
            pairs = pool.value_load(pairs_i[0:1, 0:1], min_val=1, max_val=NB_MAX // 2)

            last_token, last_row = pool.to_reg(SEQ - 1), pool.to_reg(2 * SEQ - 1)

            def gather_rows(s):
                pool.indirect_dma_start(out=x_rows[s], out_offset=None, in_=dram["h2"][:, :],
                                        in_offset=bass.IndirectOffsetOnAxis(ap=tok_col[s][:, 0:1], axis=0),
                                        bounds_check=last_token, oob_is_err=False).then_inc(gathered[s], 16)

            for s in range(2):
                pool.dma_start(dram["mark"][s], iota_row[0:1, :]).then_inc(scattered[s], 16)
            for first in range(3):
                if first == 2:
                    pool.wait_ge(xt_ready, 1)
                step(pool.tensor_copy(tok_col[first % 2][:], tok_i[:, first:first + 1]))
                gather_rows(first % 2)
            with pool.Fori(0, pairs) as i:
                for s in range(2):
                    pool.wait_ge(xt_ready, 2 * i + s + 2)
                    pool.tensor_copy(tok_col[1 - s][:], tok_i[:, bass.ds(2 * i + s + 3, 1)]).then_inc(pool_step, 1)
                    pool.wait_ge(pool_step, n[0] + 4 * i + 2 * s + 1)
                    pool.sem_inc(index_ready, 1)
                    gather_rows(1 - s)
                    pool.wait_ge(y_s, 2 * i + s + 2)
                    pool.wait_ge(y_v, 2 * i + s + 2)
                    pool.tensor_copy(row_col[s][:], row_i[:, bass.ds(2 * i + s, 1)]).then_inc(pool_step, 1)
                    pool.wait_ge(pool_step, n[0] + 4 * i + 2 * s + 2)
                    pool.sem_inc(index_ready, 1)
                    pool.indirect_dma_start(out=dram["y"][:, :],
                                            out_offset=bass.IndirectOffsetOnAxis(ap=row_col[s][:, 0:1], axis=0),
                                            in_=y_rows[s], in_offset=None,
                                            bounds_check=last_row, oob_is_err=False).then_inc(scattered[s], 16)
            for s in range(2):
                pool.wait_ge(scattered[s], 16 * pairs + 16)
            pool.wait_ge(gathered[0], 16 * pairs + 32)
            pool.wait_ge(gathered[1], 16 * pairs + 16)

        @block.scalar
        def _(act_e):
            for c in range(KC):
                act_e.activation(sq[:, c, :], x_mid[:, c, :], ACT.Square).then_inc(sq_ready, 1)
            act_e.wait_ge(var_ready, 1)
            act_e.activation(rstd[:], rstd[:], ACT.Sqrt).then_inc(std_ready, 1)
            for t in range(TC):
                act_e.wait_ge(h2t_ready, 2 * t + 2)
                act_e.activation(h2_rows[:, t, 512:1024], bank[(2 * t + 1) % 8][:], ACT.Copy).then_inc(h2t_evac_s, 1)
            act_e.wait_ge(gd_ready, 1)
            act_e.activation(gexp[:], gexp[:], ACT.Exp).then_inc(gexp_ready, 1)
            act_e.wait_ge(ed_ready, 1)
            act_e.activation(e2[:], e2[:], ACT.Exp).then_inc(eexp_ready, 1)
            act_e.wait_ge(lists_done, 1)
            act_e.sem_inc(y_s, 1)
            pairs = act_e.value_load(pairs_i[0:1, 0:1], min_val=1, max_val=NB_MAX // 2)

            def split_hi(i, s, j):
                r, q = unit_slot(s, j)
                act_e.wait_ge(raw_landed[r], unit_landed(i, s, j))
                act_e.wait_ge(unit_used, unit(i, s, j) + 1)
                act_e.activation(w_hi[q][:], raw[r][:], ACT.Copy).then_inc(hi_done, 1)

            def x_high(s, b):
                act_e.wait_ge(xt_ready, b + 1)
                act_e.activation(x_hi[s][:, 0:4, :], bank[0][:], ACT.Copy)
                act_e.activation(x_hi[s][:, 4:8, :], bank[1][:], ACT.Copy).then_inc(xhi_done, 1)

            def first_hi(n):
                act_e.wait_ge(raw_landed[n], 16)
                act_e.wait_ge(unit_used, n + 1)
                act_e.activation(w_hi[n][:], raw[n][:], ACT.Copy).then_inc(hi_done, 1)

            x_high(0, 0)
            first_hi(0)
            first_hi(1)
            x_high(1, 1)
            first_hi(2)
            first_hi(3)
            with act_e.Fori(0, pairs) as i:
                for s in range(2):
                    b = 2 * i + s
                    act_e.wait_ge(unit_used, SPLIT + unit(i, s, 0) - 2)
                    act_e.wait_ge(act_done, b + 1)
                    act_e.activation(silu_g[s], bank[2 + s][:], ACT.Silu).then_inc(silu_done, 1)
                    split_hi(i, s, 0)
                    split_hi(i, s, 1)
                    split_hi(i, s, 2)
                    act_e.wait_ge(at_ready, b + 1)
                    act_e.activation(a_hi[s][:], bank[5][:], ACT.Copy).then_inc(ahi_done, 1)
                    x_high(s, b + 2)
                    split_hi(i, s, 3)
                    split_hi(i, s, 4)
                    split_hi(i, s, 5)
                    act_e.wait_ge(unit_used, SPLIT + unit(i, s, 2) + 1)
                    act_e.wait_ge(scattered[s], 16 * i + 16)
                    act_e.activation(y_rows[s][:, 0:512], bank[6][:], ACT.Copy).then_inc(y_s, 1)

        @block.vector
        def _(dve):
            n = [0]

            def step(ins):
                n[0] += 1
                ins.then_inc(dve_step, 1)
                dve.wait_ge(dve_step, n[0])

            dve.wait_ge(ssq_ready, 1)
            dve.tensor_scalar(rstd[:], bank[0][:], 1.0 / D, NORM_EPS, ALU.mult, ALU.add).then_inc(var_ready, 1)
            step(dve.scalar_tensor_tensor(out=s2[:], in0=mod_col[:, 32:40], scalar=1.0,
                                          in1=vec["norm_ffn"], op0=ALU.add, op1=ALU.mult))
            dve.wait_ge(std_ready, 1)
            step(dve.reciprocal(rstd[:], rstd[:]))
            for c in range(KC):
                step(dve.tensor_tensor(h2[:, c, :], x_mid[:, c, :], rstd[:], ALU.mult))
                dve.tensor_scalar(h2[:, c, :], h2[:, c, :], s2[:, c:c + 1], mod_col[:, 24 + c:25 + c],
                                  ALU.mult, ALU.add).then_inc(h2_ready, 1)
            for t in range(TC):
                dve.wait_ge(h2t_ready, 2 * t + 1)
                dve.tensor_copy(h2_rows[:, t, 0:512], bank[(2 * t) % 8][:]).then_inc(h2t_evac_v, 1)
            dve.wait_ge(logits_ready, 1)
            dve.wait_ge(router_landed, 64)
            dve.wait_ge(tables_ready, 1)
            step(dve.tensor_tensor(logits[:], bank[0][:, 0:TC * 36].rearrange("p (t e) -> p t e", t=TC),
                                   b_router[:].unsqueeze(1).to_broadcast([P, TC, 36]), ALU.add))
            step(dve.tensor_copy(group8[:, :, 0:4], logits[:, :, 0:4]))
            for t in range(TC):
                step(dve.max(gmax[:, t, :], group8[:, t, :]))
                step(dve.max_index(gidx[:, t, :], gmax[:, t, :], group8[:, t, :]))
            dve.tensor_tensor(gexp[:], logits[:, :, 0:4], gmax[:, :, 0:1].to_broadcast([P, TC, 4]),
                              ALU.subtract).then_inc(gd_ready, 1)
            step(dve.tensor_copy(gidx_f[:], gidx[:, :, 0:1].rearrange("p t o -> p (t o)")))
            step(dve.tensor_tensor(g_one[:], iota_row[:, 0:4].unsqueeze(1).to_broadcast([P, TC, 4]),
                                   gidx_f[:].unsqueeze(2).to_broadcast([P, TC, 4]), ALU.is_equal))
            for g in range(4):
                dst = e_sel if g == 0 else e_part
                step(dve.tensor_tensor(dst[:], logits[:, :, 4 + 8 * g:12 + 8 * g],
                                       g_one[:, :, g:g + 1].to_broadcast([P, TC, 8]), ALU.mult))
                if g:
                    step(dve.tensor_tensor(e_sel[:], e_sel[:], e_part[:], ALU.add))
            for t in range(TC):
                step(dve.max(emax[:, t, :], e_sel[:, t, :]))
                step(dve.max_index(eidx[:, t, :], emax[:, t, :], e_sel[:, t, :]))
            dve.tensor_tensor(e2[:], emax[:, :, 1:2].rearrange("p t o -> p (t o)"),
                              emax[:, :, 0:1].rearrange("p t o -> p (t o)"), ALU.subtract).then_inc(ed_ready, 1)
            step(dve.tensor_copy(eidx_f[:], eidx[:, :, 0:2]))
            step(dve.scalar_tensor_tensor(out=flat_e[:], in0=gidx_f[:].unsqueeze(2).to_broadcast([P, TC, 2]),
                                          scalar=8.0, in1=eidx_f[:], op0=ALU.mult, op1=ALU.add))
            dve.tensor_tensor(chosen[:], iota_row[:, 0:32].unsqueeze(1).to_broadcast([P, 8, 32]),
                              flat_e[:].rearrange("p t k -> p (t k)").unsqueeze(2).to_broadcast([P, 8, 32]),
                              ALU.is_equal).then_inc(chosen_ready, 1)
            dve.wait_ge(gexp_ready, 1)
            step(dve.tensor_reduce(p_group[:], gexp[:], AX.X, ALU.add))
            step(dve.reciprocal(p_group[:], p_group[:]))
            dve.wait_ge(eexp_ready, 1)
            step(dve.tensor_scalar(den[:], e2[:], 1.0, None, ALU.add))
            step(dve.reciprocal(den[:], den[:]))
            step(dve.tensor_tensor(gates[:, :, 0], den[:], p_group[:], ALU.mult))
            step(dve.tensor_tensor(gates[:, :, 1], gates[:, :, 0], e2[:], ALU.mult))
            dve.wait_ge(ranks_ready, 1)
            step(dve.tensor_copy(totals[:], bank[2][:, 0:256]))
            step(dve.memset(before[:, 0, :], 0.0))
            for g in range(1, 8):
                step(dve.tensor_tensor(before[:, g, :], before[:, g - 1, :], totals[:, g - 1, :], ALU.add))
            step(dve.tensor_tensor(counts[:], before[:, 7, :], totals[:, 7, :], ALU.add))
            step(dve.tensor_tensor(before[:], bank[1][:, 0:256].rearrange("p (g e) -> p g e", g=8), before[:],
                                   ALU.add))
            step(dve.tensor_tensor(prod[:], before[:], chosen[:], ALU.mult))
            step(dve.tensor_reduce(rank[:], prod[:], AX.X, ALU.add))
            step(dve.tensor_scalar(n_blk[:], counts[:], 0.0, None, ALU.is_gt))
            for j in range(1, TC):
                step(dve.scalar_tensor_tensor(out=n_blk[:], in0=counts[:], scalar=128.0 * j, in1=n_blk[:],
                                              op0=ALU.is_gt, op1=ALU.add))
            step(dve.tensor_tensor_scan(end_blk[:], ones[:, 0:32], n_blk[:], 0.0, ALU.mult, ALU.add))
            step(dve.tensor_tensor(first_blk[:], end_blk[:], n_blk[:], ALU.subtract))
            step(dve.tensor_scalar(fl[:], rank[:], 128.0, None, ALU.is_ge))
            for j in range(2, TC):
                step(dve.scalar_tensor_tensor(out=fl[:], in0=rank[:], scalar=128.0 * j, in1=fl[:],
                                              op0=ALU.is_ge, op1=ALU.add))
            step(dve.scalar_tensor_tensor(out=slot[:], in0=fl[:], scalar=-128.0, in1=rank[:], op0=ALU.mult,
                                          op1=ALU.add))
            step(dve.tensor_tensor(prod[:], chosen[:], first_blk[:].unsqueeze(1).to_broadcast([P, 8, 32]),
                                   ALU.mult))
            step(dve.tensor_reduce(blk[:], prod[:], AX.X, ALU.add))
            step(dve.tensor_tensor(blk[:], blk[:], fl[:], ALU.add))
            for g in range(8):
                dve.tensor_scalar(slot_one[:, g, :], iota_row[:], slot[:, g:g + 1], None, ALU.is_equal)
                ins = dve.tensor_scalar(blk_one[:, g, :], iota_row[:, 0:NBX], blk[:, g:g + 1],
                                        iota_p[:, g:g + 1], ALU.is_equal, ALU.mult)
            ins.then_inc(ones_ready, 1)
            step(dve.tensor_tensor(le[:], end_blk[0:1, :].unsqueeze(1).to_broadcast([1, NBX, 32]),
                                   iota_row[0:1, 0:NBX].unsqueeze(2).to_broadcast([1, NBX, 32]), ALU.is_le))
            step(dve.tensor_reduce(exp_f[:], le[:], AX.X, ALU.add))
            step(dve.tensor_scalar(exp_i[:], exp_f[:], float(N_EXPERTS - 1), None, ALU.min))
            step(dve.tensor_scalar(pairs_f[:], end_blk[0:1, 31:32], 0.5, 0.25, ALU.mult, ALU.add))
            step(dve.tensor_copy(pairs_i[:], pairs_f[:]))
            dve.wait_ge(list_ready, 1)
            step(dve.tensor_copy(list_f[:], bank[3][:, 0:NBX]))
            step(dve.tensor_scalar(empty[:], list_f[:], 0.0, 65536.0, ALU.is_equal, ALU.mult))
            step(dve.scalar_tensor_tensor(out=row_f[:], in0=list_f[:], scalar=-1.0, in1=empty[:],
                                          op0=ALU.add, op1=ALU.add))
            step(dve.tensor_scalar(tok_f[:], row_f[:], float(SEQ), -float(SEQ), ALU.is_ge, ALU.mult))
            step(dve.tensor_tensor(tok_f[:], row_f[:], tok_f[:], ALU.add))
            step(dve.tensor_copy(row_i[:], row_f[:]))
            dve.tensor_copy(tok_i[:], tok_f[:]).then_inc(lists_done, 1)
            dve.sem_inc(act_done, 2)
            dve.sem_inc(lo_done, RAW)
            dve.sem_inc(y_v, 1)
            pairs = dve.value_load(pairs_i[0:1, 0:1], min_val=1, max_val=NB_MAX // 2)

            def split_lo(i, s, j):
                r, q = unit_slot(s, j)
                dve.wait_ge(hi_done, unit(i, s, j) + 1)
                dve.tensor_tensor(w_lo[q][:], raw[r][:], w_hi[q][:].bitcast(F32), ALU.subtract)\
                   .then_inc(lo_done, 1)

            def x_low(s, b):
                dve.wait_ge(xhi_done, b + 1)
                dve.tensor_tensor(x_lo[s][:, 0:4, :], bank[0][:].rearrange("p (c t) -> p c t", c=4),
                                  x_hi[s][:, 0:4, :].bitcast(F32), ALU.subtract)
                dve.tensor_tensor(x_lo[s][:, 4:8, :], bank[1][:].rearrange("p (c t) -> p c t", c=4),
                                  x_hi[s][:, 4:8, :].bitcast(F32), ALU.subtract).then_inc(xlo_done, 1)

            def first_lo(n):
                dve.wait_ge(hi_done, n + 1)
                dve.tensor_tensor(w_lo[n][:], raw[n][:], w_hi[n][:].bitcast(F32), ALU.subtract)\
                   .then_inc(lo_done, 1)

            x_low(0, 0)
            first_lo(0)
            first_lo(1)
            x_low(1, 1)
            first_lo(2)
            first_lo(3)
            with dve.Fori(0, pairs) as i:
                for s in range(2):
                    b = 2 * i + s
                    split_lo(i, s, 0)
                    split_lo(i, s, 1)
                    dve.wait_ge(silu_done, b + 1)
                    dve.wait_ge(unit_used, SPLIT + unit(i, s, 0))
                    dve.tensor_tensor(act[s], bank[4][:], silu_g[s], ALU.mult).then_inc(act_done, 1)
                    split_lo(i, s, 2)
                    dve.wait_ge(ahi_done, b + 1)
                    dve.tensor_tensor(a_lo[s][:], bank[5][:].rearrange("p (c t) -> p c t", c=4),
                                      a_hi[s][:].bitcast(F32), ALU.subtract).then_inc(alo_done, 1)
                    x_low(s, b + 2)
                    split_lo(i, s, 3)
                    split_lo(i, s, 4)
                    split_lo(i, s, 5)
                    dve.wait_ge(unit_used, SPLIT + unit(i, s, 3) + 1)
                    dve.wait_ge(scattered[s], 16 * i + 16)
                    dve.tensor_copy(y_rows[s][:, 512:1024], bank[7][:]).then_inc(y_v, 1)

        @block.tensor
        def _(pe):
            for c in range(KC):
                pe.wait_ge(sq_ready, c + 1)
                ins = pe.matmul(bank[0][:], ones[:], sq[:, c, :], start=(c == 0), stop=(c == KC - 1))
            ins.then_inc(ssq_ready, 1)
            pe.wait_ge(h2_ready, KC)
            for t in range(TC):
                for half in range(2):
                    for c in range(4):
                        ins = pe.transpose(bank[(2 * t + half) % 8][:, 128 * c:128 * c + 128],
                                           h2[:, 4 * half + c, 128 * t:128 * t + 128], ident[:])
                    ins.then_inc(h2t_ready, 1)
            pe.wait_ge(router_landed, 64)
            pe.wait_ge(h2t_evac_v, 1)
            for t in range(TC):
                for c in range(KC):
                    ins = pe.matmul(bank[0][:, 36 * t:36 * t + 36], h2[:, c, 128 * t:128 * t + 128],
                                    w_router[:, c, :], start=(c == 0), stop=(c == KC - 1))
            ins.then_inc(logits_ready, 1)
            pe.wait_ge(chosen_ready, 1)
            pe.wait_ge(tables_ready, 1)
            pe.wait_ge(h2t_evac_s, TC)
            pe.wait_ge(h2t_evac_v, TC)
            pe.matmul(bank[1][:, 0:256], tri[:], chosen[:].rearrange("p g e -> p (g e)"), start=True, stop=True)
            pe.matmul(bank[2][:, 0:256], ones[:], chosen[:].rearrange("p g e -> p (g e)"), start=True,
                      stop=True).then_inc(ranks_ready, 1)
            pe.wait_ge(ones_ready, 1)
            for g in range(8):
                ins = pe.matmul(bank[3][:, 0:NBX], slot_one[:, g, :], blk_one[:, g, :], start=(g == 0),
                                stop=(g == 7))
            ins.then_inc(list_ready, 1)
            pe.wait_ge(lists_done, 1)
            pe.sem_inc(unit_used, SPLIT)
            pairs = pe.value_load(pairs_i[0:1, 0:1], min_val=1, max_val=NB_MAX // 2)

            def gate_like(out, s, q, h):
                for k in range(4):
                    c = 4 * h + k
                    pe.matmul(out, x_hi[s][:, c, :], w_lo[q][:, k, :], start=(h == 0 and k == 0), stop=False)
                    pe.matmul(out, x_lo[s][:, c, :], w_hi[q][:, k, :], start=False, stop=False)
                    ins = pe.matmul(out, x_hi[s][:, c, :], w_hi[q][:, k, :], start=False,
                                    stop=(h == 1 and k == 3))
                return ins

            def transpose_x(s, turn):
                pe.wait_ge(gathered[s], 16 * turn + 16)
                for c in range(KC):
                    ins = pe.transpose(bank[c // 4][:, 128 * (c % 4):128 * (c % 4) + 128],
                                       x_rows[s][:, 128 * c:128 * c + 128], ident[:])
                ins.then_inc(xt_ready, 1)

            transpose_x(0, 0)
            pe.wait_ge(xlo_done, 1)
            transpose_x(1, 0)
            for h in range(2):
                pe.wait_ge(lo_done, RAW + h + 1)
                gate_like(bank[2][:], 0, h, h).then_inc(unit_used, 1)
            for h in range(2):
                pe.wait_ge(lo_done, RAW + 2 + h + 1)
                gate_like(bank[4][:], 0, 2 + h, h).then_inc(unit_used, 1)
            with pe.Fori(0, pairs) as i:
                for s in range(2):
                    b = 2 * i + s
                    pe.wait_ge(xlo_done, b + 2)
                    for h in range(2):
                        _, q = unit_slot(s, h)
                        pe.wait_ge(lo_done, RAW + unit(i, s, h) + 1)
                        gate_like(bank[3 - s][:], 1 - s, q, h).then_inc(unit_used, 1)
                    pe.wait_ge(act_done, b + 3)
                    for k in range(4):
                        ins = pe.transpose(bank[5][:, 128 * k:128 * k + 128], act[s][:, 128 * k:128 * k + 128],
                                           ident[:])
                    ins.then_inc(at_ready, 1)
                    transpose_x(s, i + 1)
                    pe.wait_ge(alo_done, b + 1)
                    for h in range(2):
                        _, q = unit_slot(s, 2 + h)
                        pe.wait_ge(lo_done, RAW + unit(i, s, 2 + h) + 1)
                        pe.wait_ge((y_s, y_v)[h], b + 1)
                        out = bank[6 + h][:]
                        for k in range(4):
                            pe.matmul(out, a_hi[s][:, k, :], w_lo[q][:, k, :], start=(k == 0), stop=False)
                            pe.matmul(out, a_lo[s][:, k, :], w_hi[q][:, k, :], start=False, stop=False)
                            ins = pe.matmul(out, a_hi[s][:, k, :], w_hi[q][:, k, :], start=False, stop=(k == 3))
                        ins.then_inc(unit_used, 1)
                    pe.wait_ge(xlo_done, b + 2)
                    for h in range(2):
                        _, q = unit_slot(s, 4 + h)
                        pe.wait_ge(lo_done, RAW + unit(i, s, 4 + h) + 1)
                        gate_like(bank[4][:], 1 - s, q, h).then_inc(unit_used, 1)
    return used


def second_stage(nc, cst, x, mod_col, vec, w, dram, out):
    used = []
    with ExitStack() as ctx:
        def sb(name, shape, dt=F32):
            return ctx.enter_context(nc.sbuf_tensor("second_" + name, shape, dt))

        def sem(name):
            used.append(ctx.enter_context(nc.semaphore("second_" + name)))
            return used[-1]

        bank = [ctx.enter_context(nc.psum_tensor(f"second_bank{i}", [P, 512], F32)) for i in range(8)]
        ident, ones, gates = cst["ident"], cst["ones"], cst["gates"]
        RAWC, SPC = 4, 2
        raw = [sb(f"c_raw{i}", [P, KC, 256]) for i in range(RAWC)]
        w_hi = [sb(f"c_hi{i}", [P, KC, 256], F32R) for i in range(SPC)]
        w_lo = [sb(f"c_lo{i}", [P, KC, 256], F32R) for i in range(SPC)]
        x_hi = sb("cx_hi", [P, KC, SEQ], F32R)
        x_lo = sb("cx_lo", [P, KC, SEQ], F32R)
        g_hi = sb("cg_hi", [P, KC, SEQ], F32R)
        g_lo = sb("cg_lo", [P, KC, SEQ], F32R)
        work = sb("c_work", [P, 12288])

        def tile(a, n):
            return work[:, a:a + n]

        f_rows = tile(0, 4096).rearrange("p (t d) -> p t d", t=TC)
        y1_rows = tile(4096, 4096).rearrange("p (t d) -> p t d", t=TC)
        sq = tile(8192, 4096).rearrange("p (c t) -> p c t", c=KC)
        q_t = tile(0, 2048).rearrange("p (c t) -> p c t", c=4)
        k_t = tile(2048, 2048).rearrange("p (c t) -> p c t", c=4)
        v_t = tile(4096, 2048).rearrange("p (t d) -> p t d", t=TC)
        u_t = tile(6144, 2048).rearrange("p (c t) -> p c t", c=4)
        cum = tile(8192, 512)
        diff = tile(8704, 512)
        pooled = [tile(9216 + 512 * g, 512) for g in range(4)]
        s_t = [tile(6144 + 512 * i, 512) for i in range(2)]
        pt_t = [tile(7168 + 512 * i, 512) for i in range(2)]
        bias_row = tile(8192, 512)
        bias_diag = tile(8704, 512).rearrange("p (i k) -> p i k", i=TC)
        att = [tile(11264 + 512 * i, 512).rearrange("p (i d) -> p i d", i=TC) for i in range(2)]
        relu_t = [tile(512 * i, 512) for i in range(2)]
        hid_t = [tile(1024 + 512 * i, 512) for i in range(2)]
        mean_t = tile(2048, 512)
        rstd = sb("c_rstd", [P, SEQ])
        out_rows = tile(8192, 4096).rearrange("p (t d) -> p t d", t=TC)
        w_forget = sb("w_forget", [P, KC, HEADS])
        w_pool = tile(11264, 512).rearrange("p (g d) -> p g d", g=4)
        b_forget = sb("b_forget", [HEADS, 1])
        z = sb("z", [HEADS, SEQ])
        az = work[0:HEADS, 8192:8704]
        cf = work[0:HEADS, 11776:12288]
        cq = sb("cq", [P, TC, HEADS])
        sel = sb("sel", [HEADS, HEADS, P])
        causal = sb("causal", [P, P])
        inv_count = sb("inv_count", [P, 16])
        IT = [(h, i) for h in range(HEADS) for i in range(TC)]
        m_diag = sb("m_diag", [P, len(IT)])
        m_off = sb("m_off", [P, len(IT)])
        m_bias = sb("m_bias", [P, len(IT)])
        r_sum = sb("r_sum", [P, len(IT)])
        r_inv = sb("r_inv", [P, len(IT)])

        y_landed = sem("y_landed")
        side_landed = sem("side_landed")
        pool_landed = sem("pool_landed")
        tables = sem("c_tables")
        dve_step = sem("c_dve_step")
        pool_step = sem("c_pool_step")
        act_step = sem("c_act_step")
        f_ready = sem("f_ready")
        ft_ready = sem("ft_ready")
        xf_ready = sem("xf_ready")
        sq_ready = sem("c_sq_ready")
        ssq_ready = sem("c_ssq_ready")
        var_ready = sem("c_var_ready")
        std_ready = sem("c_std_ready")
        x_ready = sem("cx_ready")
        xhi_done = sem("cxhi_done")
        xlo_done = sem("cxlo_done")
        raw_landed = [sem(f"c_landed{i}") for i in range(RAWC)]
        hi_done = sem("c_hi_done")
        lo_done = sem("c_lo_done")
        acc_ready = sem("c_acc_ready")
        acc_used = sem("c_acc_used")
        fl_ready = sem("fl_ready")
        az_ready = sem("az_ready")
        ln_ready = sem("ln_ready")
        cf_ready = sem("cf_ready")
        cft_ready = sem("cft_ready")
        pooled_ready = sem("pooled_ready")
        py_ready = sem("py_ready")
        ghi_done = sem("ghi_done")
        glo_done = sem("glo_done")
        bias_ready = sem("bias_ready")
        bias_used = sem("bias_used")
        s_ready = sem("cs_ready")
        s_used = sem("cs_used")
        mb_ready = sem("cmb_ready")
        p_ready = sem("cp_ready")
        pt_ready = sem("cpt_ready")
        pt_used = sem("cpt_used")
        o_ready = sem("co_ready")
        o_used = sem("co_used")
        at_ready = sem("cat_ready")
        mix_ready = sem("mix_ready")
        mix_used = sem("mix_used")
        mean_ready = sem("mean_ready")
        cent_ready = sem("cent_ready")
        hid_ready = sem("hid_ready")
        relu_done = sem("relu_done")
        square_done = sem("square_done")
        hidhi_done = sem("hidhi_done")
        hidlo_done = sem("hidlo_done")
        down_ready = sem("down_ready")
        down_used = sem("down_used")
        outt_ready = sem("outt_ready")
        left_done = sem("left_done")
        right_done = sem("right_done")
        out_stored = sem("out_stored")

        w_in = w["w_in_2"][0].rearrange("(k p) n -> p k n", p=P)
        w_out = w["w_out_2"][0].rearrange("(k p) n -> p k n", p=P)
        w_up = w["w_mlp1_2"][0].rearrange("(k p) n -> p k n", p=P)
        w_down = w["w_mlp2_2"][0].rearrange("(g k p) n -> g p k n", p=P, k=KC)
        NIN, NOUT = 8, 4
        FIRST = NIN + NOUT

        def loop_unit(g, j):
            return FIRST + 8 * g + j

        def loop_landed(g, j):
            return 16 * (FIRST // RAWC + 2 * g + j // RAWC + 1)

        block = ctx.enter_context(nc.Block())

        @block.sync
        def _(sp):
            for t in range(TC):
                sp.dma_start(f_rows[:, t, :], dram["y"][t * 128:(t + 1) * 128, :]).then_inc(y_landed, 16)
                sp.dma_start(y1_rows[:, t, :], dram["y"][SEQ + t * 128:SEQ + (t + 1) * 128, :])\
                  .then_inc(y_landed, 16)
            for n in range(FIRST):
                if n >= RAWC:
                    sp.wait_ge(lo_done, n + 1)
                src = w_in[:, :, 256 * n:256 * n + 256] if n < NIN else w_out[:, :, 256 * (n - NIN):256 * (n - NIN) + 256]
                sp.dma_start(raw[n % RAWC][:], src).then_inc(raw_landed[n % RAWC], 16)
            with sp.Fori(0, 4) as g:
                for j in range(8):
                    sp.wait_ge(lo_done, loop_unit(g, j) + 1)
                    src = w_up[:, :, bass.ds(1024 * g + 256 * j, 256)] if j < 4 else \
                        w_down[bass.ds(g, 1), :, :, 256 * (j - 4):256 * (j - 4) + 256]
                    sp.dma_start(raw[j % RAWC][:], src).then_inc(raw_landed[j % RAWC], 16)
            for t in range(TC):
                sp.wait_ge(left_done, t + 1)
                sp.wait_ge(right_done, t + 1)
                sp.dma_start(out[0, t * 128:(t + 1) * 128, :], out_rows[:, t, :]).then_inc(out_stored, 16)
            sp.wait_ge(out_stored, 16 * TC)

        @block.gpsimd
        def _(pool):
            n = [0]

            def step(ins):
                n[0] += 1
                ins.then_inc(pool_step, 1)
                pool.wait_ge(pool_step, n[0])

            with nc.allow_non_contiguous_dma(reason="a few columns"):
                pool.dma_start(w_forget[:], w_in[:, :, 2048:2056]).then_inc(side_landed, 16)
                pool.dma_start(b_forget[:], w["b_f_2"].rearrange("o h -> h o")).then_inc(side_landed, 16)
            pool.wait_ge(ssq_ready, 1)
            pool.dma_start(w_pool, w["pool_w_2"][0].rearrange("g c d -> c g d")).then_inc(pool_landed, 16)
            step(pool.memset(sel[:], 1.0))
            step(pool.affine_select(out=sel[:], in_=sel[:], compare_op=ALU.is_equal, fill=0.0, base=0,
                                    pattern=[[-1, HEADS], [0, P]], channel_multiplier=1))
            step(pool.memset(causal[:], 0.0))
            step(pool.affine_select(out=causal[:], in_=causal[:], compare_op=ALU.is_ge, fill=NEG, base=0,
                                    pattern=[[-1, P]], channel_multiplier=1))
            pool.iota(inv_count[:], pattern=[[1, 16]], base=1, channel_multiplier=0,
                      allow_small_or_imprecise_dtypes=True).then_inc(tables, 1)

        @block.scalar
        def _(act):
            def split_hi(landed, slot):
                act.wait_ge(raw_landed[slot % RAWC], landed)
                act.activation(w_hi[slot % SPC][:], raw[slot % RAWC][:], ACT.Copy).then_inc(hi_done, 1)

            def first_hi(n):
                if SPC <= n < NIN + SPC:
                    act.wait_ge(acc_ready, 2 * (n - SPC) + 2)
                elif n >= NIN + SPC:
                    act.wait_ge(mix_ready, 2 * (n - SPC - NIN) + 2)
                split_hi(16 * (n // RAWC + 1), n)

            for c in range(KC):
                act.wait_ge(xf_ready, c + 1)
                act.activation(sq[:, c, :], x[:, c, :], ACT.Square).then_inc(sq_ready, 1)
            first_hi(0)
            first_hi(1)
            act.wait_ge(var_ready, 1)
            act.activation(rstd[:], rstd[:], ACT.Sqrt).then_inc(std_ready, 1)
            for c in range(KC):
                act.wait_ge(x_ready, c + 1)
                act.activation(x_hi[:, c, :], x[:, c, :], ACT.Copy).then_inc(xhi_done, 1)
            act.wait_ge(az_ready, 1)
            act.activation(az, az, ACT.Exp, scale=-1.0).then_inc(act_step, 1)
            act.wait_ge(act_step, 1)
            act.activation(az, az, ACT.Ln, bias=1.0).then_inc(ln_ready, 1)
            for n in range(NIN):
                for k in range(2):
                    act.wait_ge(acc_ready, 2 * n + k + 1)
                    src = bank[(2 * n + k) % 4]
                    c = 2 * (n % 2) + k
                    if n < 2:
                        ins = act.activation(u_t[:, c, :], src[:], ACT.Copy)
                    elif n < 4:
                        ins = act.activation(q_t[:, c, :], src[:], ACT.Copy, scale=HD ** -0.5)
                    elif n < 6:
                        ins = act.activation(k_t[:, c, :], src[:], ACT.Copy)
                    else:
                        ins = act.activation(v_t[:, 2 * k:2 * k + 2, 256 * (n - 6):256 * (n - 6) + 256],
                                             src[:].rearrange("p (t d) -> p t d", t=2), ACT.Copy)
                    ins.then_inc(acc_used, 1)
                first_hi(n + 2)
            for g in range(4):
                act.wait_ge(py_ready, g + 1)
                act.activation(g_hi[:, g, :], bank[4 + g % 2][:], ACT.Identity,
                               scale=vec["pool_scale"][:, g:g + 1]).then_inc(ghi_done, 1)

            def p_transposed(n):
                h, i = IT[n]
                act.wait_ge(pt_ready, n + 1)
                if n >= 2:
                    act.wait_ge(o_ready, n - 1)
                act.activation(pt_t[n % 2][:, 0:128 * (i + 1)], bank[2 + n % 2][:, 0:128 * (i + 1)], ACT.Copy)\
                   .then_inc(pt_used, 1)

            def att_high(pair):
                act.wait_ge(at_ready, pair + 1)
                act.activation(g_hi[:, 4 + pair, :], bank[7][:], ACT.Copy).then_inc(ghi_done, 1)

            for n, (h, i) in enumerate(IT):
                act.wait_ge(mb_ready, n + 1)
                m = 128 * (i + 1)
                act.activation(s_t[n % 2][:, 0:m], s_t[n % 2][:, 0:m], ACT.Exp, bias=m_bias[:, n:n + 1],
                               accum_out=r_sum[:, n:n + 1]).then_inc(p_ready, 1)
                if n >= 1:
                    p_transposed(n - 1)
                if n >= 12 and n % 8 == 4:
                    att_high(n // 8 - 1)
            p_transposed(len(IT) - 1)
            att_high(3)
            for n in range(NIN + 2, FIRST):
                first_hi(n)

            def norm_part(turn):
                for c in range(KC):
                    act.wait_ge(cent_ready, KC * turn + c + 1)
                    act.activation(sq[:, c, :], x[:, c, :], ACT.Square).then_inc(sq_ready, 1)
                act.wait_ge(var_ready, turn + 2)
                act.activation(rstd[:], rstd[:], ACT.Sqrt).then_inc(std_ready, 1)

            norm_part(0)
            for c in range(KC):
                act.wait_ge(x_ready, KC + c + 1)
                act.activation(x_hi[:, c, :], x[:, c, :], ACT.Copy).then_inc(xhi_done, 1)
            with act.Fori(0, 4) as g:
                for j in range(8):
                    if 2 <= j < 6:
                        act.wait_ge(hid_ready, 8 * g + 2 * (j - 2) + 2)
                    else:
                        act.wait_ge(down_ready, 8 * g + (2 * j + 6 if j < 2 else 2 * (j - 6) + 10))
                    split_hi(loop_landed(g, j), j)
                    for k in range(2):
                        if 1 <= j <= 4:
                            t = 2 * (j - 1) + k
                            act.wait_ge(hid_ready, 8 * g + t + 1)
                            act.wait_ge(square_done, 8 * g + t + 1)
                            act.activation(relu_t[k], bank[t % 4][:], ACT.Relu).then_inc(relu_done, 1)
                            act.wait_ge(relu_done, 8 * g + t + 1)
                            act.activation(g_hi[:, t, :], relu_t[k], ACT.Square).then_inc(hidhi_done, 1)
            norm_part(1)
            for t in range(TC):
                act.wait_ge(outt_ready, 2 * t + 2)
                act.activation(out_rows[:, t, 512:1024], bank[(2 * t + 1) % 8][:], ACT.Copy).then_inc(right_done, 1)

        @block.vector
        def _(dve):
            n_step = [0]

            def step(ins):
                n_step[0] += 1
                ins.then_inc(dve_step, 1)
                dve.wait_ge(dve_step, n_step[0])

            def split_lo(n, slot):
                dve.wait_ge(hi_done, n + 1)
                dve.tensor_tensor(w_lo[slot % SPC][:], raw[slot % RAWC][:], w_hi[slot % SPC][:].bitcast(F32),
                                  ALU.subtract).then_inc(lo_done, 1)

            dve.sem_inc(lo_done, RAWC)
            dve.sem_inc(square_done, 2)
            dve.sem_inc(down_used, 4)
            for t in range(TC):
                dve.wait_ge(y_landed, 16 * 2 * TC)
                step(dve.tensor_scalar(f_rows[:, t, :], f_rows[:, t, :], gates[:, t, 0:1], None, ALU.mult))
                dve.scalar_tensor_tensor(out=f_rows[:, t, :], in0=y1_rows[:, t, :], scalar=gates[:, t, 1:2],
                                         in1=f_rows[:, t, :], op0=ALU.mult, op1=ALU.add).then_inc(f_ready, 1)
            for c in range(KC):
                dve.wait_ge(ft_ready, c + 1)
                dve.scalar_tensor_tensor(out=x[:, c, :], in0=bank[c][:], scalar=mod_col[:, 40 + c:41 + c],
                                         in1=x[:, c, :], op0=ALU.mult, op1=ALU.add).then_inc(xf_ready, 1)
            dve.wait_ge(ssq_ready, 1)
            dve.tensor_scalar(rstd[:], bank[0][:], 1.0 / D, NORM_EPS, ALU.mult, ALU.add).then_inc(var_ready, 1)
            split_lo(0, 0)
            split_lo(1, 1)
            dve.wait_ge(std_ready, 1)
            step(dve.reciprocal(rstd[:], rstd[:]))
            for c in range(KC):
                dve.scalar_tensor_tensor(out=x[:, c, :], in0=x[:, c, :], scalar=vec["final_norm"][:, c:c + 1],
                                         in1=rstd[:], op0=ALU.mult, op1=ALU.mult).then_inc(x_ready, 1)
            for c in range(KC):
                dve.wait_ge(xhi_done, c + 1)
                dve.tensor_tensor(x_lo[:, c, :], x[:, c, :], x_hi[:, c, :].bitcast(F32), ALU.subtract)\
                   .then_inc(xlo_done, 1)
            dve.wait_ge(fl_ready, 1)
            dve.wait_ge(side_landed, 32)
            step(dve.tensor_scalar(z[:], bank[4][0:HEADS, :], b_forget[:, 0:1], None, ALU.add))
            dve.scalar_tensor_tensor(out=az, in0=z[:], scalar=-1.0, in1=z[:], op0=ALU.mult, op1=ALU.max)\
               .then_inc(az_ready, 1)
            dve.wait_ge(tables, 1)
            step(dve.reciprocal(inv_count[:], inv_count[:]))
            dve.wait_ge(ln_ready, 1)
            step(dve.scalar_tensor_tensor(out=z[:], in0=z[:], scalar=0.0, in1=az, op0=ALU.min,
                                          op1=ALU.subtract))
            step(dve.tensor_tensor_scan(cf, ones[0:HEADS, 0:1].to_broadcast([HEADS, SEQ]), z[:], 0.0,
                                        ALU.mult, ALU.add))
            dve.tensor_scalar(z[:], cf, -1.0, None, ALU.mult).then_inc(cf_ready, 1)
            for n in range(2, NIN):
                split_lo(n, n)
                if n < 4:
                    continue
                g = n - 4
                win = 2 << g
                dve.wait_ge(acc_used, 4)
                step(dve.tensor_tensor_scan(cum, ones[:, 0:1].to_broadcast([P, SEQ]), u_t[:, g, :], 0.0,
                                            ALU.mult, ALU.add))
                step(dve.tensor_tensor(diff[:, win:SEQ], cum[:, win:SEQ], cum[:, 0:SEQ - win], ALU.subtract))
                step(dve.tensor_tensor(diff[:, 0:win], cum[:, 0:win], inv_count[:, 0:win], ALU.mult))
                dve.scalar_tensor_tensor(out=pooled[g][:, win:SEQ], in0=diff[:, win:SEQ], scalar=1.0 / win,
                                         in1=u_t[:, g, win:SEQ], op0=ALU.mult, op1=ALU.subtract)
                dve.tensor_tensor(pooled[g][:, 0:win], diff[:, 0:win], u_t[:, g, 0:win], ALU.subtract)\
                   .then_inc(pooled_ready, 1)
            dve.wait_ge(cft_ready, 1)
            step(dve.tensor_copy(cq[:], bank[7][:, 0:TC * HEADS].rearrange("p (t h) -> p t h", t=TC)))
            for g in range(4):
                dve.wait_ge(ghi_done, g + 1)
                dve.scalar_tensor_tensor(out=g_lo[:, g, :], in0=bank[4 + g % 2][:],
                                         scalar=vec["pool_scale"][:, g:g + 1],
                                         in1=g_hi[:, g, :].bitcast(F32), op0=ALU.mult, op1=ALU.subtract)\
                   .then_inc(glo_done, 1)
            split_lo(NIN, NIN)
            split_lo(NIN + 1, NIN + 1)

            def normed(n):
                h, i = IT[n]
                dve.wait_ge(p_ready, n + 1)
                step(dve.reciprocal(r_inv[:, n:n + 1], r_sum[:, n:n + 1]))
                dve.wait_ge(o_ready, n + 1)
                if i == 0 and h % 2 == 0 and h >= 4:
                    dve.wait_ge(at_ready, h // 2 - 1)
                ins = dve.tensor_scalar(att[h // 2 % 2][:, i, 64 * (h % 2):64 * (h % 2) + 64],
                                        bank[4 + n % 2][:, 0:HD], r_inv[:, n:n + 1], None, ALU.mult)
                ins.then_inc(o_used, 1)

            def att_low(pair):
                dve.wait_ge(ghi_done, 4 + pair + 1)
                dve.tensor_tensor(g_lo[:, 4 + pair, :], bank[7][:], g_hi[:, 4 + pair, :].bitcast(F32),
                                  ALU.subtract).then_inc(glo_done, 1)

            for n, (h, i) in enumerate(IT):
                if i == 0:
                    dve.wait_ge(bias_ready, h + 1)
                    dve.tensor_copy(bias_row, bank[6][:])
                    dve.tensor_tensor(bias_diag, bank[6][:].rearrange("p (i k) -> p i k", i=TC),
                                      causal[:].unsqueeze(1).to_broadcast([P, TC, P]), ALU.add)\
                       .then_inc(bias_used, 1)
                    dve.wait_ge(bias_used, h + 1)
                dve.wait_ge(s_ready, n + 1)
                if n >= 2:
                    dve.wait_ge(pt_ready, n - 1)
                a = 128 * i
                s = s_t[n % 2]
                if i:
                    dve.tensor_tensor_reduce(s[:, 0:a], bank[n % 2][:, 0:a], bias_row[:, 0:a], 1.0, -3.0e38,
                                             ALU.add, ALU.max, m_off[:, n:n + 1])
                ins = dve.tensor_tensor_reduce(s[:, a:a + 128], bank[n % 2][:, a:a + 128], bias_diag[:, i, :],
                                               1.0, -3.0e38, ALU.add, ALU.max, m_diag[:, n:n + 1])
                ins.then_inc(s_used, 1)
                dve.wait_ge(s_used, n + 1)
                if i:
                    step(dve.tensor_tensor(m_diag[:, n:n + 1], m_diag[:, n:n + 1], m_off[:, n:n + 1], ALU.max))
                step(dve.tensor_scalar(m_bias[:, n:n + 1], m_diag[:, n:n + 1], cq[:, i, h:h + 1], -1.0,
                                       ALU.add, ALU.mult))
                dve.tensor_tensor(m_bias[:, n:n + 1], m_bias[:, n:n + 1], cq[:, i, h:h + 1], ALU.add)\
                   .then_inc(mb_ready, 1)
                if n >= 2:
                    normed(n - 2)
                if n >= 12 and n % 8 == 4:
                    att_low(n // 8 - 1)
            normed(len(IT) - 2)
            normed(len(IT) - 1)
            att_low(3)
            for n in range(NIN + 2, FIRST):
                split_lo(n, n)
                for k in range(2):
                    c = 2 * (n - NIN - 2) + k
                    dve.wait_ge(mix_ready, c + 1)
                    dve.scalar_tensor_tensor(out=x[:, c, :], in0=x[:, c, :], scalar=ALPHA, in1=bank[c % 4][:],
                                             op0=ALU.mult, op1=ALU.add).then_inc(mix_used, 1)
            for c in range(4, KC):
                dve.wait_ge(mix_ready, c + 1)
                dve.scalar_tensor_tensor(out=x[:, c, :], in0=x[:, c, :], scalar=ALPHA, in1=bank[c % 4][:],
                                         op0=ALU.mult, op1=ALU.add).then_inc(mix_used, 1)

            def norm_part(turn, gain, offset):
                dve.wait_ge(mean_ready, turn + 1)
                step(dve.tensor_scalar(mean_t, bank[4][:], 1.0 / D, None, ALU.mult))
                for c in range(KC):
                    dve.tensor_tensor(x[:, c, :], x[:, c, :], mean_t, ALU.subtract).then_inc(cent_ready, 1)
                dve.wait_ge(ssq_ready, turn + 2)
                dve.tensor_scalar(rstd[:], bank[5][:], 1.0 / D, LN_EPS, ALU.mult, ALU.add).then_inc(var_ready, 1)
                dve.wait_ge(std_ready, turn + 2)
                step(dve.reciprocal(rstd[:], rstd[:]))
                for c in range(KC):
                    step(dve.scalar_tensor_tensor(out=x[:, c, :], in0=x[:, c, :], scalar=gain[:, c:c + 1],
                                                  in1=rstd[:], op0=ALU.mult, op1=ALU.mult))
                    dve.tensor_scalar(x[:, c, :], x[:, c, :], offset[:, c:c + 1], None, ALU.add)\
                       .then_inc(x_ready, 1)

            norm_part(0, vec["ln1_g"], vec["ln1_b"])
            for c in range(KC):
                dve.wait_ge(xhi_done, KC + c + 1)
                dve.tensor_tensor(x_lo[:, c, :], x[:, c, :], x_hi[:, c, :].bitcast(F32), ALU.subtract)\
                   .then_inc(xlo_done, 1)
            for c in range(KC):
                ins = dve.tensor_scalar(x[:, c, :], x[:, c, :], ALPHA, None, ALU.mult)
            step(ins)
            with dve.Fori(0, 4) as g:
                for j in range(8):
                    split_lo(loop_unit(g, j), j)
                    for k in range(2):
                        if 1 <= j <= 4:
                            t = 2 * (j - 1) + k
                            dve.wait_ge(relu_done, 8 * g + t + 1)
                            dve.tensor_tensor(hid_t[k], relu_t[k], relu_t[k], ALU.mult).then_inc(square_done, 1)
                            dve.wait_ge(square_done, 8 * g + t + 3)
                            dve.wait_ge(hidhi_done, 8 * g + t + 1)
                            dve.tensor_tensor(g_lo[:, t, :], hid_t[k], g_hi[:, t, :].bitcast(F32), ALU.subtract)\
                               .then_inc(hidlo_done, 1)
                        if j >= 5:
                            c = 2 * (j - 5) + k
                            dve.wait_ge(down_ready, 8 * g + c + 9)
                            dve.tensor_tensor(x[:, c, :], bank[4 + c % 4][:], x[:, c, :], ALU.add)\
                               .then_inc(down_used, 1)
                for c in range(6, KC):
                    dve.wait_ge(down_ready, 8 * g + c + 9)
                    dve.tensor_tensor(x[:, c, :], bank[4 + c % 4][:], x[:, c, :], ALU.add).then_inc(down_used, 1)
            norm_part(1, vec["ln2_g"], vec["ln2_b"])
            for t in range(TC):
                dve.wait_ge(outt_ready, 2 * t + 1)
                dve.tensor_copy(out_rows[:, t, 0:512], bank[(2 * t) % 8][:]).then_inc(left_done, 1)

        @block.tensor
        def _(pe):
            pe.sem_inc(down_ready, 8)
            pe.wait_ge(f_ready, TC)
            for c in range(KC):
                for t in range(TC):
                    ins = pe.transpose(bank[c][:, 128 * t:128 * t + 128], f_rows[:, t, 128 * c:128 * c + 128],
                                       ident[:])
                ins.then_inc(ft_ready, 1)
            for c in range(KC):
                pe.wait_ge(sq_ready, c + 1)
                ins = pe.matmul(bank[0][:], ones[:], sq[:, c, :], start=(c == 0), stop=(c == KC - 1))
            ins.then_inc(ssq_ready, 1)
            pe.wait_ge(side_landed, 32)
            for c in range(KC):
                pe.wait_ge(x_ready, c + 1)
                ins = pe.matmul(bank[4][0:HEADS, :], w_forget[:, c, :], x[:, c, :], start=(c == 0),
                                stop=(c == KC - 1))
            ins.then_inc(fl_ready, 1)

            def product(out, a_hi, a_lo, b_hi, b_lo, first, last):
                pe.matmul(out, a_hi, b_lo, start=first, stop=False)
                pe.matmul(out, a_lo, b_hi, start=False, stop=False)
                return pe.matmul(out, a_hi, b_hi, start=False, stop=last)

            def by_features(out, q, k, b_hi, b_lo, ready=None):
                for c in range(KC):
                    if ready is not None:
                        pe.wait_ge(*ready(c))
                    ins = product(out, w_hi[q][:, c, 128 * k:128 * k + 128], w_lo[q][:, c, 128 * k:128 * k + 128],
                                  b_hi[:, c, :], b_lo[:, c, :], c == 0, c == KC - 1)
                return ins

            pe.wait_ge(xlo_done, KC)
            for n in range(NIN):
                pe.wait_ge(lo_done, RAWC + n + 1)
                q = n % SPC
                for k in range(2):
                    tile_n = 2 * n + k
                    if tile_n >= 4:
                        pe.wait_ge(acc_used, tile_n - 3)
                    dst = bank[tile_n % 4]
                    if n < 6:
                        ins = by_features(dst[:], q, k, x_hi, x_lo)
                    else:
                        for t in range(2):
                            a = 128 * (2 * k + t)
                            for c in range(KC):
                                ins = product(dst[:, 256 * t:256 * t + 256], x_hi[:, c, a:a + 128],
                                              x_lo[:, c, a:a + 128], w_hi[q][:, c, :], w_lo[q][:, c, :],
                                              c == 0, c == KC - 1)
                    ins.then_inc(acc_ready, 1)
            pe.wait_ge(pool_landed, 16)
            for g in range(4):
                pe.wait_ge(pooled_ready, g + 1)
                if g >= 2:
                    pe.wait_ge(glo_done, g - 1)
                pe.matmul(bank[4 + g % 2][:], w_pool[:, g, :], pooled[g], start=True, stop=True)\
                  .then_inc(py_ready, 1)
                if g == 0:
                    pe.wait_ge(cf_ready, 1)
                    for t in range(TC):
                        ins = pe.transpose(bank[7][:, HEADS * t:HEADS * t + HEADS], cf[:, 128 * t:128 * t + 128],
                                           ident[0:HEADS, 0:HEADS])
                    ins.then_inc(cft_ready, 1)
            pe.wait_ge(acc_used, 2 * NIN)
            pe.wait_ge(glo_done, 4)

            def scores(n):
                h, i = IT[n]
                if i == 0:
                    if h:
                        pe.wait_ge(bias_used, h)
                    pe.matmul(bank[6][:], sel[:, h, :], z[:], start=True, stop=True).then_inc(bias_ready, 1)
                if n >= 2:
                    pe.wait_ge(s_used, n - 1)
                a = 64 * (h % 2)
                pe.matmul(bank[n % 2][:, 0:128 * (i + 1)], q_t[a:a + 64, h // 2, 128 * i:128 * i + 128],
                          k_t[a:a + 64, h // 2, 0:128 * (i + 1)], start=True, stop=True).then_inc(s_ready, 1)

            def turn(n):
                h, i = IT[n]
                pe.wait_ge(p_ready, n + 1)
                if n >= 2:
                    pe.wait_ge(pt_used, n - 1)
                for j in range(i + 1):
                    ins = pe.transpose(bank[2 + n % 2][:, 128 * j:128 * j + 128],
                                       s_t[n % 2][:, 128 * j:128 * j + 128], ident[:])
                ins.then_inc(pt_ready, 1)

            def values(n):
                h, i = IT[n]
                pe.wait_ge(pt_used, n + 1)
                if n >= 2:
                    pe.wait_ge(o_used, n - 1)
                for j in range(i + 1):
                    ins = pe.matmul(bank[4 + n % 2][:, 0:HD], pt_t[n % 2][:, 128 * j:128 * j + 128],
                                    v_t[:, j, HD * h:HD * h + HD], start=(j == 0), stop=(j == i))
                ins.then_inc(o_ready, 1)

            def turn_att(pair):
                pe.wait_ge(o_used, 8 * (pair + 1))
                if pair:
                    pe.wait_ge(glo_done, 4 + pair)
                for t in range(TC):
                    ins = pe.transpose(bank[7][:, 128 * t:128 * t + 128], att[pair % 2][:, t, :], ident[:])
                ins.then_inc(at_ready, 1)

            scores(0)
            for n in range(len(IT)):
                if n + 1 < len(IT):
                    scores(n + 1)
                turn(n)
                if n >= 1:
                    values(n - 1)
                if n >= 11 and n % 8 == 3:
                    turn_att(n // 8 - 1)
            values(len(IT) - 1)
            turn_att(3)
            for n in range(NIN, FIRST):
                pe.wait_ge(lo_done, RAWC + n + 1)
                for k in range(2):
                    c = 2 * (n - NIN) + k
                    if c >= 4:
                        pe.wait_ge(mix_used, c - 3)
                    ins = by_features(bank[c % 4][:], n % SPC, k, g_hi, g_lo,
                                      (lambda cc: (glo_done, max(cc + 1, 4))) if c == 0 else None)
                    ins.then_inc(mix_ready, 1)

            def norm_part(turn_, ready):
                for c in range(KC):
                    ready(c)
                    ins = pe.matmul(bank[4][:], ones[:], x[:, c, :], start=(c == 0), stop=(c == KC - 1))
                ins.then_inc(mean_ready, 1)
                for c in range(KC):
                    pe.wait_ge(sq_ready, KC * (turn_ + 1) + c + 1)
                    ins = pe.matmul(bank[5][:], ones[:], sq[:, c, :], start=(c == 0), stop=(c == KC - 1))
                ins.then_inc(ssq_ready, 1)

            norm_part(0, lambda c: pe.wait_ge(mix_used, c + 1))
            pe.wait_ge(xlo_done, 2 * KC)
            with pe.Fori(0, 4) as g:
                for j in range(8):
                    pe.wait_ge(lo_done, RAWC + loop_unit(g, j) + 1)
                    for k in range(2):
                        t = 2 * (j % 4) + k
                        if j < 4:
                            if t >= 4:
                                pe.wait_ge(hidhi_done, 8 * g + t - 3)
                            ins = by_features(bank[t % 4][:], j % SPC, k, x_hi, x_lo)
                            ins.then_inc(hid_ready, 1)
                        else:
                            pe.wait_ge(down_used, 8 * g + t + 1)
                            ins = by_features(bank[4 + t % 4][:], j % SPC, k, g_hi, g_lo,
                                              (lambda c: (hidlo_done, 8 * g + c + 1)) if t == 0 else None)
                            ins.then_inc(down_ready, 1)
            pe.wait_ge(down_used, 36)
            norm_part(1, lambda c: None)
            pe.wait_ge(x_ready, 3 * KC)
            for t in range(TC):
                for half in range(2):
                    for c in range(4):
                        ins = pe.transpose(bank[(2 * t + half) % 8][:, 128 * c:128 * c + 128],
                                           x[:, 4 * half + c, 128 * t:128 * t + 128], ident[:])
                    ins.then_inc(outt_ready, 1)


INPUTS = ["x", "c", "ctx", "c_ctx", "w_mod", "b_mod", "norm_mix", "w_in", "rpb", "w_att_out", "conv_w", "conv_b",
          "conv_ln_g", "conv_ln_b", "w_conv_out", "w_o", "norm_ffn", "w_router_group", "b_router_group",
          "w_router_expert", "b_router_expert", "w_exp_gate", "w_exp_up", "w_exp_down", "final_norm", "w_in_2",
          "b_f_2", "pool_w_2", "pool_scale_2", "w_out_2", "ln1_g_2", "ln1_b_2", "w_mlp1_2", "w_mlp2_2", "ln2_g_2",
          "ln2_b_2"]


def build_program(nc, w, out):
    with ExitStack() as ctx:
        def sb(name, shape):
            return ctx.enter_context(nc.sbuf_tensor(name, shape, F32))

        cst = {"ident": sb("ident", [P, P]), "ones": sb("ones", [P, P]), "gates": sb("gates", [P, TC, 2])}
        x_mid = sb("x_mid", [P, KC, SEQ])
        mod_col = sb("mod_col", [P, 48])
        vec_all = sb("vec_all", [P, 120])
        vec = {"norm_ffn": vec_all[:, 68:76], "final_norm": vec_all[:, 76:84], "pool_scale": vec_all[:, 84:88],
               "ln1_g": vec_all[:, 88:96], "ln1_b": vec_all[:, 96:104], "ln2_g": vec_all[:, 104:112],
               "ln2_b": vec_all[:, 112:120]}
        dram = {"h2": nc.dram_tensor("h2_rows_dram", [SEQ, D], F32),
                "mark": nc.dram_tensor("mark_dram", [2, 1, P], F32),
                "y": nc.dram_tensor("y_dram", [2 * SEQ, D], F32)}
        used = mixer_stage(nc, cst, x_mid, mod_col, vec_all, w, dram)
        zero_semaphores(nc, used)
        used = moe_stage(nc, cst, x_mid, mod_col, vec, w, dram)
        zero_semaphores(nc, used)
        second_stage(nc, cst, x_mid, mod_col, vec, w, dram, out)


def zero_semaphores(nc, used):
    with nc.Block() as block:
        @block.gpsimd
        def _(pool):
            for s in used:
                pool.sem_clear(s)


def kernel(**inputs):
    import numpy as np
    import concourse.bacc as bacc
    from concourse.bass_utils import run_bass_kernel_spmd

    nc = bacc.Bacc("TRN2", target_bir_lowering=False, num_devices=1)
    arrays, args = {}, {}
    for name in INPUTS:
        a = np.ascontiguousarray(inputs[name])
        arrays[f"in_{name}_dram"] = a
        args[name] = nc.dram_tensor(f"in_{name}_dram", a.shape, mybir.dt.from_np(a.dtype), kind="ExternalInput").ap()
    out = nc.dram_tensor("out_dram", (1, SEQ, D), F32, kind="ExternalOutput").ap()
    build_program(nc, args, out)
    r = run_bass_kernel_spmd(nc, [arrays], core_ids=[0])
    return r.results[0]["out_dram"]
```

```python
from contextlib import ExitStack

import concourse.bass as bass
from concourse import mybir

F32 = mybir.dt.float32
F32R = mybir.dt.float32r
I32 = mybir.dt.int32
U32 = mybir.dt.uint32
ALU = mybir.AluOpType
ACT = mybir.ActivationFunctionType
AX = mybir.AxisListType

P = 128
D = 1024
SEQ = 512
CTX = 256
KC = D // P
TC = SEQ // P
HEADS = 8
HD = 64
N_EXPERTS = 32
NB_MAX = 2 * SEQ // P + N_EXPERTS
NBX = 48
NORM_EPS = 1e-6
LN_EPS = 1e-5
NEG = -1.0e30
RAW = 4
SPLIT = 4
ALPHA = float(2.0 ** 0.25)


GRID = 64
WIN = 16
TAPS = 31
HALF = TAPS // 2
NDC = 2 * WIN - 1
NDR = 15
NM = NDR - 1
RING = 2


def mixer_stage(nc, cst, x_mid, kq_hi, mod_col, vec_all, w):
    used = []
    with ExitStack() as ctx:
        def sb(name, shape, dt=F32):
            return ctx.enter_context(nc.sbuf_tensor("mixer_" + name, shape, dt))

        def sem(name):
            used.append(ctx.enter_context(nc.semaphore("mixer_" + name)))
            return used[-1]

        bank = [ctx.enter_context(nc.psum_tensor(f"mixer_bank{i}", [P, 512], F32)) for i in range(8)]
        ident, ones = cst["ident"], cst["ones"]
        raw = [sb(f"a_raw{i}", [P, 2048]) for i in range(RING)]
        w_hi = [sb(f"a_hi{i}", [P, 2048], F32R) for i in range(2)]
        w_lo = [sb(f"a_lo{i}", [P, 2048], F32R) for i in range(2)]
        early = []
        for name in ("h_hi", "h_lo", "ag_hi", "ag_lo"):
            with nc.sbuf_tensor(f"mixer_{name}_early", [P, 4096], F32) as before:
                early.append(before)
            if name == "h_hi":
                h_hi = sb("h_hi", [P, KC, SEQ], F32R)
            elif name == "h_lo":
                h_lo = sb("h_lo", [P, KC, SEQ], F32R)
            elif name == "ag_hi":
                g_hi = sb("ag_hi", [P, KC, SEQ], F32R)
            else:
                g_lo = sb("ag_lo", [P, KC, SEQ], F32R)
        with nc.sbuf_tensor("mixer_vals_hi", [P, 4096], F32R) as vals_hi:
            pass
        vals = sb("vals", [P, 4096])
        table = sb("table", [P, NM * HEADS * GRID])
        LOWS = 2168
        with nc.sbuf_tensor("mixer_lows", [P, LOWS + 4096], F32R) as lows:
            pass
        work = sb("a_work", [P, LOWS + 4096])
        y_conv = sb("y_conv", [P, 4, SEQ])
        conv_w = sb("conv_w_col", [P, 128])
        c_silu = sb("c_silu", [P, KC, 2])
        mod_ctx = sb("mod_ctx", [P, 16])
        s1 = sb("s1", [P, 16])
        ssq = sb("a_ssq", [P, 8])
        IT = [(h, i) for h in range(HEADS) for i in range(TC)]
        NIT = len(IT)
        m_loc = sb("m_loc", [P, NIT])
        m_ctx = sb("m_ctx", [P, NIT])
        m_neg = sb("m_neg", [P, NIT])
        r_loc = sb("r_loc", [P, NIT])
        r_ctx = sb("r_ctx", [P, NIT])

        m = x_mid
        k_hi, q_hi = kq_hi[:, 0:4, :], kq_hi[:, 4:8, :]
        k_lo, q_lo = g_hi[:, 4:8, :], g_lo[:, 4:8, :]
        v_hi = vals_hi[:, 0:3072].rearrange("p (t d) -> p t d", t=6)
        kc_hi = vals_hi[:, 3072:4096].rearrange("p (c t) -> p c t", c=4)
        kc_lo = lows[:, LOWS:LOWS + 1024].rearrange("p (c t) -> p c t", c=4)
        v_lo = lows[:, LOWS + 1024:LOWS + 4096].rearrange("p (t d) -> p t d", t=6)
        gc_hi = g_hi[:, 0:4, :].rearrange("p a (b t) -> p (a b) t", t=CTX)
        gc_lo = g_lo[:, 0:4, :].rearrange("p a (b t) -> p (a b) t", t=CTX)
        gate_c = vals[:].rearrange("p (c t) -> p c t", c=KC)
        x_rows = table[:, 0:4096].rearrange("p (t d) -> p t d", t=TC)
        c_rows = table[:, 4096:6144].rearrange("p (t d) -> p t d", t=2)
        vec_rows = table[:, 6144:6272]
        conv_rows = table[:, 6272:6400]
        cond_rows = table[:, 6400:6528]
        rpb_rows = table[:, 6528:6528 + NDC]
        bias = table[:].rearrange("p (h m c) -> p h m c", h=HEADS, m=NM)
        UW = SEQ + 2 * HALF
        u_pad = work[:, 0:4 * UW].rearrange("p (c t) -> p c t", c=4)
        part = [work[:, LOWS + 512 * i:LOWS + 512 * i + 512].rearrange("p (s n) -> p s n", s=2) for i in range(2)]
        tmp = [work[:, LOWS + 1024 + 512 * i:LOWS + 1536 + 512 * i] for i in range(2)]
        sig = tmp
        onehot = work[:, LOWS + 3072:LOWS + 3264]
        rpb_t = work[:, LOWS + 3264:LOWS + 3384]
        junk = work[:, 0:1024]
        s_t = [work[:, 768 * i:768 * i + 768] for i in range(2)]
        late_part = [work[:, 1536 + 256 * i:1792 + 256 * i] for i in range(2)]
        sq = work[:, 0:2048].rearrange("p (c t) -> p c t", c=4)
        mean_t = work[:, 2048:2560]
        rstd = work[:, 2560:3072]

        NV = 120
        V_BMOD, V_NORM, V_CB, V_CG, V_CO = 0, 48, 56, 60, 64

        MOD = [("mod", 256 * j) for j in range(24)]
        W_IN = [("in", c) for c in (2048, 1536, 2304, 1792, 512, 768, 1024, 1280, 0, 256,
                                    2560, 2816, 3072, 3328)]
        W_ATT = [("att", 512 * j) for j in range(2)]
        W_GB = [("in", 3584 + 256 * j) for j in range(4)]
        W_CONV = [("conv", 512 * j) for j in range(2)]
        W_O = [("o", 256 * j) for j in range(4)]
        SPLITS = W_IN + W_ATT + W_GB + W_CONV + W_O
        NS = len(SPLITS)
        STREAM = MOD[0:8] + SPLITS[0:10] + MOD[8:24] + SPLITS[10:]
        place = {}
        nmod = nsplit = 0
        for pos, (kind, _) in enumerate(STREAM):
            if kind == "mod":
                place["mod", nmod] = pos
                nmod += 1
            else:
                place["split", nsplit] = pos
                nsplit += 1
        where = {pos: key for key, pos in place.items()}
        slot_of = [2 + pos if pos < 6 else pos % 2 for pos in range(len(STREAM))]

        def use_of(pos):
            return slot_of[:pos + 1].count(slot_of[pos])

        def flat(pos):
            n = slot_of[pos]
            if n < 2:
                return raw[n][:]
            return early[(n - 2) // 2][:, 2048 * (n % 2):2048 * (n % 2) + 2048]

        def name_of(s):
            return ("glu_g glu_a glu_g glu_a k k v v q q ga ga ga ga att att gb gb gb gb "
                    "conv conv o o o o").split()[s]

        COUNT = {"glu_g": 2, "glu_a": 2, "k": 3, "v": 3, "q": 2, "ga": 2, "att": 4, "gb": 2, "conv": 4, "o": 2}
        READER = {"glu_g": "act", "glu_a": "dve", "k": "dve", "v": "dve", "q": "dve", "ga": "act", "att": "dve",
                  "gb": "act", "conv": "dve", "o": "dve"}
        TILES = [(s, k) for s in range(NS) for k in range(COUNT[name_of(s)])]
        first_tile = [min(t for t, (s, _) in enumerate(TILES) if s == u) for u in range(NS)] + [len(TILES)]

        def reads_upto(engine, t):
            return sum(1 for (s, _) in TILES[:t + 1] if READER[name_of(s)] == engine)

        rows_landed = sem("rows_landed")
        cond_landed = sem("cond_landed")
        vec_landed = sem("vec_landed")
        again_landed = sem("again_landed")
        raw_landed = [sem(f"a_landed{i}") for i in range(8)]
        pool_step = sem("a_pool_step")
        dve_step = sem("a_dve_step")
        ident_ready = sem("ident_ready")
        onehot_ready = sem("onehot_ready")
        pad_ready = sem("pad_ready")
        vt_ready = sem("vt_ready")
        vt_used = sem("vt_used")
        rpbt_ready = sem("rpbt_ready")
        silu_ready = sem("silu_ready")
        part_done = sem("part_done")
        pool_part_done = sem("pool_part_done")
        part_summed = sem("part_summed")
        pe_mod_done = sem("pe_mod_done")
        kv_high = sem("kv_high")
        normed = sem("normed")
        r_summed = sem("r_summed")
        r_ready = sem("r_ready")
        s1_ready = sem("s1_ready")
        ssq_done = sem("a_ssq_done")
        var_ready = sem("a_var_ready")
        std_ready = sem("a_std_ready")
        scaled = sem("scaled")
        ht_ready = sem("ht_ready")
        tmp_ready = sem("tmp_ready")
        hhi_done = sem("hhi_done")
        hlo_done = sem("hlo_done")
        hi_done = sem("a_hi_done")
        lo_done = sem("a_lo_done")
        acc_ready = sem("a_acc_ready")
        read_act = sem("acc_read_by_act")
        read_dve = sem("acc_read_by_dve")
        tb_ready = sem("tb_ready")
        tb_used = sem("tb_used")
        masked = sem("masked")
        tap_done = sem("tap_done")
        pool_lo_done = sem("pool_lo_done")
        s_ready = sem("as_ready")
        sc_ready = sem("asc_ready")
        s_used = sem("as_used")
        mc_ready = sem("amc_ready")
        m_ready = sem("am_ready")
        p_ready = sem("ap_ready")
        pt_ready = sem("apt_ready")
        pt_high = sem("apt_high")
        pt_low = sem("apt_low")
        o_ready = sem("ao_ready")
        athi_done = sem("athi_done")
        atlo_done = sem("atlo_done")
        mean_ready = sem("a_mean_ready")
        cent_ready = sem("a_cent_ready")
        sq_ready = sem("a_sq_ready")
        cssq_ready = sem("cssq_ready")
        cvar_ready = sem("cvar_ready")
        cstd_ready = sem("cstd_ready")
        cn_ready = sem("cn_ready")
        act_step = sem("a_act_step")
        cvhi_done = sem("cvhi_done")
        cvlo_done = sem("cvlo_done")
        m_done = sem("m_done")
        mhi_done = sem("mhi_done")
        mlo_done = sem("mlo_done")
        xt_ready = sem("xt_ready")
        xt_used = sem("xt_used")

        w_in = w["w_in"][0].rearrange("(k p) n -> p k n", p=P)
        w_mod = w["w_mod"][0].rearrange("(k p) n -> p k n", p=P)
        w_att = w["w_att_out"][0].rearrange("(k p) n -> p k n", p=P)
        w_cv = w["w_conv_out"][0].rearrange("(k p) n -> p k n", p=P)
        w_o = w["w_o"][0].rearrange("(k p) n -> p k n", p=P)

        def as_k8(t):
            return t[:, :].rearrange("p (k n) -> p k n", k=KC)

        def as_k4(t):
            return t[:, :].rearrange("p (k n) -> p k n", k=4)

        BY_PE = (1, 4, 7)
        BY_DVE = [u for u in range(8) if u not in BY_PE]
        POOL_LOWS = (4, 6, 8)

        def low(engine, s):
            pos = place["split", s]
            engine.wait_ge(hi_done, s + 1)
            engine.tensor_tensor(w_lo[s % 2][:], flat(pos), w_hi[s % 2][:].bitcast(F32), ALU.subtract)\
                .then_inc(pool_lo_done if s in POOL_LOWS else lo_done, 1)

        def wait_low(engine, s):
            if s in POOL_LOWS:
                engine.wait_ge(pool_lo_done, POOL_LOWS.index(s) + 1)
            else:
                engine.wait_ge(lo_done, s + 1 - sum(1 for q in POOL_LOWS if q < s))

        def free_slot(engine, pos):
            before = [q for q in range(pos) if slot_of[q] == slot_of[pos]]
            if before:
                kind, idx = where[before[-1]]
                if kind == "split":
                    wait_low(engine, idx)
                elif idx in BY_PE:
                    engine.wait_ge(pe_mod_done, BY_PE.index(idx) + 1)
                elif idx < 8:
                    engine.wait_ge(part_done, 16 * (BY_DVE.index(idx) + 1))
                else:
                    engine.wait_ge(pool_part_done, 4 * (idx - 7))

        def wait_landed(engine, pos):
            engine.wait_ge(raw_landed[slot_of[pos]], 16 * use_of(pos))

        def kqv_tile(s, k, t, keys, ctx_keys, queries, values):
            name, b = name_of(s), bank[t % 4]
            if name == "k" and k < 2:
                return keys[:, 2 * (s - 4) + k, :], b[:]
            if name == "k":
                return ctx_keys[:, 2 * (s - 4):2 * (s - 4) + 2, :], b[:].rearrange("p (c t) -> p c t", c=2)
            if name == "q":
                return queries[:, 2 * (s - 8) + k, :], b[:]
            return values[:, 2 * k:2 * k + 2, 256 * (s - 6):256 * (s - 6) + 256], \
                b[:].rearrange("p (t d) -> p t d", t=2)

        def tap_of(engine, tap, c):
            wcol = conv_w[:, 4 * tap + c:4 * tap + c + 1]
            if tap == 0:
                return engine.tensor_scalar(y_conv[:, c, :], u_pad[:, c, 0:SEQ], wcol,
                                            vec_all[:, V_CB + c:V_CB + c + 1], ALU.mult, ALU.add)
            return engine.scalar_tensor_tensor(out=y_conv[:, c, :], in0=u_pad[:, c, tap:tap + SEQ], scalar=wcol,
                                               in1=y_conv[:, c, :], op0=ALU.mult, op1=ALU.add)

        block = ctx.enter_context(nc.Block())

        @block.sync
        def _(sp):
            sp.dma_start(cond_rows[0:KC, :], w["c"][0].rearrange("(k p) -> k p", p=P)).then_inc(cond_landed, 16)
            sp.dma_start(cond_rows[KC:2 * KC, :], w["c_ctx"].rearrange("(k p) -> k p", p=P)).then_inc(cond_landed, 16)
            sp.dma_start(x_rows, w["x"][0].rearrange("(t p) d -> p t d", p=P)).then_inc(rows_landed, 16)
            sp.dma_start(c_rows, w["ctx"][0].rearrange("(t p) d -> p t d", p=P)).then_inc(rows_landed, 16)
            sp.wait_ge(vec_landed, 16 * 14)
            for pos, (kind, col) in enumerate(STREAM):
                free_slot(sp, pos)
                if kind in ("att", "conv"):
                    src = (w_att if kind == "att" else w_cv)[:, :, col:col + 512]
                    dst = as_k4(flat(pos))
                else:
                    src = {"mod": w_mod, "in": w_in, "o": w_o}[kind][:, :, col:col + 256]
                    dst = as_k8(flat(pos))
                sp.dma_start(dst, src).then_inc(raw_landed[slot_of[pos]], 16)

        @block.gpsimd
        def _(pool):
            n = [0]

            def step(ins):
                n[0] += 1
                ins.then_inc(pool_step, 1)
                pool.wait_ge(pool_step, n[0])

            step(pool.memset(ident[:], 1.0))
            step(pool.affine_select(out=ident[:], in_=ident[:], compare_op=ALU.is_equal, fill=0.0, base=0,
                                    pattern=[[-1, P]], channel_multiplier=1))
            pool.memset(ones[:], 1.0).then_inc(ident_ready, 1)
            step(pool.memset(onehot, 0.0))
            for at in (GRID + NDC // 2 - 1, 2 * GRID + NDC // 2 - 1):
                ins = pool.affine_select(out=onehot, in_=onehot, compare_op=ALU.not_equal, fill=1.0, base=-at,
                                         pattern=[[1, 192]], channel_multiplier=1)
                if at < 2 * GRID:
                    step(ins)
                else:
                    ins.then_inc(onehot_ready, 1)

            def modulate(u):
                pos = place["mod", u]
                wait_landed(pool, pos)
                if u >= 10:
                    pool.wait_ge(part_summed, u - 1 - len(BY_PE))
                wm = as_k8(flat(pos))
                steps = 4 * (u - 8)
                pool.tensor_tensor(wm, wm, c_silu[:, :, 0:1].to_broadcast([P, KC, 256]), ALU.mult)\
                    .then_inc(pool_part_done, 1)
                pool.wait_ge(pool_part_done, steps + 1)
                pool.tensor_tensor(wm[:, 0:4, :], wm[:, 0:4, :], wm[:, 4:8, :], ALU.add).then_inc(pool_part_done, 1)
                pool.wait_ge(pool_part_done, steps + 2)
                pool.tensor_tensor(wm[:, 0:2, :], wm[:, 0:2, :], wm[:, 2:4, :], ALU.add).then_inc(pool_part_done, 1)
                pool.wait_ge(pool_part_done, steps + 3)
                pool.tensor_tensor(late_part[u % 2], wm[:, 0, :], wm[:, 1, :], ALU.add).then_inc(pool_part_done, 1)
                pool.wait_ge(pool_part_done, steps + 4)

            pool.wait_ge(ssq_done, 6)
            pool.memset(u_pad[:, :, 0:HALF], 0.0)
            pool.memset(u_pad[:, :, HALF + SEQ:UW], 0.0).then_inc(pad_ready, 1)
            for s in POOL_LOWS[:2]:
                low(pool, s)
            pool.wait_ge(tb_used, 16)
            for half in (0, 64):
                window = bias[half:half + 64, :, :, :].rearrange("p h m c -> p (h m) c")
                step(pool.affine_select(out=window[:, :, 0:GRID - WIN], in_=window[:, :, 0:GRID - WIN],
                                        compare_op=ALU.is_ge, fill=NEG, base=WIN // 2,
                                        pattern=[[0, HEADS * NM], [1, GRID - WIN]], channel_multiplier=-1))
                pool.affine_select(out=window[:, :, WIN:GRID], in_=window[:, :, WIN:GRID],
                                   compare_op=ALU.is_ge, fill=NEG, base=WIN // 2 - 1 - WIN,
                                   pattern=[[0, HEADS * NM], [-1, GRID - WIN]], channel_multiplier=1)\
                    .then_inc(masked, 1)
            pool.wait_ge(masked, 2)
            low(pool, POOL_LOWS[2])
            pool.wait_ge(tap_done, 4 * TAPS)
            for u in range(8, 24):
                modulate(u)
            pool.wait_ge(s_used, NIT)
            pool.dma_start(x_rows, w["x"][0].rearrange("(t p) d -> p t d", p=P)).then_inc(again_landed, 16)
            pool.wait_ge(again_landed, 16)

        @block.scalar
        def _(act):
            for i, (name, a) in enumerate((("b_mod", 0), ("norm_mix", 48), ("conv_b", 56), ("conv_ln_g", 60),
                                           ("conv_ln_b", 64), ("norm_ffn", 68), ("final_norm", 76),
                                           ("pool_scale_2", 84), ("ln1_g_2", 88), ("ln1_b_2", 96),
                                           ("ln2_g_2", 104), ("ln2_b_2", 112))):
                src = w[name] if name == "final_norm" else w[name][0]
                rows = src.shape[0] // P
                act.dma_start(vec_rows[a:a + rows, :], src.rearrange("(k p) -> k p", p=P)).then_inc(vec_landed, 16)
            act.dma_start(conv_rows[0:4 * TAPS, :], w["conv_w"][0].rearrange("t (c p) -> (t c) p", p=P))\
               .then_inc(vec_landed, 16)
            act.dma_start(rpb_rows[0:HEADS * NDR, :], w["rpb"][0].rearrange("h r c -> (h r) c"))\
               .then_inc(vec_landed, 16)
            act.wait_ge(vt_ready, 1)
            act.activation(c_silu[:].rearrange("p k s -> p s k"),
                           bank[0][:, 0:16].rearrange("p (s k) -> p s k", s=2), ACT.Silu).then_inc(silu_ready, 1)
            act.wait_ge(rows_landed, 32)
            for t in range(6):
                src = x_rows[:, t, :] if t < 4 else c_rows[:, t - 4, :]
                act.activation(junk, src, ACT.Square, accum_out=ssq[:, t:t + 1]).then_inc(ssq_done, 1)
                act.wait_ge(ssq_done, t + 1)
            act.wait_ge(var_ready, 1)
            act.activation(ssq[:, 0:6], ssq[:, 0:6], ACT.Sqrt).then_inc(std_ready, 1)

            def high(s):
                pos = place["split", s]
                if s >= 12 or 2 <= s < 10:
                    act.wait_ge(acc_ready, first_tile[s - 1])
                elif s >= 10:
                    act.wait_ge(o_ready, s + 5)
                wait_landed(act, pos)
                act.activation(w_hi[s % 2][:], flat(pos), ACT.Copy).then_inc(hi_done, 1)

            for c in range(2 * KC):
                act.wait_ge(tmp_ready, c + 1)
                if c < KC:
                    act.activation(h_hi[:, c, :], tmp[c % 2], ACT.Copy).then_inc(hhi_done, 1)
                else:
                    act.activation(gc_hi[:, c - KC, :], tmp[c % 2][:, 0:CTX], ACT.Copy).then_inc(hhi_done, 1)
                if c == KC - 1:
                    high(0)
                    high(1)

            def table_part(b):
                act.wait_ge(tb_ready, b + 1)
                src = bank[(4, 5, 6)[b % 3]][:, 0:480].rearrange("p (c h m) -> p h m c", c=4, h=HEADS)
                act.activation(bias[0:64, :, :, 4 * b:4 * b + 4], src[0:64, :, 1:NDR, :], ACT.Copy)
                act.activation(bias[64:128, :, :, 4 * b:4 * b + 4], src[64:128, :, 0:NM, :], ACT.Copy)\
                   .then_inc(tb_used, 1)

            def read_tiles(s):
                name = name_of(s)
                for t in range(first_tile[s], first_tile[s + 1]):
                    k = t - first_tile[s]
                    src = bank[t % 4]
                    act.wait_ge(acc_ready, t + 1)
                    if name == "glu_g":
                        if s == 2:
                            act.wait_ge(read_dve, k + 1)
                        else:
                            act.wait_ge(hlo_done, 2 * KC - 1 + k)
                        ins = act.activation(sig[k], src[:], ACT.Sigmoid)
                    elif name == "ga":
                        ins = act.activation(m[:, 2 * (s - 10) + k, :], src[:], ACT.Sigmoid)
                    else:
                        ins = act.activation(gate_c[:, 2 * (s - 16) + k, :], src[:], ACT.Sigmoid)
                    ins.then_inc(read_act, 1)

            def high_tiles(s):
                for t in range(first_tile[s], first_tile[s + 1]):
                    act.wait_ge(acc_ready, t + 1)
                    dst, src = kqv_tile(s, t - first_tile[s], t, k_hi, kc_hi, q_hi, v_hi)
                    act.activation(dst, src, ACT.Copy, scale=HD ** -0.5 if name_of(s) == "q" else 1.0)\
                       .then_inc(kv_high, 1)

            for s in range(10):
                if 2 <= s < 6:
                    for b in range(4 * (s - 2), 4 * (s - 1)):
                        table_part(b)
                if READER[name_of(s)] == "act":
                    read_tiles(s)
                if s >= 4:
                    high_tiles(s)
                if s < 8:
                    high(s + 2)

            def turned_high(n):
                act.wait_ge(pt_ready, 2 * n + 2)
                if n >= 2:
                    act.wait_ge(o_ready, n - 1)
                for b in range(3):
                    act.activation(w_hi[n % 2][:, 512 * b:512 * b + 512], bank[3 + b][:], ACT.Copy)\
                       .then_inc(pt_high, 1)

            def att_high(n):
                h, half = n // 2, n % 2
                a = 64 * (h % 2)
                act.wait_ge(o_ready, n + 1)
                act.activation(g_hi[a:a + 64, h // 2, CTX * half:CTX * half + CTX], bank[6][a:a + 64, 0:CTX],
                               ACT.Copy).then_inc(athi_done, 1)

            for n in range(NIT):
                act.wait_ge(m_ready, n + 1)
                act.activation(s_t[n % 2][:, 0:512], s_t[n % 2][:, 0:512], ACT.Exp, bias=m_neg[:, n:n + 1],
                               accum_out=r_loc[:, n:n + 1])
                act.activation(s_t[n % 2][:, 512:768], bank[2][:, 0:CTX], ACT.Exp,
                               bias=m_neg[:, n:n + 1], accum_out=r_ctx[:, n:n + 1]).then_inc(p_ready, 1)
                if n >= 2 and n % 2 == 0:
                    turned_high(n // 2 - 1)
                if n >= 5 and n % 2 == 1:
                    att_high((n - 5) // 2)
            turned_high(15)
            att_high(14)
            high(10)
            att_high(15)
            high(11)

            def norm_squares():
                for c in range(4):
                    act.wait_ge(cent_ready, c + 1)
                    act.activation(sq[:, c, :], y_conv[:, c, :], ACT.Square).then_inc(sq_ready, 1)

            def norm_root():
                act.wait_ge(cvar_ready, 1)
                act.activation(rstd, rstd, ACT.Sqrt).then_inc(cstd_ready, 1)

            def norm_silu():
                for c in range(4):
                    act.wait_ge(cn_ready, c + 1)
                    act.activation(y_conv[:, c, :], y_conv[:, c, :], ACT.Silu,
                                   scale=vec_all[:, V_CG + c:V_CG + c + 1], bias=vec_all[:, V_CO + c:V_CO + c + 1])\
                       .then_inc(act_step, 1)
                for c in range(4):
                    act.wait_ge(act_step, c + 1)
                    act.activation(g_hi[:, 4 + c, :], y_conv[:, c, :], ACT.Copy).then_inc(cvhi_done, 1)

            def merged_high(c):
                act.wait_ge(m_done, c + 1)
                act.activation(h_hi[:, c, :], m[:, c, :], ACT.Copy).then_inc(mhi_done, 1)

            for s in range(10, NS):
                if s == 10:
                    norm_squares()
                if READER[name_of(s)] == "act":
                    read_tiles(s)
                if s == 11:
                    norm_root()
                if s == 13:
                    norm_silu()
                if s != 21 and s + 2 < NS:
                    high(s + 2)
                if name_of(s) == "conv":
                    for c in range(4 * (s - 20), 4 * (s - 19)):
                        merged_high(c)
                if s == 21:
                    high(s + 2)

        @block.vector
        def _(dve):
            n_step = [0]

            def step(ins):
                n_step[0] += 1
                ins.then_inc(dve_step, 1)
                dve.wait_ge(dve_step, n_step[0])

            dve.wait_ge(vt_ready, 2)
            dve.tensor_copy(vec_all[:, 0:NV], bank[1][:, 0:NV])
            dve.tensor_copy(conv_w[:, 0:4 * TAPS], bank[2][:, 0:4 * TAPS])
            dve.tensor_copy(rpb_t[0:NDC, 0:HEADS * NDR], bank[3][0:NDC, 0:HEADS * NDR]).then_inc(vt_used, 1)

            def modulate(u):
                pos, n = place["mod", u], BY_DVE.index(u)
                wait_landed(dve, pos)
                if n >= 2:
                    dve.wait_ge(part_summed, n - 1)
                for k in range(KC):
                    for c in range(2):
                        wk, dst = as_k8(flat(pos))[:, k, :], part[n % 2][:, c, :]
                        if k == 0:
                            ins = dve.tensor_scalar(dst, wk, c_silu[:, k, c:c + 1], None, ALU.mult)
                        else:
                            dve.wait_ge(part_done, 16 * n + 2 * k + c - 1)
                            ins = dve.scalar_tensor_tensor(out=dst, in0=wk, scalar=c_silu[:, k, c:c + 1], in1=dst,
                                                           op0=ALU.mult, op1=ALU.add)
                        ins.then_inc(part_done, 1)

            dve.wait_ge(silu_ready, 1)
            modulate(BY_DVE[0])
            dve.wait_ge(ssq_done, 6)
            dve.tensor_scalar(ssq[:, 0:6], ssq[:, 0:6], 1.0 / D, NORM_EPS, ALU.mult, ALU.add).then_inc(var_ready, 1)
            modulate(BY_DVE[1])
            dve.wait_ge(std_ready, 1)
            step(dve.reciprocal(ssq[:, 0:6], ssq[:, 0:6]))
            for t in range(6):
                src = x_rows[:, t, :] if t < 4 else c_rows[:, t - 4, :]
                dve.tensor_scalar(src, src, ssq[:, t:t + 1], None, ALU.mult).then_inc(scaled, 1)
            for u in BY_DVE[2:]:
                modulate(u)
            dve.wait_ge(vt_used, 1)
            dve.wait_ge(part_summed, len(BY_DVE))
            dve.wait_ge(pe_mod_done, len(BY_PE))
            mod_acc = bank[7][:, 0:96].rearrange("p (j s) -> p j s", s=2)
            dve.tensor_tensor(mod_col[:, 0:16], mod_acc[:, 0:16, 0], vec_all[:, V_BMOD:V_BMOD + 16], ALU.add)
            step(dve.tensor_tensor(mod_ctx[:], mod_acc[:, 0:16, 1], vec_all[:, V_BMOD:V_BMOD + 16], ALU.add))
            for i, src in enumerate((mod_col, mod_ctx)):
                ins = dve.scalar_tensor_tensor(out=s1[:, 8 * i:8 * i + 8], in0=src[:, 8:16], scalar=1.0,
                                               in1=vec_all[:, V_NORM:V_NORM + KC], op0=ALU.add, op1=ALU.mult)
            step(ins)

            def h_low(c):
                dve.wait_ge(hhi_done, c + 1)
                if c < KC:
                    ins = dve.tensor_tensor(h_lo[:, c, :], tmp[c % 2], h_hi[:, c, :].bitcast(F32), ALU.subtract)
                else:
                    ins = dve.tensor_tensor(gc_lo[:, c - KC, :], tmp[c % 2][:, 0:CTX],
                                            gc_hi[:, c - KC, :].bitcast(F32), ALU.subtract)
                ins.then_inc(hlo_done, 1)

            for c in range(2 * KC):
                dve.wait_ge(ht_ready, c + 1)
                b = bank[(4, 5, 6)[c % 3]]
                if c >= 2:
                    dve.wait_ge(hlo_done, c - 1)
                if c < KC:
                    ins = dve.tensor_scalar(tmp[c % 2], b[:], s1[:, c:c + 1], mod_col[:, c:c + 1], ALU.mult, ALU.add)
                else:
                    ins = dve.tensor_scalar(tmp[c % 2][:, 0:CTX], b[:, 0:CTX], s1[:, c:c + 1],
                                            mod_ctx[:, c - KC:c - KC + 1], ALU.mult, ALU.add)
                ins.then_inc(tmp_ready, 1)
                if c >= 1:
                    h_low(c - 1)
                if c == KC:
                    low(dve, 0)
                    low(dve, 1)
            h_low(2 * KC - 1)

            def read_tiles(s):
                name = name_of(s)
                for t in range(first_tile[s], first_tile[s + 1]):
                    k = t - first_tile[s]
                    src = bank[t % 4]
                    dve.wait_ge(acc_ready, t + 1)
                    if name == "glu_a":
                        j = (s - 1) // 2
                        dve.wait_ge(read_act, 2 * j + k + 1)
                        if t == first_tile[1]:
                            dve.wait_ge(pad_ready, 1)
                        dve.tensor_tensor(u_pad[:, 2 * j + k, HALF:HALF + SEQ], src[:], sig[k], ALU.mult)\
                           .then_inc(read_dve, 1)
                    elif name == "att":
                        c = 4 * (s - 14) + k
                        dve.wait_ge(read_act, reads_upto("act", first_tile[14]))
                        dve.tensor_tensor(m[:, c, :], m[:, c, :], src[:], ALU.mult).then_inc(read_dve, 1)
                    elif name == "conv":
                        c = 4 * (s - 20) + k
                        dve.wait_ge(read_act, reads_upto("act", first_tile[20]))
                        dve.tensor_tensor(gate_c[:, c, :], gate_c[:, c, :], src[:], ALU.mult).then_inc(read_dve, 1)
                        dve.wait_ge(read_dve, reads_upto("dve", t))
                        dve.tensor_tensor(m[:, c, :], m[:, c, :], gate_c[:, c, :], ALU.add).then_inc(m_done, 1)
                    else:
                        c = 2 * (s - 22) + k
                        dve.wait_ge(xt_used, c + 1)
                        dve.scalar_tensor_tensor(out=x_mid[:, c, :], in0=src[:], scalar=mod_col[:, 16 + c:17 + c],
                                                 in1=m[:, c, :], op0=ALU.mult, op1=ALU.add)\
                           .then_inc(read_dve, 1)

            taps = [(tap, 2 * pair + c) for pair in range(2) for tap in range(TAPS) for c in range(2)]
            TAPS_AFTER = {1: 12, 2: 26, 3: 38, 4: 58, 5: 78, 6: 98, 7: 116, 8: len(taps)}

            def convolve(first, last):
                for n in range(first, last):
                    tap, c = taps[n]
                    if tap == 0:
                        dve.wait_ge(read_dve, 2 if c < 2 else 4)
                        dve.wait_ge(pad_ready, 1)
                    else:
                        dve.wait_ge(tap_done, n - 1)
                    tap_of(dve, tap, c).then_inc(tap_done, 1)

            def low_tiles(s):
                for t in range(first_tile[s], first_tile[s + 1]):
                    k = t - first_tile[s]
                    dve.wait_ge(kv_high, t - first_tile[4] + 1)
                    if name_of(s) == "v" and k == 2:
                        dve.wait_ge(tb_ready, 16)
                    hi, src = kqv_tile(s, k, t, k_hi, kc_hi, q_hi, v_hi)
                    lo, _ = kqv_tile(s, k, t, k_lo, kc_lo, q_lo, v_lo)
                    if name_of(s) == "q":
                        ins = dve.scalar_tensor_tensor(out=lo, in0=src, scalar=HD ** -0.5, in1=hi.bitcast(F32),
                                                       op0=ALU.mult, op1=ALU.subtract)
                    else:
                        ins = dve.tensor_tensor(lo, src, hi.bitcast(F32), ALU.subtract)
                    ins.then_inc(read_dve, 1)

            for s in range(10):
                if s >= 4:
                    low_tiles(s)
                elif READER[name_of(s)] == "dve":
                    read_tiles(s)
                if s < 8 and s + 2 not in POOL_LOWS:
                    low(dve, s + 2)
                if s in TAPS_AFTER:
                    convolve(TAPS_AFTER.get(s - 1, 0), TAPS_AFTER[s])
            dve.wait_ge(tap_done, len(taps))

            def whole_sum(n):
                dve.wait_ge(p_ready, n + 1)
                dve.tensor_tensor(r_loc[:, n:n + 1], r_loc[:, n:n + 1], r_ctx[:, n:n + 1], ALU.add)\
                   .then_inc(r_summed, 1)

            def inverse_sum(n):
                dve.wait_ge(r_summed, n + 1)
                dve.reciprocal(r_loc[:, n:n + 1], r_loc[:, n:n + 1]).then_inc(r_ready, 1)

            def normalise(n):
                dve.wait_ge(r_ready, n + 1)
                dve.tensor_scalar(s_t[n % 2], s_t[n % 2], r_loc[:, n:n + 1], None, ALU.mult).then_inc(normed, 1)

            def turned_low(n):
                for b in range(3):
                    dve.wait_ge(pt_high, 3 * n + b + 1)
                    dve.tensor_tensor(w_lo[n % 2][:, 512 * b:512 * b + 512], bank[3 + b][:],
                                      w_hi[n % 2][:, 512 * b:512 * b + 512].bitcast(F32), ALU.subtract)\
                       .then_inc(pt_low, 1)

            def att_low(n):
                h, half = n // 2, n % 2
                a = 64 * (h % 2)
                dve.wait_ge(athi_done, n + 1)
                dve.tensor_tensor(g_lo[a:a + 64, h // 2, CTX * half:CTX * half + CTX], bank[6][a:a + 64, 0:CTX],
                                  g_hi[a:a + 64, h // 2, CTX * half:CTX * half + CTX].bitcast(F32),
                                  ALU.subtract).then_inc(atlo_done, 1)

            dve.wait_ge(masked, 2)
            for n, (h, i) in enumerate(IT):
                dve.wait_ge(s_ready, n + 1)
                if n >= 2:
                    dve.wait_ge(pt_ready, n - 1)
                a = 6 - 2 * i
                dve.tensor_tensor_reduce(s_t[n % 2][:, 0:512], bank[n % 2][:],
                                         bias[:, h, a:a + 8, :].rearrange("p m c -> p (m c)"), 1.0, -3.0e38,
                                         ALU.add, ALU.max, m_loc[:, n:n + 1]).then_inc(s_used, 1)
                if n >= 1:
                    whole_sum(n - 1)
                dve.wait_ge(sc_ready, n + 1)
                dve.reduce_max(m_ctx[:, n:n + 1], bank[2][:, 0:CTX], axis=AX.X).then_inc(mc_ready, 1)
                if n >= 1:
                    inverse_sum(n - 1)
                dve.wait_ge(s_used, n + 1)
                dve.wait_ge(mc_ready, n + 1)
                dve.tensor_scalar(m_neg[:, n:n + 1], m_loc[:, n:n + 1], m_ctx[:, n:n + 1], -1.0, ALU.max, ALU.mult)\
                   .then_inc(m_ready, 1)
                if n >= 3 and n % 2 == 1:
                    turned_low((n - 3) // 2)
                if n >= 1:
                    normalise(n - 1)
                if n >= 5 and n % 2 == 1:
                    att_low((n - 5) // 2)
            whole_sum(NIT - 1)
            inverse_sum(NIT - 1)
            normalise(NIT - 1)
            turned_low(15)
            att_low(14)
            low(dve, 10)
            att_low(15)
            low(dve, 11)
            dve.wait_ge(part_summed, 24 - len(BY_PE))
            step(dve.tensor_tensor(mod_col[:, 16:48], mod_acc[:, 16:48, 0], vec_all[:, V_BMOD + 16:V_BMOD + 48],
                                   ALU.add))

            def norm_mean():
                dve.wait_ge(mean_ready, 1)
                step(dve.tensor_scalar(mean_t, bank[4][:], 1.0 / 512, None, ALU.mult))
                for c in range(4):
                    dve.tensor_tensor(y_conv[:, c, :], y_conv[:, c, :], mean_t, ALU.subtract).then_inc(cent_ready, 1)

            def norm_var():
                dve.wait_ge(cssq_ready, 1)
                dve.tensor_scalar(rstd, bank[5][:], 1.0 / 512, NORM_EPS, ALU.mult, ALU.add).then_inc(cvar_ready, 1)
                dve.wait_ge(cstd_ready, 1)
                step(dve.reciprocal(rstd, rstd))
                for c in range(4):
                    dve.tensor_tensor(y_conv[:, c, :], y_conv[:, c, :], rstd, ALU.mult).then_inc(cn_ready, 1)

            def conv_low():
                for c in range(4):
                    dve.wait_ge(cvhi_done, c + 1)
                    dve.tensor_tensor(g_lo[:, 4 + c, :], y_conv[:, c, :], g_hi[:, 4 + c, :].bitcast(F32),
                                      ALU.subtract).then_inc(cvlo_done, 1)

            def merged_low(c):
                dve.wait_ge(mhi_done, c + 1)
                dve.tensor_tensor(h_lo[:, c, :], m[:, c, :], h_hi[:, c, :].bitcast(F32), ALU.subtract)\
                   .then_inc(mlo_done, 1)

            for s in range(10, NS):
                if s == 10:
                    norm_mean()
                if READER[name_of(s)] == "dve":
                    read_tiles(s)
                if s == 11:
                    norm_var()
                if s != 21 and s + 2 < NS:
                    low(dve, s + 2)
                if s == 14:
                    conv_low()
                if name_of(s) == "conv":
                    for c in range(4 * (s - 20), 4 * (s - 19)):
                        merged_low(c)
                if s == 21:
                    low(dve, s + 2)
                if s == 21:
                    dve.wait_ge(mlo_done, KC)
                    for c in range(KC):
                        dve.wait_ge(xt_ready, c + 1)
                        dve.tensor_copy(x_mid[:, c, :], bank[4 + c % 4][:]).then_inc(xt_used, 1)

        @block.tensor
        def _(pe):
            pe.wait_ge(ident_ready, 1)
            pe.wait_ge(cond_landed, 32)
            pe.transpose(bank[0][:, 0:16], cond_rows[0:16, :], ident[0:16, 0:16]).then_inc(vt_ready, 1)
            pe.wait_ge(vec_landed, 16 * 14)
            pe.transpose(bank[1][:, 0:NV], vec_rows[0:NV, :], ident[0:NV, 0:NV])
            pe.transpose(bank[2][:, 0:4 * TAPS], conv_rows[0:4 * TAPS, :], ident[0:4 * TAPS, 0:4 * TAPS])
            pe.transpose(bank[3][0:NDC, 0:HEADS * NDR], rpb_rows[0:HEADS * NDR, :],
                         ident[0:HEADS * NDR, 0:HEADS * NDR]).then_inc(vt_ready, 1)

            mod_acc = bank[7][:, 0:96].rearrange("p (j s) -> p j s", s=2)

            def modulation(u):
                if u in BY_PE:
                    pos = place["mod", u]
                    wait_landed(pe, pos)
                    for k in range(2):
                        for c in range(KC):
                            ins = pe.matmul(mod_acc[:, 2 * u + k, :], as_k8(flat(pos))[:, c, 128 * k:128 * k + 128],
                                            c_silu[:, c, :], start=(c == 0), stop=(c == KC - 1))
                    ins.then_inc(pe_mod_done, 1)
                    return
                if u < 8:
                    pe.wait_ge(part_done, 16 * (BY_DVE.index(u) + 1))
                else:
                    pe.wait_ge(pool_part_done, 4 * (u - 7))
                for k in range(2):
                    for c in range(2 if u < 8 else 1):
                        src = part[BY_DVE.index(u) % 2][:, c, :] if u < 8 else late_part[u % 2]
                        ins = pe.matmul(mod_acc[:, 2 * u + k, c:c + 1], src[:, 128 * k:128 * k + 128], ones[:, 0:1],
                                        start=True, stop=True)
                ins.then_inc(part_summed, 1)

            pe.wait_ge(silu_ready, 1)
            for u in range(8):
                modulation(u)

            def turned(c):
                if c >= 3:
                    pe.wait_ge(tmp_ready, c - 2)
                b = bank[(4, 5, 6)[c % 3]]
                nt, rows = (4, x_rows) if c < KC else (2, c_rows)
                cc = c % KC
                for t in range(nt):
                    ins = pe.transpose(b[:, 128 * t:128 * t + 128], rows[:, t, 128 * cc:128 * cc + 128], ident[:])
                ins.then_inc(ht_ready, 1)

            pe.wait_ge(scaled, 6)
            for c in range(2 * KC):
                turned(c)

            def product(out, a_hi, a_lo, b_hi, b_lo, first, last):
                pe.matmul(out, a_hi, b_lo, start=first, stop=False)
                pe.matmul(out, a_lo, b_hi, start=False, stop=False)
                return pe.matmul(out, a_hi, b_hi, start=False, stop=last)

            def features(out, s, k, b_hi, b_lo, n, merged=False):
                hi, lo = as_k8(w_hi[s % 2]), as_k8(w_lo[s % 2])
                for c in range(KC):
                    if merged:
                        pe.wait_ge(mlo_done, c + 1)
                    ins = product(out, hi[:, c, 128 * k:128 * k + 128], lo[:, c, 128 * k:128 * k + 128],
                                  b_hi[:, c, 0:n], b_lo[:, c, 0:n], c == 0, c == KC - 1)
                return ins

            def positions(out, s, b_hi, b_lo, t):
                hi, lo = as_k8(w_hi[s % 2]), as_k8(w_lo[s % 2])
                for c in range(KC):
                    ins = product(out, b_hi[:, c, 128 * t:128 * t + 128], b_lo[:, c, 128 * t:128 * t + 128],
                                  hi[:, c, :], lo[:, c, :], c == 0, c == KC - 1)
                return ins

            def half_features(out, s, k, at):
                hi, lo = as_k4(w_hi[s % 2]), as_k4(w_lo[s % 2])
                for c in range(4):
                    ins = product(out, hi[:, c, 128 * k:128 * k + 128], lo[:, c, 128 * k:128 * k + 128],
                                  g_hi[:, at + c, :], g_lo[:, at + c, :], c == 0, c == 3)
                return ins

            def unit(s):
                name = name_of(s)
                wait_low(pe, s)
                if s == 0:
                    pe.wait_ge(hlo_done, KC)
                if s == 4:
                    pe.wait_ge(hlo_done, 2 * KC)
                if s == 14:
                    pe.wait_ge(atlo_done, 16)
                if s == 20:
                    pe.wait_ge(cvlo_done, 4)
                for t in range(first_tile[s], first_tile[s + 1]):
                    k = t - first_tile[s]
                    if t >= 4:
                        engine = READER[name_of(TILES[t - 4][0])]
                        pe.wait_ge(read_act if engine == "act" else read_dve, reads_upto(engine, t - 4))
                    dst = bank[t % 4]
                    if name == "k" and k == 2:
                        features(dst[:, 0:256], s, 0, gc_hi, gc_lo, CTX)
                        ins = features(dst[:, 256:512], s, 1, gc_hi, gc_lo, CTX)
                    elif name == "v":
                        b_hi, b_lo, t0 = (h_hi, h_lo, 2 * k) if k < 2 else (gc_hi, gc_lo, 0)
                        positions(dst[:, 0:256], s, b_hi, b_lo, t0)
                        ins = positions(dst[:, 256:512], s, b_hi, b_lo, t0 + 1)
                    elif name in ("att", "conv"):
                        ins = half_features(dst[:], s, k, 0 if name == "att" else 4)
                    else:
                        ins = features(dst[:], s, k, h_hi, h_lo, SEQ, merged=(s == 22 and k == 0))
                    ins.then_inc(acc_ready, 1)

            def table_part(b):
                if b == 0:
                    pe.wait_ge(onehot_ready, 1)
                    pe.wait_ge(tmp_ready, 2 * KC)
                if b >= 3:
                    pe.wait_ge(tb_used, b - 2)
                for q in range(4):
                    ck = 4 * b + q
                    ins = pe.matmul(bank[(4, 5, 6)[b % 3]][:, 120 * q:120 * q + 120],
                                    onehot[0:NDC, GRID - 1 - ck:GRID - 1 - ck + 128], rpb_t[0:NDC, 0:120],
                                    start=True, stop=True)
                ins.then_inc(tb_ready, 1)

            for s in range(10):
                if 2 <= s < 6:
                    for b in range(4 * (s - 2), 4 * (s - 1)):
                        table_part(b)
                unit(s)
            pe.wait_ge(read_dve, reads_upto("dve", first_tile[10] - 1))

            def scores(n):
                h, i = IT[n]
                if n >= 2:
                    pe.wait_ge(s_used, n - 1)
                a, c, q = 64 * (h % 2), h // 2, 128 * i
                product(bank[n % 2][:], q_hi[a:a + 64, c, q:q + 128], q_lo[a:a + 64, c, q:q + 128],
                        k_hi[a:a + 64, c, :], k_lo[a:a + 64, c, :], True, True).then_inc(s_ready, 1)

            def context_scores(n):
                h, i = IT[n]
                if n:
                    pe.wait_ge(p_ready, n)
                a, c, q = 64 * (h % 2), h // 2, 128 * i
                product(bank[2][:, 0:CTX], q_hi[a:a + 64, c, q:q + 128], q_lo[a:a + 64, c, q:q + 128],
                        kc_hi[a:a + 64, c, :], kc_lo[a:a + 64, c, :], True, True).then_inc(sc_ready, 1)

            def turn(n):
                pe.wait_ge(normed, n + 1)
                for j in range(6):
                    if n % 2 == 0 and n >= 2 and j % 2 == 0:
                        pe.wait_ge(pt_low, 3 * (n // 2 - 1) + j // 2 + 1)
                    ins = pe.transpose(bank[3 + j // 2][:, 256 * (j % 2) + 128 * (n % 2):256 * (j % 2) + 128 * (n % 2) + 128],
                                       s_t[n % 2][:, 128 * j:128 * j + 128], ident[:])
                ins.then_inc(pt_ready, 1)

            def values(n):
                h = n // 2
                pe.wait_ge(pt_low, 3 * n + 3)
                if n:
                    pe.wait_ge(atlo_done, n)
                for j in range(6):
                    ins = product(bank[6][:, 0:CTX], v_hi[:, j, 128 * (h // 2):128 * (h // 2) + 128],
                                  v_lo[:, j, 128 * (h // 2):128 * (h // 2) + 128],
                                  w_hi[n % 2][:, CTX * j:CTX * j + CTX], w_lo[n % 2][:, CTX * j:CTX * j + CTX],
                                  j == 0, j == 5)
                ins.then_inc(o_ready, 1)

            scores(0)
            context_scores(0)
            for n in range(NIT):
                if n + 1 < NIT:
                    scores(n + 1)
                if n >= 1:
                    turn(n - 1)
                if n + 1 < NIT:
                    context_scores(n + 1)
                if n % 2 == 0 and n >= 4:
                    values(n // 2 - 2)
                if n % 2 == 1:
                    modulation(8 + n // 2)
            turn(NIT - 1)
            values(14)
            values(15)
            for c in range(4):
                ins = pe.matmul(bank[4][:], ones[:], y_conv[:, c, :], start=(c == 0), stop=(c == 3))
            ins.then_inc(mean_ready, 1)
            for s in range(10, NS):
                if s == 22:
                    pe.wait_ge(again_landed, 16)
                    for c in range(KC):
                        if c >= 4:
                            pe.wait_ge(xt_used, c - 3)
                        for t in range(TC):
                            ins = pe.transpose(bank[4 + c % 4][:, 128 * t:128 * t + 128],
                                               x_rows[:, t, 128 * c:128 * c + 128], ident[:])
                        ins.then_inc(xt_ready, 1)
                unit(s)
                if s == 10:
                    for c in range(4):
                        pe.wait_ge(sq_ready, c + 1)
                        ins = pe.matmul(bank[5][:], ones[:], sq[:, c, :], start=(c == 0), stop=(c == 3))
                    ins.then_inc(cssq_ready, 1)
    return used


def moe_stage(nc, cst, x_mid, mod_col, vec, w, dram):
    used = []
    with ExitStack() as ctx:
        def sb(name, shape, dt=F32):
            return ctx.enter_context(nc.sbuf_tensor("moe_" + name, shape, dt))

        def sem(name):
            used.append(ctx.enter_context(nc.semaphore("moe_" + name)))
            return used[-1]

        bank = [ctx.enter_context(nc.psum_tensor(f"moe_bank{i}", [P, 512], F32)) for i in range(8)]
        ident, ones = cst["ident"], cst["ones"]
        gates = cst["gates"]

        raw = [sb(f"expert_raw{i}", [P, 4, 512]) for i in range(RAW)]
        w_hi = [sb(f"expert_hi{i}", [P, 4, 512], F32R) for i in range(SPLIT)]
        w_lo = [sb(f"expert_lo{i}", [P, 4, 512], F32R) for i in range(SPLIT)]
        pool0 = sb("moe_tiles", [P, 8192])
        x_rows = [pool0[:, 1024 * i:1024 * (i + 1)] for i in range(2)]
        silu_g = [pool0[:, 2048 + 512 * i:2560 + 512 * i] for i in range(2)]
        act = [pool0[:, 3072 + 512 * i:3584 + 512 * i] for i in range(2)]
        y_rows = [pool0[:, 4096 + 1024 * i:5120 + 1024 * i] for i in range(2)]
        h2 = pool0[:, 0:4096].rearrange("p (c t) -> p c t", c=KC)
        sq = pool0[:, 4096:8192].rearrange("p (c t) -> p c t", c=KC)
        h2_rows = pool0[:, 4096:8192].rearrange("p (t d) -> p t d", t=TC)
        x_hi = [sb(f"x_hi{i}", [P, KC, 128], F32R) for i in range(2)]
        x_lo = [sb(f"x_lo{i}", [P, KC, 128], F32R) for i in range(2)]
        a_hi = [sb(f"a_hi{i}", [P, 4, 128], F32R) for i in range(2)]
        a_lo = [sb(f"a_lo{i}", [P, 4, 128], F32R) for i in range(2)]

        rstd = sb("moe_rstd", [P, SEQ])
        s2 = sb("s2", [P, KC])
        w_router = sb("w_router", [P, KC, 36])
        b_router = sb("b_router", [P, 36])
        logits = sb("logits", [P, TC, 36])
        group8 = sb("group8", [P, TC, 8])
        gmax = sb("gmax", [P, TC, 8])
        gidx = sb("gidx", [P, TC, 8], U32)
        gidx_f = sb("gidx_f", [P, TC])
        gexp = sb("gexp", [P, TC, 4])
        p_group = sb("p_group", [P, TC])
        g_one = sb("g_one", [P, TC, 4])
        e_sel = sb("e_sel", [P, TC, 8])
        e_part = sb("e_part", [P, TC, 8])
        emax = sb("emax", [P, TC, 8])
        eidx = sb("eidx", [P, TC, 8], U32)
        eidx_f = sb("eidx_f", [P, TC, 2])
        e2 = sb("e2", [P, TC])
        den = sb("den", [P, TC])
        flat_e = sb("flat_e", [P, TC, 2])
        chosen = sb("chosen", [P, 8, 32])
        totals = sb("totals", [P, 8, 32])
        before = sb("before", [P, 8, 32])
        prod = sb("prod", [P, 8, 32])
        rank = sb("rank", [P, 8])
        counts = sb("counts", [P, 32])
        n_blk = sb("n_blk", [P, 32])
        end_blk = sb("end_blk", [P, 32])
        first_blk = sb("first_blk", [P, 32])
        fl = sb("fl", [P, 8])
        slot = sb("slot", [P, 8])
        blk = sb("blk", [P, 8])
        ident1 = sb("ident1", [P, 8])
        slot_one = sb("slot_one", [P, 8, 128])
        blk_one = sb("blk_one", [P, 8, NBX])
        list_f = sb("list_f", [P, NBX])
        empty = sb("empty", [P, NBX])
        row_f = sb("row_f", [P, NBX])
        tok_f = sb("tok_f", [P, NBX])
        row_i = sb("row_i", [P, NBX], I32)
        tok_i = sb("tok_i", [P, NBX], I32)
        le = sb("le", [1, NBX, 32])
        exp_f = sb("exp_f", [1, NBX])
        exp_i = sb("exp_i", [1, NBX], I32)
        pairs_f = sb("pairs_f", [1, 1])
        pairs_i = sb("pairs_i", [1, 1], I32)
        iota_row = sb("iota_row", [P, 128])
        iota_p = sb("iota_p", [P, 8])
        tri = sb("tri", [P, 128])
        tok_col = [sb(f"tok_col{i}", [P, 1], I32) for i in range(2)]
        row_col = [sb(f"row_col{i}", [P, 1], I32) for i in range(2)]

        router_landed = sem("router_landed")
        tables_ready = sem("tables_ready")
        index_ready = sem("index_ready")
        pool_step = sem("pool_step")
        dve_step = sem("moe_dve_step")
        sq_ready = sem("sq_ready")
        ssq_ready = sem("ssq_ready")
        var_ready = sem("var_ready")
        std_ready = sem("std_ready")
        h2_ready = sem("h2_ready")
        h2t_ready = sem("h2t_ready")
        h2t_evac = sem("h2t_evac")
        hn_ready = sem("hn_ready")
        pair_ready = sem("pair_ready")
        experts_done = sem("experts_done")
        h2_stored = sem("h2_stored")
        logits_ready = sem("logits_ready")
        gd_ready = sem("gd_ready")
        gexp_ready = sem("gexp_ready")
        ed_ready = sem("ed_ready")
        eexp_ready = sem("eexp_ready")
        chosen_ready = sem("chosen_ready")
        ranks_ready = sem("ranks_ready")
        ones_ready = sem("ones_ready")
        list_ready = sem("list_ready")
        lists_done = sem("lists_done")
        raw_landed = [sem(f"expert_landed{i}") for i in range(RAW)]
        hi_done = sem("expert_hi_done")
        lo_done = sem("expert_lo_done")
        unit_used = sem("expert_unit_used")
        gathered = [sem(f"gathered{i}") for i in range(2)]
        xt_ready = sem("xt_ready")
        xhi_done = sem("xhi_done")
        xlo_done = sem("xlo_done")
        silu_done = sem("silu_done")
        act_done = sem("act_done")
        at_ready = sem("at_ready")
        ahi_done = sem("ahi_done")
        alo_done = sem("alo_done")
        y_s = sem("y_s")
        y_v = sem("y_v")
        scattered = [sem(f"scattered{i}") for i in range(2)]

        wg = w["w_exp_gate"][0].rearrange("e (h k p) f -> e h p k f", p=P, k=4)
        wu = w["w_exp_up"][0].rearrange("e (h k p) f -> e h p k f", p=P, k=4)
        wd = w["w_exp_down"][0].rearrange("e (k p) (h f) -> e h p k f", p=P, f=512)

        def unit(i, s, j):
            return 4 + 12 * i + 6 * s + j

        def unit_slot(s, j):
            return (4 + 6 * s + j) % RAW, (4 + 6 * s + j) % SPLIT

        def unit_landed(i, s, j):
            return 16 * (12 // RAW * i + (4 + 6 * s + j) // RAW + 1)

        block = ctx.enter_context(nc.Block())

        @block.sync
        def _(sp):
            with nc.allow_non_contiguous_dma(reason="router columns"):
                sp.dma_start(w_router[:, :, 0:4],
                             w["w_router_group"][0].rearrange("(k p) g -> p k g", p=P)).then_inc(router_landed, 16)
                sp.dma_start(w_router[:, :, 4:36],
                             w["w_router_expert"][0].rearrange("(k p) g -> p k g", p=P)).then_inc(router_landed, 16)
                sp.dma_start(b_router[:, 0:4], w["b_router_group"].to_broadcast([P, 4])).then_inc(router_landed, 16)
                sp.dma_start(b_router[:, 4:36], w["b_router_expert"].to_broadcast([P, 32])).then_inc(router_landed, 16)
            for t in range(TC):
                sp.wait_ge(h2t_evac, 2 * t + 2)
                sp.dma_start(dram["h2"][t * 128:(t + 1) * 128, :], h2_rows[:, t, :]).then_inc(h2_stored, 16)
            sp.wait_ge(experts_done, 1)
            pairs = sp.value_load(pairs_i[0:1, 0:1], min_val=1, max_val=NB_MAX // 2)
            first = sp.value_load(exp_i[0:1, 0:1], min_val=0, max_val=31)
            for n, src in enumerate((wg, wg, wu, wu)):
                sp.dma_start(raw[n][:], src[bass.ds(first, 1), n % 2]).then_inc(raw_landed[n], 16)
            with sp.Fori(0, pairs) as i:
                for s in range(2):
                    here = sp.value_load(exp_i[0:1, bass.ds(2 * i + s, 1)], min_val=0, max_val=31)
                    after = sp.value_load(exp_i[0:1, bass.ds(2 * i + s + 1, 1)], min_val=0, max_val=31)
                    for j, (src, e) in enumerate(((wg, after), (wd, here), (wu, after))):
                        for h in range(2):
                            r, _ = unit_slot(s, 2 * j + h)
                            sp.wait_ge(lo_done, unit(i, s, 2 * j + h) + 1)
                            sp.dma_start(raw[r][:], src[bass.ds(e, 1), h]).then_inc(raw_landed[r], 16)

        @block.gpsimd
        def _(pool):
            n = [0]

            def step(ins):
                n[0] += 1
                ins.then_inc(pool_step, 1)
                pool.wait_ge(pool_step, n[0])

            step(pool.iota(iota_row[:], pattern=[[1, 128]], base=0, channel_multiplier=0,
                           allow_small_or_imprecise_dtypes=True))
            step(pool.iota(iota_p[:].rearrange("p (t k) -> p t k", k=2), pattern=[[128, TC], [SEQ, 2]], base=1,
                           channel_multiplier=1, allow_small_or_imprecise_dtypes=True))
            step(pool.memset(tri[:], 1.0))
            step(pool.affine_select(out=tri[:], in_=tri[:], compare_op=ALU.is_gt, fill=0.0, base=0,
                                    pattern=[[1, 128]], channel_multiplier=-1))
            pool.memset(group8[:], -3.0e38).then_inc(tables_ready, 1)
            pool.wait_ge(h2t_ready, 2 * TC)
            for s in range(2):
                step(pool.memset(x_rows[s], 0.0))
            pool.wait_ge(lists_done, 1)
            pool.wait_ge(h2_stored, 16 * TC)
            pairs = pool.value_load(pairs_i[0:1, 0:1], min_val=1, max_val=NB_MAX // 2)

            last_token, last_row = pool.to_reg(SEQ - 1), pool.to_reg(2 * SEQ - 1)

            def gather_rows(s):
                pool.indirect_dma_start(out=x_rows[s], out_offset=None, in_=dram["h2"][:, :],
                                        in_offset=bass.IndirectOffsetOnAxis(ap=tok_col[s][:, 0:1], axis=0),
                                        bounds_check=last_token, oob_is_err=False).then_inc(gathered[s], 16)

            for s in range(2):
                pool.dma_start(dram["mark"][s], iota_row[0:1, :]).then_inc(scattered[s], 16)
            for first in range(3):
                if first == 2:
                    pool.wait_ge(xt_ready, 1)
                step(pool.tensor_copy(tok_col[first % 2][:], tok_i[:, first:first + 1]))
                gather_rows(first % 2)
            with pool.Fori(0, pairs) as i:
                for s in range(2):
                    pool.wait_ge(xt_ready, 2 * i + s + 2)
                    pool.tensor_copy(tok_col[1 - s][:], tok_i[:, bass.ds(2 * i + s + 3, 1)]).then_inc(pool_step, 1)
                    pool.wait_ge(pool_step, n[0] + 4 * i + 2 * s + 1)
                    pool.sem_inc(index_ready, 1)
                    gather_rows(1 - s)
                    pool.wait_ge(y_s, 2 * i + s + 2)
                    pool.wait_ge(y_v, 2 * i + s + 2)
                    pool.tensor_copy(row_col[s][:], row_i[:, bass.ds(2 * i + s, 1)]).then_inc(pool_step, 1)
                    pool.wait_ge(pool_step, n[0] + 4 * i + 2 * s + 2)
                    pool.sem_inc(index_ready, 1)
                    pool.indirect_dma_start(out=dram["y"][:, :],
                                            out_offset=bass.IndirectOffsetOnAxis(ap=row_col[s][:, 0:1], axis=0),
                                            in_=y_rows[s], in_offset=None,
                                            bounds_check=last_row, oob_is_err=False).then_inc(scattered[s], 16)
            for s in range(2):
                pool.wait_ge(scattered[s], 16 * pairs + 16)
            pool.wait_ge(gathered[0], 16 * pairs + 32)
            pool.wait_ge(gathered[1], 16 * pairs + 16)

        @block.scalar
        def _(act_e):
            for c in range(KC):
                act_e.activation(sq[:, c, :], x_mid[:, c, :], ACT.Square).then_inc(sq_ready, 1)
            act_e.wait_ge(var_ready, 1)
            act_e.activation(rstd[:], rstd[:], ACT.Sqrt).then_inc(std_ready, 1)
            for c in range(KC):
                act_e.wait_ge(hn_ready, c + 1)
                act_e.activation(h2[:, c, :], h2[:, c, :], ACT.Identity, scale=s2[:, c:c + 1],
                                 bias=mod_col[:, 24 + c:25 + c]).then_inc(h2_ready, 1)
            for t in range(TC):
                for half in range(2):
                    act_e.wait_ge(h2t_ready, 2 * t + half + 1)
                    act_e.activation(h2_rows[:, t, 512 * half:512 * half + 512], bank[4 + (2 * t + half) % 4][:],
                                     ACT.Copy).then_inc(h2t_evac, 1)
            act_e.wait_ge(gd_ready, 1)
            act_e.activation(gexp[:], gexp[:], ACT.Exp).then_inc(gexp_ready, 1)
            act_e.wait_ge(ed_ready, 1)
            act_e.activation(e2[:], e2[:], ACT.Exp).then_inc(eexp_ready, 1)
            act_e.wait_ge(lists_done, 1)
            act_e.sem_inc(y_s, 1)
            pairs = act_e.value_load(pairs_i[0:1, 0:1], min_val=1, max_val=NB_MAX // 2)

            def split_hi(i, s, j):
                r, q = unit_slot(s, j)
                act_e.wait_ge(raw_landed[r], unit_landed(i, s, j))
                act_e.wait_ge(unit_used, unit(i, s, j) + 1)
                act_e.activation(w_hi[q][:], raw[r][:], ACT.Copy).then_inc(hi_done, 1)

            def x_high(s, b):
                act_e.wait_ge(xt_ready, b + 1)
                act_e.activation(x_hi[s][:, 0:4, :], bank[0][:], ACT.Copy)
                act_e.activation(x_hi[s][:, 4:8, :], bank[1][:], ACT.Copy).then_inc(xhi_done, 1)

            def first_hi(n):
                act_e.wait_ge(raw_landed[n], 16)
                act_e.wait_ge(unit_used, n + 1)
                act_e.activation(w_hi[n][:], raw[n][:], ACT.Copy).then_inc(hi_done, 1)

            x_high(0, 0)
            first_hi(0)
            first_hi(1)
            x_high(1, 1)
            first_hi(2)
            first_hi(3)
            with act_e.Fori(0, pairs) as i:
                for s in range(2):
                    b = 2 * i + s
                    act_e.wait_ge(unit_used, SPLIT + unit(i, s, 0) - 2)
                    act_e.wait_ge(act_done, b + 1)
                    act_e.activation(silu_g[s], bank[2 + s][:], ACT.Silu).then_inc(silu_done, 1)
                    split_hi(i, s, 0)
                    split_hi(i, s, 1)
                    split_hi(i, s, 2)
                    act_e.wait_ge(at_ready, b + 1)
                    act_e.activation(a_hi[s][:], bank[5][:], ACT.Copy).then_inc(ahi_done, 1)
                    x_high(s, b + 2)
                    split_hi(i, s, 3)
                    split_hi(i, s, 4)
                    split_hi(i, s, 5)
                    act_e.wait_ge(unit_used, SPLIT + unit(i, s, 2) + 1)
                    act_e.wait_ge(scattered[s], 16 * i + 16)
                    act_e.activation(y_rows[s][:, 0:512], bank[6][:], ACT.Copy).then_inc(y_s, 1)

        @block.vector
        def _(dve):
            n = [0]

            def step(ins):
                n[0] += 1
                ins.then_inc(dve_step, 1)
                dve.wait_ge(dve_step, n[0])

            for p in range(4):
                dve.wait_ge(sq_ready, 2 * p + 2)
                dve.tensor_tensor(sq[:, 2 * p, :], sq[:, 2 * p, :], sq[:, 2 * p + 1, :], ALU.add)\
                   .then_inc(pair_ready, 1)
            dve.wait_ge(ssq_ready, 1)
            dve.tensor_scalar(rstd[:], bank[0][:], 1.0 / D, NORM_EPS, ALU.mult, ALU.add).then_inc(var_ready, 1)
            step(dve.scalar_tensor_tensor(out=s2[:], in0=mod_col[:, 32:40], scalar=1.0,
                                          in1=vec["norm_ffn"], op0=ALU.add, op1=ALU.mult))
            dve.wait_ge(std_ready, 1)
            step(dve.reciprocal(rstd[:], rstd[:]))
            for c in range(KC):
                dve.tensor_tensor(h2[:, c, :], x_mid[:, c, :], rstd[:], ALU.mult).then_inc(hn_ready, 1)
            dve.wait_ge(logits_ready, 1)
            dve.wait_ge(router_landed, 64)
            dve.wait_ge(tables_ready, 1)
            step(dve.tensor_tensor(logits[:], bank[0][:, 0:TC * 36].rearrange("p (t e) -> p t e", t=TC),
                                   b_router[:].unsqueeze(1).to_broadcast([P, TC, 36]), ALU.add))
            step(dve.tensor_copy(group8[:, :, 0:4], logits[:, :, 0:4]))
            for t in range(TC):
                step(dve.max(gmax[:, t, :], group8[:, t, :]))
                step(dve.max_index(gidx[:, t, :], gmax[:, t, :], group8[:, t, :]))
            dve.tensor_tensor(gexp[:], logits[:, :, 0:4], gmax[:, :, 0:1].to_broadcast([P, TC, 4]),
                              ALU.subtract).then_inc(gd_ready, 1)
            step(dve.tensor_copy(gidx_f[:], gidx[:, :, 0:1].rearrange("p t o -> p (t o)")))
            step(dve.tensor_tensor(g_one[:], iota_row[:, 0:4].unsqueeze(1).to_broadcast([P, TC, 4]),
                                   gidx_f[:].unsqueeze(2).to_broadcast([P, TC, 4]), ALU.is_equal))
            for g in range(4):
                dst = e_sel if g == 0 else e_part
                step(dve.tensor_tensor(dst[:], logits[:, :, 4 + 8 * g:12 + 8 * g],
                                       g_one[:, :, g:g + 1].to_broadcast([P, TC, 8]), ALU.mult))
                if g:
                    step(dve.tensor_tensor(e_sel[:], e_sel[:], e_part[:], ALU.add))
            for t in range(TC):
                step(dve.max(emax[:, t, :], e_sel[:, t, :]))
                step(dve.max_index(eidx[:, t, :], emax[:, t, :], e_sel[:, t, :]))
            dve.tensor_tensor(e2[:], emax[:, :, 1:2].rearrange("p t o -> p (t o)"),
                              emax[:, :, 0:1].rearrange("p t o -> p (t o)"), ALU.subtract).then_inc(ed_ready, 1)
            step(dve.tensor_copy(eidx_f[:], eidx[:, :, 0:2]))
            step(dve.scalar_tensor_tensor(out=flat_e[:], in0=gidx_f[:].unsqueeze(2).to_broadcast([P, TC, 2]),
                                          scalar=8.0, in1=eidx_f[:], op0=ALU.mult, op1=ALU.add))
            dve.tensor_tensor(chosen[:], iota_row[:, 0:32].unsqueeze(1).to_broadcast([P, 8, 32]),
                              flat_e[:].rearrange("p t k -> p (t k)").unsqueeze(2).to_broadcast([P, 8, 32]),
                              ALU.is_equal).then_inc(chosen_ready, 1)
            dve.wait_ge(gexp_ready, 1)
            step(dve.tensor_reduce(p_group[:], gexp[:], AX.X, ALU.add))
            step(dve.reciprocal(p_group[:], p_group[:]))
            dve.wait_ge(eexp_ready, 1)
            step(dve.tensor_scalar(den[:], e2[:], 1.0, None, ALU.add))
            step(dve.reciprocal(den[:], den[:]))
            step(dve.tensor_tensor(gates[:, :, 0], den[:], p_group[:], ALU.mult))
            step(dve.tensor_tensor(gates[:, :, 1], gates[:, :, 0], e2[:], ALU.mult))
            dve.wait_ge(ranks_ready, 1)
            step(dve.tensor_copy(totals[:], bank[2][:, 0:256]))
            step(dve.memset(before[:, 0, :], 0.0))
            for g in range(1, 8):
                step(dve.tensor_tensor(before[:, g, :], before[:, g - 1, :], totals[:, g - 1, :], ALU.add))
            step(dve.tensor_tensor(counts[:], before[:, 7, :], totals[:, 7, :], ALU.add))
            step(dve.tensor_tensor(before[:], bank[1][:, 0:256].rearrange("p (g e) -> p g e", g=8), before[:],
                                   ALU.add))
            step(dve.tensor_tensor(prod[:], before[:], chosen[:], ALU.mult))
            step(dve.tensor_reduce(rank[:], prod[:], AX.X, ALU.add))
            step(dve.tensor_scalar(n_blk[:], counts[:], 0.0, None, ALU.is_gt))
            for j in range(1, TC):
                step(dve.scalar_tensor_tensor(out=n_blk[:], in0=counts[:], scalar=128.0 * j, in1=n_blk[:],
                                              op0=ALU.is_gt, op1=ALU.add))
            step(dve.tensor_tensor_scan(end_blk[:], ones[:, 0:32], n_blk[:], 0.0, ALU.mult, ALU.add))
            step(dve.tensor_tensor(first_blk[:], end_blk[:], n_blk[:], ALU.subtract))
            step(dve.tensor_scalar(fl[:], rank[:], 128.0, None, ALU.is_ge))
            for j in range(2, TC):
                step(dve.scalar_tensor_tensor(out=fl[:], in0=rank[:], scalar=128.0 * j, in1=fl[:],
                                              op0=ALU.is_ge, op1=ALU.add))
            step(dve.scalar_tensor_tensor(out=slot[:], in0=fl[:], scalar=-128.0, in1=rank[:], op0=ALU.mult,
                                          op1=ALU.add))
            step(dve.tensor_tensor(prod[:], chosen[:], first_blk[:].unsqueeze(1).to_broadcast([P, 8, 32]),
                                   ALU.mult))
            step(dve.tensor_reduce(blk[:], prod[:], AX.X, ALU.add))
            step(dve.tensor_tensor(blk[:], blk[:], fl[:], ALU.add))
            for g in range(8):
                dve.tensor_scalar(slot_one[:, g, :], iota_row[:], slot[:, g:g + 1], None, ALU.is_equal)
                ins = dve.tensor_scalar(blk_one[:, g, :], iota_row[:, 0:NBX], blk[:, g:g + 1],
                                        iota_p[:, g:g + 1], ALU.is_equal, ALU.mult)
            ins.then_inc(ones_ready, 1)
            step(dve.tensor_tensor(le[:], end_blk[0:1, :].unsqueeze(1).to_broadcast([1, NBX, 32]),
                                   iota_row[0:1, 0:NBX].unsqueeze(2).to_broadcast([1, NBX, 32]), ALU.is_le))
            step(dve.tensor_reduce(exp_f[:], le[:], AX.X, ALU.add))
            step(dve.tensor_scalar(exp_i[:], exp_f[:], float(N_EXPERTS - 1), None, ALU.min))
            step(dve.tensor_scalar(pairs_f[:], end_blk[0:1, 31:32], 0.5, 0.25, ALU.mult, ALU.add))
            dve.tensor_copy(pairs_i[:], pairs_f[:]).then_inc(experts_done, 1)
            dve.wait_ge(experts_done, 1)
            dve.wait_ge(list_ready, 1)
            step(dve.tensor_copy(list_f[:], bank[3][:, 0:NBX]))
            step(dve.tensor_scalar(empty[:], list_f[:], 0.0, 65536.0, ALU.is_equal, ALU.mult))
            step(dve.scalar_tensor_tensor(out=row_f[:], in0=list_f[:], scalar=-1.0, in1=empty[:],
                                          op0=ALU.add, op1=ALU.add))
            step(dve.tensor_scalar(tok_f[:], row_f[:], float(SEQ), -float(SEQ), ALU.is_ge, ALU.mult))
            step(dve.tensor_tensor(tok_f[:], row_f[:], tok_f[:], ALU.add))
            step(dve.tensor_copy(row_i[:], row_f[:]))
            dve.tensor_copy(tok_i[:], tok_f[:]).then_inc(lists_done, 1)
            dve.sem_inc(act_done, 2)
            dve.sem_inc(lo_done, RAW)
            dve.sem_inc(y_v, 1)
            pairs = dve.value_load(pairs_i[0:1, 0:1], min_val=1, max_val=NB_MAX // 2)

            def split_lo(i, s, j):
                r, q = unit_slot(s, j)
                dve.wait_ge(hi_done, unit(i, s, j) + 1)
                dve.tensor_tensor(w_lo[q][:], raw[r][:], w_hi[q][:].bitcast(F32), ALU.subtract)\
                   .then_inc(lo_done, 1)

            def x_low(s, b):
                dve.wait_ge(xhi_done, b + 1)
                dve.tensor_tensor(x_lo[s][:, 0:4, :], bank[0][:].rearrange("p (c t) -> p c t", c=4),
                                  x_hi[s][:, 0:4, :].bitcast(F32), ALU.subtract)
                dve.tensor_tensor(x_lo[s][:, 4:8, :], bank[1][:].rearrange("p (c t) -> p c t", c=4),
                                  x_hi[s][:, 4:8, :].bitcast(F32), ALU.subtract).then_inc(xlo_done, 1)

            def first_lo(n):
                dve.wait_ge(hi_done, n + 1)
                dve.tensor_tensor(w_lo[n][:], raw[n][:], w_hi[n][:].bitcast(F32), ALU.subtract)\
                   .then_inc(lo_done, 1)

            x_low(0, 0)
            first_lo(0)
            first_lo(1)
            x_low(1, 1)
            first_lo(2)
            first_lo(3)
            with dve.Fori(0, pairs) as i:
                for s in range(2):
                    b = 2 * i + s
                    split_lo(i, s, 0)
                    split_lo(i, s, 1)
                    dve.wait_ge(silu_done, b + 1)
                    dve.wait_ge(unit_used, SPLIT + unit(i, s, 0))
                    dve.tensor_tensor(act[s], bank[4][:], silu_g[s], ALU.mult).then_inc(act_done, 1)
                    split_lo(i, s, 2)
                    dve.wait_ge(ahi_done, b + 1)
                    dve.tensor_tensor(a_lo[s][:], bank[5][:].rearrange("p (c t) -> p c t", c=4),
                                      a_hi[s][:].bitcast(F32), ALU.subtract).then_inc(alo_done, 1)
                    x_low(s, b + 2)
                    split_lo(i, s, 3)
                    split_lo(i, s, 4)
                    split_lo(i, s, 5)
                    dve.wait_ge(unit_used, SPLIT + unit(i, s, 3) + 1)
                    dve.wait_ge(scattered[s], 16 * i + 16)
                    dve.tensor_copy(y_rows[s][:, 512:1024], bank[7][:]).then_inc(y_v, 1)

        @block.tensor
        def _(pe):
            for p in range(4):
                pe.wait_ge(pair_ready, p + 1)
                ins = pe.matmul(bank[0][:], ones[:], sq[:, 2 * p, :], start=(p == 0), stop=(p == 3))
            ins.then_inc(ssq_ready, 1)
            pe.wait_ge(h2_ready, KC)
            pe.wait_ge(router_landed, 64)
            for t in range(TC):
                for c in range(KC):
                    ins = pe.matmul(bank[0][:, 36 * t:36 * t + 36], h2[:, c, 128 * t:128 * t + 128],
                                    w_router[:, c, :], start=(c == 0), stop=(c == KC - 1))
            ins.then_inc(logits_ready, 1)
            for n in range(2 * TC):
                t, half = n // 2, n % 2
                if n >= 4:
                    pe.wait_ge(h2t_evac, n - 3)
                for c in range(4):
                    ins = pe.transpose(bank[4 + n % 4][:, 128 * c:128 * c + 128],
                                       h2[:, 4 * half + c, 128 * t:128 * t + 128], ident[:])
                ins.then_inc(h2t_ready, 1)
            pe.wait_ge(chosen_ready, 1)
            pe.wait_ge(tables_ready, 1)
            pe.matmul(bank[1][:, 0:256], tri[:], chosen[:].rearrange("p g e -> p (g e)"), start=True, stop=True)
            pe.matmul(bank[2][:, 0:256], ones[:], chosen[:].rearrange("p g e -> p (g e)"), start=True,
                      stop=True).then_inc(ranks_ready, 1)
            pe.wait_ge(ones_ready, 1)
            for g in range(8):
                ins = pe.matmul(bank[3][:, 0:NBX], slot_one[:, g, :], blk_one[:, g, :], start=(g == 0),
                                stop=(g == 7))
            ins.then_inc(list_ready, 1)
            pe.wait_ge(h2t_evac, 2 * TC)
            pe.wait_ge(lists_done, 1)
            pe.sem_inc(unit_used, SPLIT)
            pairs = pe.value_load(pairs_i[0:1, 0:1], min_val=1, max_val=NB_MAX // 2)

            def gate_like(out, s, q, h):
                for k in range(4):
                    c = 4 * h + k
                    pe.matmul(out, x_hi[s][:, c, :], w_lo[q][:, k, :], start=(h == 0 and k == 0), stop=False)
                    pe.matmul(out, x_lo[s][:, c, :], w_hi[q][:, k, :], start=False, stop=False)
                    ins = pe.matmul(out, x_hi[s][:, c, :], w_hi[q][:, k, :], start=False,
                                    stop=(h == 1 and k == 3))
                return ins

            def transpose_x(s, turn):
                pe.wait_ge(gathered[s], 16 * turn + 16)
                for c in range(KC):
                    ins = pe.transpose(bank[c // 4][:, 128 * (c % 4):128 * (c % 4) + 128],
                                       x_rows[s][:, 128 * c:128 * c + 128], ident[:])
                ins.then_inc(xt_ready, 1)

            transpose_x(0, 0)
            pe.wait_ge(xlo_done, 1)
            transpose_x(1, 0)
            for h in range(2):
                pe.wait_ge(lo_done, RAW + h + 1)
                gate_like(bank[2][:], 0, h, h).then_inc(unit_used, 1)
            for h in range(2):
                pe.wait_ge(lo_done, RAW + 2 + h + 1)
                gate_like(bank[4][:], 0, 2 + h, h).then_inc(unit_used, 1)
            with pe.Fori(0, pairs) as i:
                for s in range(2):
                    b = 2 * i + s
                    pe.wait_ge(xlo_done, b + 2)
                    for h in range(2):
                        _, q = unit_slot(s, h)
                        pe.wait_ge(lo_done, RAW + unit(i, s, h) + 1)
                        gate_like(bank[3 - s][:], 1 - s, q, h).then_inc(unit_used, 1)
                    pe.wait_ge(act_done, b + 3)
                    for k in range(4):
                        ins = pe.transpose(bank[5][:, 128 * k:128 * k + 128], act[s][:, 128 * k:128 * k + 128],
                                           ident[:])
                    ins.then_inc(at_ready, 1)
                    transpose_x(s, i + 1)
                    pe.wait_ge(alo_done, b + 1)
                    for h in range(2):
                        _, q = unit_slot(s, 2 + h)
                        pe.wait_ge(lo_done, RAW + unit(i, s, 2 + h) + 1)
                        pe.wait_ge((y_s, y_v)[h], b + 1)
                        out = bank[6 + h][:]
                        for k in range(4):
                            pe.matmul(out, a_hi[s][:, k, :], w_lo[q][:, k, :], start=(k == 0), stop=False)
                            pe.matmul(out, a_lo[s][:, k, :], w_hi[q][:, k, :], start=False, stop=False)
                            ins = pe.matmul(out, a_hi[s][:, k, :], w_hi[q][:, k, :], start=False, stop=(k == 3))
                        ins.then_inc(unit_used, 1)
                    pe.wait_ge(xlo_done, b + 2)
                    for h in range(2):
                        _, q = unit_slot(s, 4 + h)
                        pe.wait_ge(lo_done, RAW + unit(i, s, 4 + h) + 1)
                        gate_like(bank[4][:], 1 - s, q, h).then_inc(unit_used, 1)
    return used


def second_stage(nc, cst, x, mod_col, vec, w, dram, out):
    used = []
    with ExitStack() as ctx:
        def sb(name, shape, dt=F32):
            return ctx.enter_context(nc.sbuf_tensor("second_" + name, shape, dt))

        def sem(name):
            used.append(ctx.enter_context(nc.semaphore("second_" + name)))
            return used[-1]

        bank = [ctx.enter_context(nc.psum_tensor(f"second_bank{i}", [P, 512], F32)) for i in range(8)]
        ident, ones, gates = cst["ident"], cst["ones"], cst["gates"]
        RAWC, SPC = 4, 2
        raw = [sb(f"c_raw{i}", [P, KC, 256]) for i in range(RAWC)]
        w_hi = [sb(f"c_hi{i}", [P, KC, 256], F32R) for i in range(SPC)]
        w_lo = [sb(f"c_lo{i}", [P, KC, 256], F32R) for i in range(SPC)]
        x_hi = sb("cx_hi", [P, KC, SEQ], F32R)
        x_lo = sb("cx_lo", [P, KC, SEQ], F32R)
        g_hi = sb("cg_hi", [P, KC, SEQ], F32R)
        g_lo = sb("cg_lo", [P, KC, SEQ], F32R)
        work = sb("c_work", [P, 12288])

        def tile(a, n):
            return work[:, a:a + n]

        f_rows = tile(0, 4096).rearrange("p (t d) -> p t d", t=TC)
        y1_rows = tile(4096, 4096).rearrange("p (t d) -> p t d", t=TC)
        sq = tile(8192, 4096).rearrange("p (c t) -> p c t", c=KC)
        q_t = tile(0, 2048).rearrange("p (c t) -> p c t", c=4)
        k_t = tile(2048, 2048).rearrange("p (c t) -> p c t", c=4)
        v_t = tile(4096, 2048).rearrange("p (t d) -> p t d", t=TC)
        u_t = tile(6144, 2048).rearrange("p (c t) -> p c t", c=4)
        cum = tile(8192, 512)
        diff = tile(8704, 512)
        pooled = [tile(9216 + 512 * g, 512) for g in range(4)]
        s_t = [tile(6144 + 512 * i, 512) for i in range(2)]
        pt_t = [tile(7168 + 512 * i, 512) for i in range(2)]
        bias_row = tile(8192, 512)
        bias_diag = tile(8704, 512).rearrange("p (i k) -> p i k", i=TC)
        att = [tile(11264 + 512 * i, 512).rearrange("p (i d) -> p i d", i=TC) for i in range(2)]
        relu_t = [tile(512 * i, 512) for i in range(2)]
        hid_t = [tile(1024 + 512 * i, 512) for i in range(2)]
        mean_t = tile(2048, 512)
        rstd = sb("c_rstd", [P, SEQ])
        out_rows = tile(8192, 4096).rearrange("p (t d) -> p t d", t=TC)
        w_forget = sb("w_forget", [P, KC, HEADS])
        w_pool = tile(11264, 512).rearrange("p (g d) -> p g d", g=4)
        b_forget = sb("b_forget", [HEADS, 1])
        z = sb("z", [HEADS, SEQ])
        az = work[0:HEADS, 8192:8704]
        cf = work[0:HEADS, 11776:12288]
        cq = sb("cq", [P, TC, HEADS])
        sel = sb("sel", [HEADS, HEADS, P])
        causal = sb("causal", [P, P])
        inv_count = sb("inv_count", [P, 16])
        IT = [(h, i) for h in range(HEADS) for i in range(TC)]
        m_diag = sb("m_diag", [P, len(IT)])
        m_off = sb("m_off", [P, len(IT)])
        m_bias = sb("m_bias", [P, len(IT)])
        r_sum = sb("r_sum", [P, len(IT)])
        r_inv = sb("r_inv", [P, len(IT)])

        y_landed = [sem(f"y_landed{t}") for t in range(TC)]
        pair_ready = sem("pair_ready")
        side_landed = sem("side_landed")
        pool_landed = sem("pool_landed")
        tables = sem("c_tables")
        dve_step = sem("c_dve_step")
        pool_step = sem("c_pool_step")
        act_step = sem("c_act_step")
        f_ready = sem("f_ready")
        ft_ready = sem("ft_ready")
        xf_ready = sem("xf_ready")
        sq_ready = sem("c_sq_ready")
        ssq_ready = sem("c_ssq_ready")
        var_ready = sem("c_var_ready")
        std_ready = sem("c_std_ready")
        x_ready = sem("cx_ready")
        xhi_done = sem("cxhi_done")
        xlo_done = sem("cxlo_done")
        raw_landed = [sem(f"c_landed{i}") for i in range(RAWC)]
        hi_done = sem("c_hi_done")
        lo_done = sem("c_lo_done")
        acc_ready = sem("c_acc_ready")
        acc_used = sem("c_acc_used")
        fl_ready = sem("fl_ready")
        az_ready = sem("az_ready")
        ln_ready = sem("ln_ready")
        cf_ready = sem("cf_ready")
        cft_ready = sem("cft_ready")
        pooled_ready = sem("pooled_ready")
        py_ready = sem("py_ready")
        ghi_done = sem("ghi_done")
        glo_done = sem("glo_done")
        bias_ready = sem("bias_ready")
        bias_used = sem("bias_used")
        s_ready = sem("cs_ready")
        s_used = sem("cs_used")
        mb_ready = sem("cmb_ready")
        p_ready = sem("cp_ready")
        pt_ready = sem("cpt_ready")
        pt_used = sem("cpt_used")
        o_ready = sem("co_ready")
        o_used = sem("co_used")
        at_ready = sem("cat_ready")
        mix_ready = sem("mix_ready")
        mix_used = sem("mix_used")
        mean_ready = sem("mean_ready")
        cent_ready = sem("cent_ready")
        hid_ready = sem("hid_ready")
        relu_done = sem("relu_done")
        square_done = sem("square_done")
        hidhi_done = sem("hidhi_done")
        hidlo_done = sem("hidlo_done")
        down_ready = sem("down_ready")
        down_used = sem("down_used")
        outt_ready = sem("outt_ready")
        left_done = sem("left_done")
        right_done = sem("right_done")
        out_stored = sem("out_stored")

        w_in = w["w_in_2"][0].rearrange("(k p) n -> p k n", p=P)
        w_out = w["w_out_2"][0].rearrange("(k p) n -> p k n", p=P)
        w_up = w["w_mlp1_2"][0].rearrange("(k p) n -> p k n", p=P)
        w_down = w["w_mlp2_2"][0].rearrange("(g k p) n -> g p k n", p=P, k=KC)
        NIN, NOUT = 8, 4
        FIRST = NIN + NOUT

        def loop_unit(g, j):
            return FIRST + 8 * g + j

        def loop_landed(g, j):
            return 16 * (FIRST // RAWC + 2 * g + j // RAWC + 1)

        block = ctx.enter_context(nc.Block())

        @block.sync
        def _(sp):
            for t in range(TC):
                sp.dma_start(f_rows[:, t, :], dram["y"][t * 128:(t + 1) * 128, :]).then_inc(y_landed[t], 16)
                sp.dma_start(y1_rows[:, t, :], dram["y"][SEQ + t * 128:SEQ + (t + 1) * 128, :])\
                  .then_inc(y_landed[t], 16)
            for n in range(FIRST):
                if n >= RAWC:
                    sp.wait_ge(lo_done, n + 1)
                src = w_in[:, :, 256 * n:256 * n + 256] if n < NIN else w_out[:, :, 256 * (n - NIN):256 * (n - NIN) + 256]
                sp.dma_start(raw[n % RAWC][:], src).then_inc(raw_landed[n % RAWC], 16)
            with sp.Fori(0, 4) as g:
                for j in range(8):
                    sp.wait_ge(lo_done, loop_unit(g, j) + 1)
                    src = w_up[:, :, bass.ds(1024 * g + 256 * j, 256)] if j < 4 else \
                        w_down[bass.ds(g, 1), :, :, 256 * (j - 4):256 * (j - 4) + 256]
                    sp.dma_start(raw[j % RAWC][:], src).then_inc(raw_landed[j % RAWC], 16)
            for half, done in enumerate((left_done, right_done)):
                for t in range(TC):
                    sp.wait_ge(done, t + 1)
                    sp.dma_start(out[0, t * 128:(t + 1) * 128, 512 * half:512 * half + 512],
                                 out_rows[:, t, 512 * half:512 * half + 512]).then_inc(out_stored, 16)
            sp.wait_ge(out_stored, 16 * 2 * TC)

        @block.gpsimd
        def _(pool):
            n = [0]

            def step(ins):
                n[0] += 1
                ins.then_inc(pool_step, 1)
                pool.wait_ge(pool_step, n[0])

            with nc.allow_non_contiguous_dma(reason="a few columns"):
                pool.dma_start(w_forget[:], w_in[:, :, 2048:2056]).then_inc(side_landed, 16)
                pool.dma_start(b_forget[:], w["b_f_2"].rearrange("o h -> h o")).then_inc(side_landed, 16)
            pool.wait_ge(ssq_ready, 1)
            pool.dma_start(w_pool, w["pool_w_2"][0].rearrange("g c d -> c g d")).then_inc(pool_landed, 16)
            step(pool.memset(sel[:], 1.0))
            step(pool.affine_select(out=sel[:], in_=sel[:], compare_op=ALU.is_equal, fill=0.0, base=0,
                                    pattern=[[-1, HEADS], [0, P]], channel_multiplier=1))
            step(pool.memset(causal[:], 0.0))
            step(pool.affine_select(out=causal[:], in_=causal[:], compare_op=ALU.is_ge, fill=NEG, base=0,
                                    pattern=[[-1, P]], channel_multiplier=1))
            pool.iota(inv_count[:], pattern=[[1, 16]], base=1, channel_multiplier=0,
                      allow_small_or_imprecise_dtypes=True).then_inc(tables, 1)

        @block.scalar
        def _(act):
            def split_hi(landed, slot):
                act.wait_ge(raw_landed[slot % RAWC], landed)
                act.activation(w_hi[slot % SPC][:], raw[slot % RAWC][:], ACT.Copy).then_inc(hi_done, 1)

            def first_hi(n):
                if SPC <= n < NIN + SPC:
                    act.wait_ge(acc_ready, 2 * (n - SPC) + 2)
                elif n >= NIN + SPC:
                    act.wait_ge(mix_ready, 2 * (n - SPC - NIN) + 2)
                split_hi(16 * (n // RAWC + 1), n)

            for c in range(KC):
                act.wait_ge(xf_ready, c + 1)
                act.activation(sq[:, c, :], x[:, c, :], ACT.Square).then_inc(sq_ready, 1)
            first_hi(0)
            first_hi(1)
            act.wait_ge(var_ready, 1)
            act.activation(rstd[:], rstd[:], ACT.Sqrt).then_inc(std_ready, 1)
            for c in range(KC):
                act.wait_ge(x_ready, c + 1)
                act.activation(x_hi[:, c, :], x[:, c, :], ACT.Copy).then_inc(xhi_done, 1)
            act.wait_ge(az_ready, 1)
            act.activation(az, az, ACT.Exp, scale=-1.0).then_inc(act_step, 1)
            act.wait_ge(act_step, 1)
            act.activation(az, az, ACT.Ln, bias=1.0).then_inc(ln_ready, 1)
            for n in range(NIN):
                for k in range(2):
                    act.wait_ge(acc_ready, 2 * n + k + 1)
                    src = bank[(2 * n + k) % 4]
                    c = 2 * (n % 2) + k
                    if n < 2:
                        ins = act.activation(u_t[:, c, :], src[:], ACT.Copy)
                    elif n < 4:
                        ins = act.activation(q_t[:, c, :], src[:], ACT.Copy, scale=HD ** -0.5)
                    elif n < 6:
                        ins = act.activation(k_t[:, c, :], src[:], ACT.Copy)
                    else:
                        ins = act.activation(v_t[:, 2 * k:2 * k + 2, 256 * (n - 6):256 * (n - 6) + 256],
                                             src[:].rearrange("p (t d) -> p t d", t=2), ACT.Copy)
                    ins.then_inc(acc_used, 1)
                first_hi(n + 2)
            for g in range(4):
                act.wait_ge(py_ready, g + 1)
                act.activation(g_hi[:, g, :], bank[4 + g % 2][:], ACT.Identity,
                               scale=vec["pool_scale"][:, g:g + 1]).then_inc(ghi_done, 1)

            def p_transposed(n):
                h, i = IT[n]
                act.wait_ge(pt_ready, n + 1)
                if n >= 2:
                    act.wait_ge(o_ready, n - 1)
                act.activation(pt_t[n % 2][:, 0:128 * (i + 1)], bank[2 + n % 2][:, 0:128 * (i + 1)], ACT.Copy)\
                   .then_inc(pt_used, 1)

            def att_high(pair):
                act.wait_ge(at_ready, pair + 1)
                act.activation(g_hi[:, 4 + pair, :], bank[7][:], ACT.Copy).then_inc(ghi_done, 1)

            for n, (h, i) in enumerate(IT):
                act.wait_ge(mb_ready, n + 1)
                m = 128 * (i + 1)
                act.activation(s_t[n % 2][:, 0:m], s_t[n % 2][:, 0:m], ACT.Exp, bias=m_bias[:, n:n + 1],
                               accum_out=r_sum[:, n:n + 1]).then_inc(p_ready, 1)
                if n >= 1:
                    p_transposed(n - 1)
                if n >= 12 and n % 8 == 4:
                    att_high(n // 8 - 1)
            p_transposed(len(IT) - 1)
            att_high(3)
            for n in range(NIN + 2, FIRST):
                first_hi(n)

            def norm_part(turn):
                for c in range(KC):
                    act.wait_ge(cent_ready, KC * turn + c + 1)
                    act.activation(sq[:, c, :], x[:, c, :], ACT.Square).then_inc(sq_ready, 1)
                act.wait_ge(var_ready, turn + 2)
                act.activation(rstd[:], rstd[:], ACT.Sqrt).then_inc(std_ready, 1)

            norm_part(0)
            for c in range(KC):
                act.wait_ge(x_ready, KC + c + 1)
                act.activation(x_hi[:, c, :], x[:, c, :], ACT.Copy).then_inc(xhi_done, 1)
            with act.Fori(0, 4) as g:
                for j in range(8):
                    if 2 <= j < 6:
                        act.wait_ge(hid_ready, 8 * g + 2 * (j - 2) + 2)
                    else:
                        act.wait_ge(down_ready, 8 * g + (2 * j + 6 if j < 2 else 2 * (j - 6) + 10))
                    split_hi(loop_landed(g, j), j)
                    for k in range(2):
                        if 1 <= j <= 4:
                            t = 2 * (j - 1) + k
                            act.wait_ge(hid_ready, 8 * g + t + 1)
                            act.wait_ge(square_done, 8 * g + t + 1)
                            act.activation(relu_t[k], bank[t % 4][:], ACT.Relu).then_inc(relu_done, 1)
                            act.wait_ge(relu_done, 8 * g + t + 1)
                            act.activation(g_hi[:, t, :], relu_t[k], ACT.Square).then_inc(hidhi_done, 1)
            norm_part(1)
            for t in range(TC):
                act.wait_ge(outt_ready, t + 1)
                act.activation(out_rows[:, t, 0:512], bank[t][:], ACT.Copy).then_inc(left_done, 1)

        @block.vector
        def _(dve):
            n_step = [0]

            def step(ins):
                n_step[0] += 1
                ins.then_inc(dve_step, 1)
                dve.wait_ge(dve_step, n_step[0])

            def split_lo(n, slot):
                dve.wait_ge(hi_done, n + 1)
                dve.tensor_tensor(w_lo[slot % SPC][:], raw[slot % RAWC][:], w_hi[slot % SPC][:].bitcast(F32),
                                  ALU.subtract).then_inc(lo_done, 1)

            dve.sem_inc(lo_done, RAWC)
            dve.sem_inc(square_done, 2)
            dve.sem_inc(down_used, 4)
            for t in range(TC):
                dve.wait_ge(y_landed[t], 32)
                step(dve.tensor_scalar(f_rows[:, t, :], f_rows[:, t, :], gates[:, t, 0:1], None, ALU.mult))
                dve.scalar_tensor_tensor(out=f_rows[:, t, :], in0=y1_rows[:, t, :], scalar=gates[:, t, 1:2],
                                         in1=f_rows[:, t, :], op0=ALU.mult, op1=ALU.add).then_inc(f_ready, 1)
            for c in range(KC):
                dve.wait_ge(ft_ready, c + 1)
                dve.scalar_tensor_tensor(out=x[:, c, :], in0=bank[c][:], scalar=mod_col[:, 40 + c:41 + c],
                                         in1=x[:, c, :], op0=ALU.mult, op1=ALU.add).then_inc(xf_ready, 1)

            def square_pairs(turn):
                for p in range(4):
                    dve.wait_ge(sq_ready, KC * turn + 2 * p + 2)
                    dve.tensor_tensor(sq[:, 2 * p, :], sq[:, 2 * p, :], sq[:, 2 * p + 1, :], ALU.add)\
                       .then_inc(pair_ready, 1)

            def x_pair(p):
                dve.tensor_tensor(sq[:, 2 * p, :], x[:, 2 * p, :], x[:, 2 * p + 1, :], ALU.add)\
                   .then_inc(pair_ready, 1)

            square_pairs(0)
            dve.wait_ge(ssq_ready, 1)
            dve.tensor_scalar(rstd[:], bank[0][:], 1.0 / D, NORM_EPS, ALU.mult, ALU.add).then_inc(var_ready, 1)
            split_lo(0, 0)
            split_lo(1, 1)
            dve.wait_ge(std_ready, 1)
            step(dve.reciprocal(rstd[:], rstd[:]))
            for c in range(KC):
                dve.scalar_tensor_tensor(out=x[:, c, :], in0=x[:, c, :], scalar=vec["final_norm"][:, c:c + 1],
                                         in1=rstd[:], op0=ALU.mult, op1=ALU.mult).then_inc(x_ready, 1)

            def x_low(n):
                c = n % KC
                dve.wait_ge(xhi_done, n + 1)
                dve.tensor_tensor(x_lo[:, c, :], x[:, c, :], x_hi[:, c, :].bitcast(F32), ALU.subtract)\
                   .then_inc(xlo_done, 1)

            for c in range(KC):
                x_low(c)
            dve.wait_ge(fl_ready, 1)
            dve.wait_ge(side_landed, 32)
            step(dve.tensor_scalar(z[:], bank[4][0:HEADS, :], b_forget[:, 0:1], None, ALU.add))
            dve.scalar_tensor_tensor(out=az, in0=z[:], scalar=-1.0, in1=z[:], op0=ALU.mult, op1=ALU.max)\
               .then_inc(az_ready, 1)
            dve.wait_ge(tables, 1)
            step(dve.reciprocal(inv_count[:], inv_count[:]))
            dve.wait_ge(ln_ready, 1)
            step(dve.scalar_tensor_tensor(out=z[:], in0=z[:], scalar=0.0, in1=az, op0=ALU.min,
                                          op1=ALU.subtract))
            step(dve.tensor_tensor_scan(cf, ones[0:HEADS, 0:1].to_broadcast([HEADS, SEQ]), z[:], 0.0,
                                        ALU.mult, ALU.add))
            dve.tensor_scalar(z[:], cf, -1.0, None, ALU.mult).then_inc(cf_ready, 1)
            for n in range(2, NIN):
                split_lo(n, n)
                if n < 4:
                    continue
                g = n - 4
                win = 2 << g
                dve.wait_ge(acc_used, 4)
                step(dve.tensor_tensor_scan(cum, ones[:, 0:1].to_broadcast([P, SEQ]), u_t[:, g, :], 0.0,
                                            ALU.mult, ALU.add))
                step(dve.tensor_tensor(diff[:, win:SEQ], cum[:, win:SEQ], cum[:, 0:SEQ - win], ALU.subtract))
                step(dve.tensor_tensor(diff[:, 0:win], cum[:, 0:win], inv_count[:, 0:win], ALU.mult))
                dve.scalar_tensor_tensor(out=pooled[g][:, win:SEQ], in0=diff[:, win:SEQ], scalar=1.0 / win,
                                         in1=u_t[:, g, win:SEQ], op0=ALU.mult, op1=ALU.subtract)
                dve.tensor_tensor(pooled[g][:, 0:win], diff[:, 0:win], u_t[:, g, 0:win], ALU.subtract)\
                   .then_inc(pooled_ready, 1)
            dve.wait_ge(cft_ready, 1)
            step(dve.tensor_copy(cq[:], bank[7][:, 0:TC * HEADS].rearrange("p (t h) -> p t h", t=TC)))
            for g in range(4):
                dve.wait_ge(ghi_done, g + 1)
                dve.scalar_tensor_tensor(out=g_lo[:, g, :], in0=bank[4 + g % 2][:],
                                         scalar=vec["pool_scale"][:, g:g + 1],
                                         in1=g_hi[:, g, :].bitcast(F32), op0=ALU.mult, op1=ALU.subtract)\
                   .then_inc(glo_done, 1)
            split_lo(NIN, NIN)
            split_lo(NIN + 1, NIN + 1)

            def normed(n):
                h, i = IT[n]
                dve.wait_ge(p_ready, n + 1)
                step(dve.reciprocal(r_inv[:, n:n + 1], r_sum[:, n:n + 1]))
                dve.wait_ge(o_ready, n + 1)
                if i == 0 and h % 2 == 0 and h >= 4:
                    dve.wait_ge(at_ready, h // 2 - 1)
                ins = dve.tensor_scalar(att[h // 2 % 2][:, i, 64 * (h % 2):64 * (h % 2) + 64],
                                        bank[4 + n % 2][:, 0:HD], r_inv[:, n:n + 1], None, ALU.mult)
                ins.then_inc(o_used, 1)

            def att_low(pair):
                dve.wait_ge(ghi_done, 4 + pair + 1)
                dve.tensor_tensor(g_lo[:, 4 + pair, :], bank[7][:], g_hi[:, 4 + pair, :].bitcast(F32),
                                  ALU.subtract).then_inc(glo_done, 1)

            for n, (h, i) in enumerate(IT):
                if i == 0:
                    dve.wait_ge(bias_ready, h + 1)
                    dve.tensor_copy(bias_row, bank[6][:])
                    dve.tensor_tensor(bias_diag, bank[6][:].rearrange("p (i k) -> p i k", i=TC),
                                      causal[:].unsqueeze(1).to_broadcast([P, TC, P]), ALU.add)\
                       .then_inc(bias_used, 1)
                    dve.wait_ge(bias_used, h + 1)
                dve.wait_ge(s_ready, n + 1)
                if n >= 2:
                    dve.wait_ge(pt_ready, n - 1)
                a = 128 * i
                s = s_t[n % 2]
                if i:
                    dve.tensor_tensor_reduce(s[:, 0:a], bank[n % 2][:, 0:a], bias_row[:, 0:a], 1.0, -3.0e38,
                                             ALU.add, ALU.max, m_off[:, n:n + 1])
                ins = dve.tensor_tensor_reduce(s[:, a:a + 128], bank[n % 2][:, a:a + 128], bias_diag[:, i, :],
                                               1.0, -3.0e38, ALU.add, ALU.max, m_diag[:, n:n + 1])
                ins.then_inc(s_used, 1)
                dve.wait_ge(s_used, n + 1)
                if i:
                    step(dve.tensor_tensor(m_diag[:, n:n + 1], m_diag[:, n:n + 1], m_off[:, n:n + 1], ALU.max))
                step(dve.tensor_scalar(m_bias[:, n:n + 1], m_diag[:, n:n + 1], cq[:, i, h:h + 1], -1.0,
                                       ALU.add, ALU.mult))
                dve.tensor_tensor(m_bias[:, n:n + 1], m_bias[:, n:n + 1], cq[:, i, h:h + 1], ALU.add)\
                   .then_inc(mb_ready, 1)
                if n >= 2:
                    normed(n - 2)
                if n >= 12 and n % 8 == 4:
                    att_low(n // 8 - 1)
            normed(len(IT) - 2)
            normed(len(IT) - 1)
            att_low(3)
            for n in range(NIN + 2, FIRST):
                split_lo(n, n)
                for k in range(2):
                    c = 2 * (n - NIN - 2) + k
                    dve.wait_ge(mix_ready, c + 1)
                    dve.scalar_tensor_tensor(out=x[:, c, :], in0=x[:, c, :], scalar=ALPHA, in1=bank[c % 4][:],
                                             op0=ALU.mult, op1=ALU.add).then_inc(mix_used, 1)
                dve.wait_ge(mix_used, c + 1)
                x_pair(c // 2)
            for c in range(4, KC):
                dve.wait_ge(mix_ready, c + 1)
                dve.scalar_tensor_tensor(out=x[:, c, :], in0=x[:, c, :], scalar=ALPHA, in1=bank[c % 4][:],
                                         op0=ALU.mult, op1=ALU.add).then_inc(mix_used, 1)
                if c % 2:
                    dve.wait_ge(mix_used, c + 1)
                    x_pair(c // 2)

            def norm_part(turn, gain, offset):
                dve.wait_ge(mean_ready, turn + 1)
                step(dve.tensor_scalar(mean_t, bank[4][:], 1.0 / D, None, ALU.mult))
                for c in range(KC):
                    dve.tensor_tensor(x[:, c, :], x[:, c, :], mean_t, ALU.subtract).then_inc(cent_ready, 1)
                square_pairs(turn + 1)
                dve.wait_ge(ssq_ready, turn + 2)
                dve.tensor_scalar(rstd[:], bank[5][:], 1.0 / D, LN_EPS, ALU.mult, ALU.add).then_inc(var_ready, 1)
                dve.wait_ge(std_ready, turn + 2)
                step(dve.reciprocal(rstd[:], rstd[:]))
                for c in range(KC):
                    step(dve.scalar_tensor_tensor(out=x[:, c, :], in0=x[:, c, :], scalar=gain[:, c:c + 1],
                                                  in1=rstd[:], op0=ALU.mult, op1=ALU.mult))
                    dve.tensor_scalar(x[:, c, :], x[:, c, :], offset[:, c:c + 1], None, ALU.add)\
                       .then_inc(x_ready, 1)
                    if turn == 0 and c:
                        x_low(KC + c - 1)

            norm_part(0, vec["ln1_g"], vec["ln1_b"])
            x_low(2 * KC - 1)
            split_lo(loop_unit(0, 0), 0)
            for c in range(KC):
                ins = dve.tensor_scalar(x[:, c, :], x[:, c, :], ALPHA, None, ALU.mult)
            step(ins)

            def down_added(g, c):
                dve.wait_ge(down_ready, 8 * g + c + 9)
                dve.tensor_tensor(x[:, c, :], bank[4 + c % 4][:], x[:, c, :], ALU.add).then_inc(down_used, 1)

            def group(g, last):
                for j in range(8):
                    if j:
                        split_lo(loop_unit(g, j), j)
                    for k in range(2):
                        if 1 <= j <= 4:
                            t = 2 * (j - 1) + k
                            dve.wait_ge(relu_done, 8 * g + t + 1)
                            dve.tensor_tensor(hid_t[k], relu_t[k], relu_t[k], ALU.mult).then_inc(square_done, 1)
                            dve.wait_ge(square_done, 8 * g + t + 3)
                            dve.wait_ge(hidhi_done, 8 * g + t + 1)
                            dve.tensor_tensor(g_lo[:, t, :], hid_t[k], g_hi[:, t, :].bitcast(F32), ALU.subtract)\
                               .then_inc(hidlo_done, 1)
                        if j >= 5:
                            down_added(g, 2 * (j - 5) + k)
                if not last:
                    split_lo(loop_unit(g, 8), 8)
                for c in range(6, KC):
                    down_added(g, c)

            with dve.Fori(0, 3) as g:
                group(g, False)
            group(3, True)
            dve.wait_ge(down_used, 36)
            for p in range(4):
                x_pair(p)
            norm_part(1, vec["ln2_g"], vec["ln2_b"])
            for t in range(TC):
                dve.wait_ge(outt_ready, TC + t + 1)
                dve.tensor_copy(out_rows[:, t, 512:1024], bank[TC + t][:]).then_inc(right_done, 1)

        @block.tensor
        def _(pe):
            pe.sem_inc(down_ready, 8)
            for t in range(TC):
                pe.wait_ge(f_ready, t + 1)
                for c in range(KC):
                    ins = pe.transpose(bank[c][:, 128 * t:128 * t + 128], f_rows[:, t, 128 * c:128 * c + 128],
                                       ident[:])
                    if t == TC - 1:
                        ins.then_inc(ft_ready, 1)

            def column_sums(dst, first_pair):
                for p in range(4):
                    pe.wait_ge(pair_ready, first_pair + p + 1)
                    ins = pe.matmul(dst[:], ones[:], sq[:, 2 * p, :], start=(p == 0), stop=(p == 3))
                return ins

            column_sums(bank[0], 0).then_inc(ssq_ready, 1)
            pe.wait_ge(side_landed, 32)
            for c in range(KC):
                pe.wait_ge(x_ready, c + 1)
                ins = pe.matmul(bank[4][0:HEADS, :], w_forget[:, c, :], x[:, c, :], start=(c == 0),
                                stop=(c == KC - 1))
            ins.then_inc(fl_ready, 1)

            def product(out, a_hi, a_lo, b_hi, b_lo, first, last):
                pe.matmul(out, a_hi, b_lo, start=first, stop=False)
                pe.matmul(out, a_lo, b_hi, start=False, stop=False)
                return pe.matmul(out, a_hi, b_hi, start=False, stop=last)

            def by_features(out, q, k, b_hi, b_lo, ready=None, chunks=range(KC)):
                for c in chunks:
                    if ready is not None:
                        pe.wait_ge(*ready(c))
                    ins = product(out, w_hi[q][:, c, 128 * k:128 * k + 128], w_lo[q][:, c, 128 * k:128 * k + 128],
                                  b_hi[:, c, :], b_lo[:, c, :], c == 0, c == KC - 1)
                return ins

            pe.wait_ge(xlo_done, KC)
            for n in range(NIN):
                pe.wait_ge(lo_done, RAWC + n + 1)
                q = n % SPC
                for k in range(2):
                    tile_n = 2 * n + k
                    if tile_n >= 4:
                        pe.wait_ge(acc_used, tile_n - 3)
                    dst = bank[tile_n % 4]
                    if n < 6:
                        ins = by_features(dst[:], q, k, x_hi, x_lo)
                    else:
                        for t in range(2):
                            a = 128 * (2 * k + t)
                            for c in range(KC):
                                ins = product(dst[:, 256 * t:256 * t + 256], x_hi[:, c, a:a + 128],
                                              x_lo[:, c, a:a + 128], w_hi[q][:, c, :], w_lo[q][:, c, :],
                                              c == 0, c == KC - 1)
                    ins.then_inc(acc_ready, 1)
            pe.wait_ge(pool_landed, 16)
            for g in range(4):
                pe.wait_ge(pooled_ready, g + 1)
                if g >= 2:
                    pe.wait_ge(glo_done, g - 1)
                pe.matmul(bank[4 + g % 2][:], w_pool[:, g, :], pooled[g], start=True, stop=True)\
                  .then_inc(py_ready, 1)
                if g == 0:
                    pe.wait_ge(cf_ready, 1)
                    for t in range(TC):
                        ins = pe.transpose(bank[7][:, HEADS * t:HEADS * t + HEADS], cf[:, 128 * t:128 * t + 128],
                                           ident[0:HEADS, 0:HEADS])
                    ins.then_inc(cft_ready, 1)
            pe.wait_ge(acc_used, 2 * NIN)
            pe.wait_ge(glo_done, 4)

            def scores(n):
                h, i = IT[n]
                if i == 0:
                    if h:
                        pe.wait_ge(bias_used, h)
                    pe.matmul(bank[6][:], sel[:, h, :], z[:], start=True, stop=True).then_inc(bias_ready, 1)
                if n >= 2:
                    pe.wait_ge(s_used, n - 1)
                a = 64 * (h % 2)
                pe.matmul(bank[n % 2][:, 0:128 * (i + 1)], q_t[a:a + 64, h // 2, 128 * i:128 * i + 128],
                          k_t[a:a + 64, h // 2, 0:128 * (i + 1)], start=True, stop=True).then_inc(s_ready, 1)

            def turn(n):
                h, i = IT[n]
                pe.wait_ge(p_ready, n + 1)
                if n >= 2:
                    pe.wait_ge(pt_used, n - 1)
                for j in range(i + 1):
                    ins = pe.transpose(bank[2 + n % 2][:, 128 * j:128 * j + 128],
                                       s_t[n % 2][:, 128 * j:128 * j + 128], ident[:])
                ins.then_inc(pt_ready, 1)

            def values(n):
                h, i = IT[n]
                pe.wait_ge(pt_used, n + 1)
                if n >= 2:
                    pe.wait_ge(o_used, n - 1)
                for j in range(i + 1):
                    ins = pe.matmul(bank[4 + n % 2][:, 0:HD], pt_t[n % 2][:, 128 * j:128 * j + 128],
                                    v_t[:, j, HD * h:HD * h + HD], start=(j == 0), stop=(j == i))
                ins.then_inc(o_ready, 1)

            def turn_att(pair):
                pe.wait_ge(o_used, 8 * (pair + 1))
                if pair:
                    pe.wait_ge(glo_done, 4 + pair)
                for t in range(TC):
                    ins = pe.transpose(bank[7][:, 128 * t:128 * t + 128], att[pair % 2][:, t, :], ident[:])
                ins.then_inc(at_ready, 1)

            scores(0)
            for n in range(len(IT)):
                if n + 1 < len(IT):
                    scores(n + 1)
                turn(n)
                if n >= 1:
                    values(n - 1)
                if n >= 11 and n % 8 == 3:
                    turn_att(n // 8 - 1)
            values(len(IT) - 1)
            turn_att(3)
            for n in range(NIN, FIRST):
                pe.wait_ge(lo_done, RAWC + n + 1)
                for k in range(2):
                    c = 2 * (n - NIN) + k
                    if c >= 4:
                        pe.wait_ge(mix_used, c - 3)
                    ins = by_features(bank[c % 4][:], n % SPC, k, g_hi, g_lo,
                                      (lambda cc: (glo_done, max(cc + 1, 4))) if c == 0 else None)
                    ins.then_inc(mix_ready, 1)

            def norm_part(turn):
                column_sums(bank[4], 8 * turn + 4).then_inc(mean_ready, 1)
                column_sums(bank[5], 8 * turn + 8).then_inc(ssq_ready, 1)

            norm_part(0)
            with pe.Fori(0, 4) as g:
                for j in range(8):
                    pe.wait_ge(lo_done, RAWC + loop_unit(g, j) + 1)
                    if j == 4:
                        for k in range(2):
                            pe.wait_ge(down_used, 8 * g + k + 1)
                            by_features(bank[4 + k][:], j % SPC, k, g_hi, g_lo,
                                        lambda c: (hidlo_done, 8 * g + c + 1), range(6))
                        for k in range(2):
                            by_features(bank[4 + k][:], j % SPC, k, g_hi, g_lo,
                                        lambda c: (hidlo_done, 8 * g + c + 1), range(6, KC)).then_inc(down_ready, 1)
                        continue
                    for k in range(2):
                        t = 2 * (j % 4) + k
                        if j < 4:
                            if t >= 4:
                                pe.wait_ge(hidhi_done, 8 * g + t - 3)
                            ins = by_features(bank[t % 4][:], j % SPC, k, x_hi, x_lo,
                                              (lambda c: (xlo_done, KC + c + 1)) if t == 0 else None)
                            ins.then_inc(hid_ready, 1)
                        else:
                            pe.wait_ge(down_used, 8 * g + t + 1)
                            by_features(bank[4 + t % 4][:], j % SPC, k, g_hi, g_lo).then_inc(down_ready, 1)
            norm_part(1)
            for half in range(2):
                for c in range(4 * half, 4 * half + 4):
                    pe.wait_ge(x_ready, 2 * KC + c + 1)
                    for t in range(TC):
                        ins = pe.transpose(bank[TC * half + t][:, 128 * (c % 4):128 * (c % 4) + 128],
                                           x[:, c, 128 * t:128 * t + 128], ident[:])
                        if c % 4 == 3:
                            ins.then_inc(outt_ready, 1)


INPUTS = ["x", "c", "ctx", "c_ctx", "w_mod", "b_mod", "norm_mix", "w_in", "rpb", "w_att_out", "conv_w", "conv_b",
          "conv_ln_g", "conv_ln_b", "w_conv_out", "w_o", "norm_ffn", "w_router_group", "b_router_group",
          "w_router_expert", "b_router_expert", "w_exp_gate", "w_exp_up", "w_exp_down", "final_norm", "w_in_2",
          "b_f_2", "pool_w_2", "pool_scale_2", "w_out_2", "ln1_g_2", "ln1_b_2", "w_mlp1_2", "w_mlp2_2", "ln2_g_2",
          "ln2_b_2"]


def build_program(nc, w, out):
    with ExitStack() as ctx:
        def sb(name, shape):
            return ctx.enter_context(nc.sbuf_tensor(name, shape, F32))

        cst = {"ident": sb("ident", [P, P]), "ones": sb("ones", [P, P]), "gates": sb("gates", [P, TC, 2])}
        with nc.sbuf_tensor("keys_queries_hi", [P, KC, SEQ], F32R) as kq_hi:
            pass
        x_mid = sb("x_mid", [P, KC, SEQ])
        mod_col = sb("mod_col", [P, 48])
        vec_all = sb("vec_all", [P, 120])
        vec = {"norm_ffn": vec_all[:, 68:76], "final_norm": vec_all[:, 76:84], "pool_scale": vec_all[:, 84:88],
               "ln1_g": vec_all[:, 88:96], "ln1_b": vec_all[:, 96:104], "ln2_g": vec_all[:, 104:112],
               "ln2_b": vec_all[:, 112:120]}
        dram = {"h2": nc.dram_tensor("h2_rows_dram", [SEQ, D], F32),
                "mark": nc.dram_tensor("mark_dram", [2, 1, P], F32),
                "y": nc.dram_tensor("y_dram", [2 * SEQ, D], F32)}
        used = mixer_stage(nc, cst, x_mid, kq_hi, mod_col, vec_all, w)
        zero_semaphores(nc, used)
        used = moe_stage(nc, cst, x_mid, mod_col, vec, w, dram)
        zero_semaphores(nc, used)
        second_stage(nc, cst, x_mid, mod_col, vec, w, dram, out)


def zero_semaphores(nc, used):
    with nc.Block() as block:
        @block.gpsimd
        def _(pool):
            for s in used:
                pool.sem_clear(s)


def kernel(**inputs):
    import numpy as np
    import concourse.bacc as bacc
    from concourse.bass_utils import run_bass_kernel_spmd

    nc = bacc.Bacc("TRN2", target_bir_lowering=False, num_devices=1)
    arrays, args = {}, {}
    for name in INPUTS:
        a = np.ascontiguousarray(inputs[name])
        arrays[f"in_{name}_dram"] = a
        args[name] = nc.dram_tensor(f"in_{name}_dram", a.shape, mybir.dt.from_np(a.dtype), kind="ExternalInput").ap()
    out = nc.dram_tensor("out_dram", (1, SEQ, D), F32, kind="ExternalOutput").ap()
    build_program(nc, args, out)
    r = run_bass_kernel_spmd(nc, [arrays], core_ids=[0])
    return r.results[0]["out_dram"]
```
